# Optimizing a Trainium2 kernel written in Bass

```python
import math
import jax, jax.numpy as jnp
from jax import lax
import numpy as np

D_MODEL = 1024
BATCH = 1
SEQ = 1024
DEPTH = 4
DEC_BATCH = 8
DEC_SEQ = 1
PAST_LEN = 2048
PAGE_SIZE = 128

N_MIXERS = 3
N_A_LAYERS = (DEPTH + 2) // 3
N_B_LAYERS = (DEPTH + 1) // 3
N_C_LAYERS = DEPTH // 3

A_HEADS = 8
A_NOPE = 64
A_ROPE = 32
A_QK = A_NOPE + A_ROPE
A_V = 64
A_Q_LORA = 384
A_KV_LORA = 256
A_WIDTH = A_HEADS * A_V
A_IN = A_Q_LORA + A_KV_LORA + A_ROPE + A_WIDTH
ROPE_THETA = 10000.0
Q_BLOCK = 128

B_EXPAND = 128
B_HEADS = D_MODEL // B_EXPAND
B_DK = B_EXPAND
B_WIDTH = D_MODEL
B_DV = B_WIDTH // B_HEADS
B_CHUNK = 64

C_WIDTH = D_MODEL
C_HEADS = 8
C_BW = C_WIDTH // C_HEADS
C_CONV = 4
C_GATE_C = 8.0

EPS = 1e-6

kernel_name = 'mla_hgrn2_rglru_hybrid_step'

def rmsnorm(x, g):
    xf = x.astype(jnp.float32)
    y = xf * lax.rsqrt(jnp.mean(xf * xf, axis=-1, keepdims=True) + EPS)
    return (y * g.astype(jnp.float32)).astype(x.dtype)

def rope_cos_sin(pos, dtype):
    inv = 1.0 / (ROPE_THETA ** (jnp.arange(0, A_ROPE, 2, dtype=jnp.float32) / A_ROPE))
    ang = pos.astype(jnp.float32)[:, None] * inv[None, :]
    ang = jnp.concatenate([ang, ang], axis=-1)
    return jnp.cos(ang).astype(dtype), jnp.sin(ang).astype(dtype)

def apply_rope(x, cos, sin):
    x1, x2 = jnp.split(x, 2, axis=-1)
    return x * cos + jnp.concatenate([-x2, x1], axis=-1) * sin

def mla_project(h, pos, w_in, g_ql, g_kv, w_uq, g_q):
    b, s, _ = h.shape
    cq, ckv, kpe, gate = jnp.split(h @ w_in, [A_Q_LORA, A_Q_LORA + A_KV_LORA, A_Q_LORA + A_KV_LORA + A_ROPE], axis=-1)
    cos, sin = rope_cos_sin(pos, h.dtype)
    q = (rmsnorm(cq, g_ql) @ w_uq).reshape(b, s, A_HEADS, A_QK)
    q = jnp.concatenate([q[..., :A_NOPE], apply_rope(q[..., A_NOPE:], cos[:, None], sin[:, None])], axis=-1)
    q = rmsnorm(q, g_q)
    ckv = rmsnorm(ckv, g_kv)
    kpe = apply_rope(kpe, cos, sin)
    return q, ckv, kpe, gate

def mla_expand(ckv, kpe, w_ukv, g_k):
    kv = jnp.einsum('bnc,chd->bnhd', ckv, w_ukv.reshape(A_KV_LORA, A_HEADS, A_NOPE + A_V))
    k_nope, v = kv[..., :A_NOPE], kv[..., A_NOPE:]
    k_pe = jnp.broadcast_to(kpe[:, :, None, :], k_nope.shape[:-1] + (A_ROPE,))
    k = jnp.concatenate([k_nope, k_pe.astype(k_nope.dtype)], axis=-1)
    return rmsnorm(k, g_k), v

def mla_prompt_attention(q, k, v):
    b, s = q.shape[:2]
    nqb = s // Q_BLOCK
    scale = A_QK ** -0.5
    qb = q.reshape(b, nqb, Q_BLOCK, A_HEADS, A_QK).swapaxes(0, 1)
    kpos = jnp.arange(s)

    def one_block(args):
        bi, qblk = args
        sc = jnp.einsum('bqhd,bkhd->bhqk', qblk, k).astype(jnp.float32) * scale
        qpos = bi * Q_BLOCK + jnp.arange(Q_BLOCK)
        sc = jnp.where(kpos[None, :] <= qpos[:, None], sc, -jnp.inf)
        p = jax.nn.softmax(sc, axis=-1).astype(v.dtype)
        return jnp.einsum('bhqk,bkhd->bqhd', p, v)

    o = lax.map(one_block, (jnp.arange(nqb), qb))
    return o.swapaxes(0, 1).reshape(b, s, A_HEADS, A_V)

def mla_sample_attention(q, k_new, v_new, cache_ckv, cache_kpe, la, page_table, w_ukv, g_k):
    db, ds = q.shape[:2]
    scale = A_QK ** -0.5

    def update(carry, k, v, mask):
        m, l, acc = carry
        sc = jnp.einsum('bqhd,bkhd->bhqk', q, k.astype(q.dtype)).astype(jnp.float32) * scale
        if mask is not None:
            sc = jnp.where(mask, sc, -jnp.inf)
        m_new = jnp.maximum(m, sc.max(axis=-1))
        p = jnp.exp(sc - m_new[..., None])
        corr = jnp.exp(m - m_new)
        l = l * corr + p.sum(axis=-1)
        acc = acc * corr[..., None] + jnp.einsum('bhqk,bkhd->bhqd', p, v.astype(jnp.float32))
        return (m_new, l, acc)

    def page_step(carry, phys):
        k, v = mla_expand(cache_ckv[la, phys], cache_kpe[la, phys], w_ukv, g_k)
        return update(carry, k, v, None), None

    init = (jnp.full((db, A_HEADS, ds), -jnp.inf, jnp.float32),
            jnp.zeros((db, A_HEADS, ds), jnp.float32),
            jnp.zeros((db, A_HEADS, ds, A_V), jnp.float32))
    carry, _ = lax.scan(page_step, init, page_table.T)
    causal = jnp.arange(ds)[None, :] <= jnp.arange(ds)[:, None]
    m, l, acc = update(carry, k_new, v_new, causal)
    return (acc / l[..., None]).astype(q.dtype).transpose(0, 2, 1, 3)

def mla_out(o, gate, w_out):
    b, s = o.shape[:2]
    return (o.reshape(b, s, A_WIDTH) * jax.nn.silu(gate)) @ w_out

def hgrn_project(h, w_in, lb):
    b, s, _ = h.shape
    q, f, i, gate = jnp.split(h @ w_in, 4, axis=-1)
    ff = f.astype(jnp.float32)
    lbf = lb.astype(jnp.float32)
    g = jnp.log(lbf + (1.0 - lbf) * jax.nn.sigmoid(ff))
    k = (1.0 - lbf) * jax.nn.sigmoid(-ff)

    def heads(t, d):
        return t.reshape(b, s, B_HEADS, d).transpose(0, 2, 1, 3)

    qf = jax.nn.silu(q).astype(jnp.float32) * (B_DK ** -0.5)
    return heads(qf, B_DK), heads(k, B_DK), heads(i.astype(jnp.float32), B_DV), heads(g, B_DK), gate

def gla_chunk(state, inp):
    q, k, v, g = inp
    c = q.shape[2]
    bcum = jnp.cumsum(g, axis=2)
    inter = jnp.einsum('bhtk,bhkv->bhtv', q * jnp.exp(bcum), state)
    causal = jnp.arange(c)[:, None] >= jnp.arange(c)[None, :]
    diff = jnp.where(causal[None, None, :, :, None], bcum[:, :, :, None, :] - bcum[:, :, None, :, :], -jnp.inf)
    att = jnp.einsum('bhtk,bhtsk,bhsk->bhts', q, jnp.exp(diff), k)
    o = inter + jnp.einsum('bhts,bhsv->bhtv', att, v)
    blast = bcum[:, :, -1:, :]
    new_state = jnp.exp(blast[:, :, 0, :])[..., None] * state + jnp.einsum('bhsk,bhsv->bhkv', k * jnp.exp(blast - bcum), v)
    return new_state, o

def to_chunks(t):
    b, hh, s, d = t.shape
    return t.reshape(b, hh, s // B_CHUNK, B_CHUNK, d).transpose(2, 0, 1, 3, 4)

def from_chunks(t):
    nc, b, hh, c, d = t.shape
    return t.transpose(1, 2, 0, 3, 4).reshape(b, hh, nc * c, d)

def hgrn_out(o, gate, g_norm, w_out):
    b, hh, s, dv = o.shape
    o = rmsnorm(o.transpose(0, 2, 1, 3), g_norm).reshape(b, s, B_WIDTH).astype(gate.dtype)
    return (o * jax.nn.silu(gate)) @ w_out

def lru_combine(lhs, rhs):
    a1, b1 = lhs
    a2, b2 = rhs
    return a1 * a2, a2 * b1 + b2

def rglru_layer(h, conv_buf, h0, w_in, conv_w, conv_b, w_a, b_a, w_x, b_x, lam, w_out):
    b, s, _ = h.shape
    xb, gate = jnp.split(h @ w_in, 2, axis=-1)
    xpad = jnp.concatenate([conv_buf.astype(xb.dtype), xb], axis=1)
    y = conv_b + sum(xpad[:, j:j + s] * conv_w[j] for j in range(C_CONV))
    new_buf = xpad[:, s:]
    yh = y.reshape(b, s, C_HEADS, C_BW)
    r = jax.nn.sigmoid(jnp.einsum('bsnd,nde->bsne', yh, w_a).reshape(b, s, C_WIDTH) + b_a)
    i = jax.nn.sigmoid(jnp.einsum('bsnd,nde->bsne', yh, w_x).reshape(b, s, C_WIDTH) + b_x)
    log_a = -C_GATE_C * r.astype(jnp.float32) * jax.nn.softplus(-lam.astype(jnp.float32))
    a = jnp.exp(log_a)
    u = jnp.sqrt(-jnp.expm1(2.0 * log_a)) * (i * y).astype(jnp.float32)
    u = u.at[:, 0].add(a[:, 0] * h0.astype(jnp.float32))
    _, hs = lax.associative_scan(lru_combine, (a, u), axis=1)
    out = (hs.astype(h.dtype) * jax.nn.silu(gate)) @ w_out
    return out, new_buf, hs[:, -1]

def setup_inputs(seed: int = 0) -> dict:
    key = jax.random.key(seed)
    ks = iter(jax.random.split(key, 40))

    def nrm(shape, scale):
        return jax.random.normal(next(ks), shape, jnp.float32) * scale

    def gain(shape):
        return 1.0 + nrm(shape, 0.1)

    n_pages = PAST_LEN // PAGE_SIZE
    n_used = DEC_BATCH * n_pages
    n_pool = n_used + n_used // 4
    x_prompt = nrm((BATCH, SEQ, D_MODEL), 1.0)
    x_sample = nrm((DEC_BATCH, DEC_SEQ, D_MODEL), 1.0)
    cache_ckv = nrm((N_A_LAYERS, n_pool, PAGE_SIZE, A_KV_LORA), 1.0)
    cache_kpe = nrm((N_A_LAYERS, n_pool, PAGE_SIZE, A_ROPE), 1.0)
    page_table = jax.random.permutation(next(ks), n_pool)[:n_used].reshape(DEC_BATCH, n_pages).astype(jnp.int32)
    state_hgrn = nrm((N_B_LAYERS, DEC_BATCH, B_HEADS, B_DK, B_DV), 0.5)
    state_conv = nrm((N_C_LAYERS, DEC_BATCH, C_CONV - 1, C_WIDTH), 1.0)
    state_lru = nrm((N_C_LAYERS, DEC_BATCH, C_WIDTH), 0.5)
    norm_g = gain((DEPTH, D_MODEL))
    mla_w_in = nrm((N_A_LAYERS, D_MODEL, A_IN), D_MODEL ** -0.5)
    mla_g_q_lora = gain((N_A_LAYERS, A_Q_LORA))
    mla_g_kv = gain((N_A_LAYERS, A_KV_LORA))
    mla_w_uq = nrm((N_A_LAYERS, A_Q_LORA, A_HEADS * A_QK), A_Q_LORA ** -0.5)
    mla_w_ukv = nrm((N_A_LAYERS, A_KV_LORA, A_HEADS * (A_NOPE + A_V)), A_KV_LORA ** -0.5)
    mla_g_q = gain((N_A_LAYERS, A_QK))
    mla_g_k = gain((N_A_LAYERS, A_QK))
    mla_w_out = nrm((N_A_LAYERS, A_WIDTH, D_MODEL), A_WIDTH ** -0.5)
    hgrn_w_in = nrm((N_B_LAYERS, D_MODEL, 4 * B_WIDTH), D_MODEL ** -0.5)
    hgrn_lower_bounds = nrm((DEPTH, B_HEADS * B_DK), 1.0)
    hgrn_g_norm = gain((N_B_LAYERS, B_DV))
    hgrn_w_out = nrm((N_B_LAYERS, B_WIDTH, D_MODEL), B_WIDTH ** -0.5)
    rglru_w_in = nrm((N_C_LAYERS, D_MODEL, 2 * C_WIDTH), D_MODEL ** -0.5)
    rglru_conv_w = nrm((N_C_LAYERS, C_CONV, C_WIDTH), C_CONV ** -0.5)
    rglru_conv_b = nrm((N_C_LAYERS, C_WIDTH), 0.02)
    rglru_w_a = nrm((N_C_LAYERS, C_HEADS, C_BW, C_BW), C_BW ** -0.5)
    rglru_b_a = nrm((N_C_LAYERS, C_WIDTH), 0.1)
    rglru_w_x = nrm((N_C_LAYERS, C_HEADS, C_BW, C_BW), C_BW ** -0.5)
    rglru_b_x = nrm((N_C_LAYERS, C_WIDTH), 0.1)
    a_pow = jax.random.uniform(next(ks), (N_C_LAYERS, C_WIDTH), jnp.float32, 0.9, 0.999)
    a_base = a_pow ** (1.0 / C_GATE_C)
    rglru_L = jnp.log(a_base) - jnp.log1p(-a_base)
    rglru_w_out = nrm((N_C_LAYERS, C_WIDTH, D_MODEL), C_WIDTH ** -0.5)
    return {'x_prompt': x_prompt, 'x_sample': x_sample, 'cache_ckv': cache_ckv, 'cache_kpe': cache_kpe,
            'page_table': page_table, 'state_hgrn': state_hgrn, 'state_conv': state_conv, 'state_lru': state_lru,
            'norm_g': norm_g, 'mla_w_in': mla_w_in, 'mla_g_q_lora': mla_g_q_lora, 'mla_g_kv': mla_g_kv,
            'mla_w_uq': mla_w_uq, 'mla_w_ukv': mla_w_ukv, 'mla_g_q': mla_g_q, 'mla_g_k': mla_g_k,
            'mla_w_out': mla_w_out, 'hgrn_w_in': hgrn_w_in, 'hgrn_lower_bounds': hgrn_lower_bounds,
            'hgrn_g_norm': hgrn_g_norm, 'hgrn_w_out': hgrn_w_out, 'rglru_w_in': rglru_w_in,
            'rglru_conv_w': rglru_conv_w, 'rglru_conv_b': rglru_conv_b, 'rglru_w_a': rglru_w_a,
            'rglru_b_a': rglru_b_a, 'rglru_w_x': rglru_w_x, 'rglru_b_x': rglru_b_x, 'rglru_L': rglru_L,
            'rglru_w_out': rglru_w_out}

def reference(x_prompt, x_sample, cache_ckv, cache_kpe, page_table, state_hgrn, state_conv, state_lru,
              norm_g, mla_w_in, mla_g_q_lora, mla_g_kv, mla_w_uq, mla_w_ukv, mla_g_q, mla_g_k, mla_w_out,
              hgrn_w_in, hgrn_lower_bounds, hgrn_g_norm, hgrn_w_out, rglru_w_in, rglru_conv_w, rglru_conv_b,
              rglru_w_a, rglru_b_a, rglru_w_x, rglru_b_x, rglru_L, rglru_w_out):
    f32 = jnp.float32
    bsz, s_p, _ = x_prompt.shape
    s_s = x_sample.shape[1]
    past_len = page_table.shape[1] * PAGE_SIZE
    pos_p = jnp.arange(s_p)
    pos_s = past_len + jnp.arange(s_s)
    smx = jax.nn.softmax(hgrn_lower_bounds.astype(f32), axis=0)
    lower_bounds = jnp.cumsum(smx, axis=0) - smx[0]

    xp, xs = x_prompt, x_sample
    ckv_p, kpe_p, ckv_s, kpe_s = [], [], [], []
    hg_p, hg_s = [], []
    cv_p, cv_s, lr_p, lr_s = [], [], [], []
    for li in range(DEPTH):
        kind, j = li % N_MIXERS, li // N_MIXERS
        hp = rmsnorm(xp, norm_g[li])
        hs = rmsnorm(xs, norm_g[li])
        if kind == 0:
            qp, cp, kp, gp = mla_project(hp, pos_p, mla_w_in[j], mla_g_q_lora[j], mla_g_kv[j], mla_w_uq[j], mla_g_q[j])
            k_p, v_p = mla_expand(cp, kp, mla_w_ukv[j], mla_g_k[j])
            dp = mla_out(mla_prompt_attention(qp, k_p, v_p), gp, mla_w_out[j])
            qs, cs, kss, gs = mla_project(hs, pos_s, mla_w_in[j], mla_g_q_lora[j], mla_g_kv[j], mla_w_uq[j], mla_g_q[j])
            k_s, v_s = mla_expand(cs, kss, mla_w_ukv[j], mla_g_k[j])
            o_s = mla_sample_attention(qs, k_s, v_s, cache_ckv, cache_kpe, j, page_table, mla_w_ukv[j], mla_g_k[j])
            ds_ = mla_out(o_s, gs, mla_w_out[j])
            ckv_p.append(cp)
            kpe_p.append(kp)
            ckv_s.append(cs)
            kpe_s.append(kss)
        elif kind == 1:
            qp, kp, vp, gp, gatep = hgrn_project(hp, hgrn_w_in[j], lower_bounds[li])
            s0 = jnp.zeros((bsz, B_HEADS, B_DK, B_DV), f32)
            sp, op = lax.scan(gla_chunk, s0, (to_chunks(qp), to_chunks(kp), to_chunks(vp), to_chunks(gp)))
            dp = hgrn_out(from_chunks(op), gatep, hgrn_g_norm[j], hgrn_w_out[j])
            qs, kss, vs, gs, gates = hgrn_project(hs, hgrn_w_in[j], lower_bounds[li])
            ss, o_s = gla_chunk(state_hgrn[j].astype(f32), (qs, kss, vs, gs))
            ds_ = hgrn_out(o_s, gates, hgrn_g_norm[j], hgrn_w_out[j])
            hg_p.append(sp)
            hg_s.append(ss)
        else:
            dp, bufp, hlp = rglru_layer(hp, jnp.zeros((bsz, C_CONV - 1, C_WIDTH), hp.dtype), jnp.zeros((bsz, C_WIDTH), f32),
                                        rglru_w_in[j], rglru_conv_w[j], rglru_conv_b[j], rglru_w_a[j], rglru_b_a[j],
                                        rglru_w_x[j], rglru_b_x[j], rglru_L[j], rglru_w_out[j])
            ds_, bufs, hls = rglru_layer(hs, state_conv[j], state_lru[j],
                                         rglru_w_in[j], rglru_conv_w[j], rglru_conv_b[j], rglru_w_a[j], rglru_b_a[j],
                                         rglru_w_x[j], rglru_b_x[j], rglru_L[j], rglru_w_out[j])
            cv_p.append(bufp)
            cv_s.append(bufs)
            lr_p.append(hlp)
            lr_s.append(hls)
        xp = xp + dp.astype(xp.dtype)
        xs = xs + ds_.astype(xs.dtype)

    new_ckv_prompt = jnp.stack(ckv_p)
    new_kpe_prompt = jnp.stack(kpe_p)
    new_ckv_sample = jnp.stack(ckv_s)
    new_kpe_sample = jnp.stack(kpe_s)
    hgrn_prompt = jnp.stack(hg_p)
    hgrn_sample = jnp.stack(hg_s)
    conv_prompt = jnp.stack(cv_p)
    conv_sample = jnp.stack(cv_s)
    lru_prompt = jnp.stack(lr_p)
    lru_sample = jnp.stack(lr_s)
    return (xp, xs, new_ckv_prompt, new_kpe_prompt, new_ckv_sample, new_kpe_sample,
            hgrn_prompt, hgrn_sample, conv_prompt, conv_sample, lru_prompt, lru_sample)


_drawn_inputs = setup_inputs


def setup_inputs(seed=0):
    import zlib

    import numpy as np

    out = dict(_drawn_inputs(seed))
    spreads = {}
    factors = {'cache_kpe': 3.447, 'mla_g_q_lora': 5.345, 'mla_g_q': 5.729, 'mla_g_k': 5.839}
    for name, (base, spread) in spreads.items():
        noise = np.random.default_rng([zlib.crc32(name.encode()), seed]).standard_normal(out[name].shape)
        drawn = base * np.exp(spread * noise) if base else spread * noise
        out[name] = __import__('jax').numpy.asarray(drawn.astype(out[name].dtype))
    for name, factor in factors.items():
        out[name] = (out[name] * factor).astype(out[name].dtype)
    return out
```

```python
from contextlib import ExitStack

import concourse.bass as bass
import numpy as np
from concourse import mybir

F32 = mybir.dt.float32
I32 = mybir.dt.int32
ACT = mybir.ActivationFunctionType
ALU = mybir.AluOpType
AX = mybir.AxisListType

P = 128
D = 1024
KD = D // P
SEQ = 1024
NS = 8
T = SEQ + NS
NT = 3
TT = T // NT
QT = SEQ // P
EPS = 1e-6

H = 8
NOPE, ROPE, DV = 64, 32, 64
QK = NOPE + ROPE
QL, KVL = 384, 256
NQL, NKV = QL // P, KVL // P
NG = H * DV // P
PAGES, PAGE = 16, 128
NAT = KVL + ROPE
SCALE = QK ** -0.5

LEVELS = 7
C_ONE, C_EPS, C_LNSCALE = 0, 1, 2
TINY = [1.0, EPS, float(np.log(SCALE))]


def wait(engine, sem, count):
    if not (isinstance(count, int) and count <= 0):
        engine.wait_ge(sem, count)


def tiles(n=NT):
    return [(t, slice(t * TT, (t + 1) * TT)) for t in range(n)]


class Chip:

    def __init__(self, nc, ctx, dram):
        self.nc, self.dram = nc, dram

        def sb(name, shape, dt=F32):
            return ctx.enter_context(nc.sbuf_tensor(name, shape, dt))

        self.x = sb("residual", [P, KD, T])
        self.h = sb("normed", [P, KD, T])
        self.ident = sb("ident", [P, P])
        self.ones = sb("ones", [P, P])
        self.const = sb("const", [P, len(TINY)])
        self.gains = sb("gains", [P, 4, KD])
        self.ps = ctx.enter_context(nc.psum_tensor("ps", [P, 8, 512], F32))

    def eps(self, rows=P):
        return self.const[0:rows, C_EPS:C_EPS + 1]


MOST_SEMS = 64


class Stage:

    count = 0
    used = []

    def __init__(self, c):
        self.nc = c.nc
        self.ctx = ExitStack()
        self.sems = []
        self.tag = f"_{Stage.count}"
        Stage.count += 1

    def __enter__(self):
        self.ctx.__enter__()
        return self

    def __exit__(self, *a):
        done = self.ctx.__exit__(*a)
        Stage.used += self.sems
        if len(self.nc.free_semaphores) < MOST_SEMS:
            self.nc.clear_and_free_semaphores(Stage.used)
            self.nc.all_engine_barrier()
            Stage.used = []
        return done

    def sb(self, name, shape, dt=F32):
        return self.ctx.enter_context(self.nc.sbuf_tensor(name + self.tag, shape, dt))

    def sem(self, name):
        self.sems.append(self.nc.alloc_semaphore(name + self.tag))
        return self.sems[-1]

    def block(self):
        return self.ctx.enter_context(self.nc.Block())


def load_inputs(c):
    nc, dram = c.nc, c.dram
    with Stage(c) as st:
        landed = st.sem("inputs_landed")
        block = st.block()

        @block.sync
        def _(sp):
            sp.dma_start(c.x[:, :, :], dram["x"]).then_inc(landed, 16)
            sp.dma_start(c.ident[:, :], dram["ident"]).then_inc(landed, 16)
            sp.dma_start(c.ones[:, :], dram["ones"]).then_inc(landed, 16)
            sp.dma_start(c.const[:, :], dram["const"]).then_inc(landed, 16)
            sp.dma_start(c.gains[:, :, :], dram["norm_g"]).then_inc(landed, 16)
            sp.wait_ge(landed, 16 * 5)


def rms_norm(c, layer):
    nc = c.nc
    with Stage(c) as st:
        sq = st.sb("squares", [P, 2, T])
        rstd = st.sb("rstd", [P, T])
        squared = st.sem("squared")
        summed = st.sem("summed")
        logged = st.sem("logged")
        rstd_ready = st.sem("rstd_ready")
        block = st.block()
        sums = c.ps[:, 0:NT, 0:TT]

        @block.scalar
        def _(act):
            for k in range(KD):
                if k >= 2:
                    act.wait_ge(summed, k - 1)
                nc.scalar.activation(sq[:, k % 2, :], c.x[:, k, :], ACT.Square).then_inc(squared, 1)
            act.wait_ge(summed, KD)
            nc.scalar.activation(rstd[:, :].rearrange("p (a t) -> p a t", a=NT), sums, ACT.Ln,
                                 scale=1.0 / D, bias=c.eps()).then_inc(logged, 1)
            act.wait_ge(logged, 1)
            nc.scalar.activation(rstd[:, :], rstd[:, :], ACT.Exp, scale=-0.5).then_inc(rstd_ready, 1)

        @block.tensor
        def _(pe):
            for k in range(KD):
                pe.wait_ge(squared, k + 1)
                for t, cols in tiles():
                    mm = nc.tensor.matmul(c.ps[:, t, 0:TT], c.ones[:, :], sq[:, k % 2, cols],
                                          start=(k == 0), stop=(k == KD - 1))
                mm.then_inc(summed, 1)

        @block.vector
        def _(dve):
            dve.wait_ge(rstd_ready, 1)
            for k in range(KD):
                nc.vector.scalar_tensor_tensor(c.h[:, k, :], c.x[:, k, :], c.gains[:, layer, k:k + 1],
                                               rstd[:, :], op0=ALU.mult, op1=ALU.mult)


def streamed_projection(c, w, blocks, kt, src, drain):
    nc = c.nc
    with Stage(c) as st:
        ws = st.sb("w_slots", [P, 2, kt, P])
        w_landed = [st.sem("w_landed0"), st.sem("w_landed1")]
        summed = st.sem("block_summed")
        drained = st.sem("block_drained")
        block = st.block()
        pairs = blocks // 2

        @block.sync
        def _(sp):
            for u in range(2):
                sp.dma_start(ws[:, u, :, :], w[u]).then_inc(w_landed[u], 16)
            with sp.Fori(1, pairs) as i:
                for u in range(2):
                    sp.wait_ge(summed, 2 * i + (u - 1))
                    sp.dma_start(ws[:, u, :, :], w[bass.ds(2 * i + u, 1)].rearrange("a p k m -> p (a k) m")) \
                      .then_inc(w_landed[u], 16)
            if blocks % 2:
                sp.wait_ge(summed, blocks - 2)
                sp.dma_start(ws[:, 0, :, :], w[blocks - 1]).then_inc(w_landed[0], 16)

        @block.tensor
        def _(pe):
            def one(m, u, landed, first=False):
                pe.wait_ge(w_landed[u], landed)
                if not first:
                    pe.wait_ge(drained, m - 1)
                for t, cols in tiles():
                    for k in range(kt):
                        mm = nc.tensor.matmul(c.ps[:, NT * u + t, 0:TT], ws[:, u, k, :], src[:, k, cols],
                                              start=(k == 0), stop=(k == kt - 1))
                mm.then_inc(summed, 1)

            for u in range(2):
                one(u, u, 16, first=True)
            with pe.Fori(1, pairs) as i:
                for u in range(2):
                    one(2 * i + u, u, 16 * i + 16)
            if blocks % 2:
                one(blocks - 1, 0, 16 * (pairs + 1))

        @block.vector
        def _(dve):
            def one(m, u):
                dve.wait_ge(summed, m + 1)
                drain(m, c.ps[:, NT * u:NT * u + NT, 0:TT]).then_inc(drained, 1)

            with dve.Fori(0, pairs) as i:
                for u in range(2):
                    one(2 * i + u, u)
            if blocks % 2:
                one(blocks - 1, 0)


def split_tiles(ap):
    return ap.rearrange("p (a t) -> p a t", a=NT)


def block_of(buf, m):
    return buf[:, bass.ds(m, 1), :].rearrange("p b (a t) -> p (b a) t", a=NT)


def output_projection(c, w, kt, src):
    streamed_projection(c, w, KD, kt, src, lambda m, psum: c.nc.vector.tensor_tensor(
        block_of(c.x, m), psum, block_of(c.x, m), ALU.add))



class Mla:

    def __init__(self, st):
        self.z = st.sb("latents", [P, NQL + NKV + NG, T])
        self.cq = self.z[:, 0:NQL, :]
        self.ckv = self.z[:, NQL:NQL + NKV, :]
        self.gate = self.z[:, NQL + NKV:, :]
        self.trig = st.sb("trig", [P, T])
        self.kraw = st.sb("kraw", [P, T])
        self.v = st.sb("values", [P, QT + 1, H * DV])
        self.wuv = st.sb("w_uv", [P, NKV, H * DV])
        self.qs = st.sb("sample_queries", [QK, H, NS])
        self.snew = st.sb("new_token_scores", [P, NS, H])
        self.accn = st.sb("sample_latents", [P, NKV, H, NS])


def latent_norm(nc, c, engine, which, buf, n, width, gain, sq, rstd, s):
    if which == "scalar":
        for k in range(n):
            if k >= 2:
                engine.wait_ge(s["summed"], k - 1)
            nc.scalar.activation(sq[:, k % 2, :], buf[:, k, :], ACT.Square).then_inc(s["squared"], 1)
        engine.wait_ge(s["summed"], n)
        nc.scalar.activation(split_tiles(rstd[:, :]), c.ps[:, NT:2 * NT, 0:TT], ACT.Ln,
                             scale=1.0 / width, bias=c.eps()).then_inc(s["logged"], 1)
        engine.wait_ge(s["logged"], 1)
        nc.scalar.activation(rstd[:, :], rstd[:, :], ACT.Exp, scale=-0.5).then_inc(s["rstd"], 1)
    elif which == "tensor":
        for k in range(n):
            engine.wait_ge(s["squared"], k + 1)
            for t, cols in tiles():
                mm = nc.tensor.matmul(c.ps[:, NT + t, 0:TT], c.ones[:, :], sq[:, k % 2, cols],
                                      start=(k == 0), stop=(k == n - 1))
            mm.then_inc(s["summed"], 1)
    else:
        engine.wait_ge(s["rstd"], 1)
        for k in range(n):
            nc.vector.scalar_tensor_tensor(buf[:, k, :], buf[:, k, :], gain[:, k:k + 1], rstd[:, :],
                                           op0=ALU.mult, op1=ALU.mult).then_inc(s["done"], 1)


def mla_latents(c, m, j):
    nc, dram = c.nc, c.dram
    with Stage(c) as st:
        wkpe = st.sb("w_kpe", [P, KD, 2 * ROPE])
        gql = st.sb("g_q_lora", [P, NQL])
        gkv = st.sb("g_kv", [P, NKV])
        sq = st.sb("squares", [P, 2, T])
        rstd = st.sb("rstd", [P, 2, T])
        rot = st.sb("rotated", [P, 2, T])
        loads = st.sem("loads")
        kpe_summed = st.sem("kpe_summed")
        kpe_parts = st.sem("kpe_parts")
        kpe_done = st.sem("kpe_done")
        sem_kv = {k: st.sem("ckv_" + k) for k in ("squared", "summed", "logged", "rstd", "done")}
        sem_q = {k: st.sem("cq_" + k) for k in ("squared", "summed", "logged", "rstd", "done")}
        v_summed = st.sem("v_summed")
        v_drained = st.sem("v_drained")
        stored = st.sem("stored")
        block = st.block()

        @block.sync
        def _(sp):
            sp.dma_start(wkpe[:, :, :], dram["w_kpe"][j]).then_inc(loads, 16)
            sp.dma_start(m.trig[:, :], dram["trig"]).then_inc(loads, 16)
            sp.dma_start(gql[:, :], dram["g_q_lora"][j]).then_inc(loads, 16)
            sp.dma_start(gkv[:, :], dram["g_kv"][j]).then_inc(loads, 16)
            sp.dma_start(m.wuv[:, :, :], dram["w_uv"][j]).then_inc(loads, 16)
            sp.wait_ge(sem_kv["done"], NKV)
            sp.dma_start(dram["o_ckv"][j], m.ckv).then_inc(stored, 16)
            sp.wait_ge(kpe_done, 1)
            sp.dma_start(dram["o_kpe"][j], m.kraw[NOPE:QK, :]).then_inc(stored, 16)
            sp.wait_ge(stored, 32)

        @block.tensor
        def _(pe):
            latent_norm(nc, c, pe, "tensor", m.ckv, NKV, KVL, gkv, sq, rstd[:, 0, :], sem_kv)
            pe.wait_ge(loads, 16 * 5)
            for t, cols in tiles():
                for k in range(KD):
                    mm = nc.tensor.matmul(c.ps[NOPE:P, t, 0:TT], wkpe[:, k, :], c.h[:, k, cols],
                                          start=(k == 0), stop=(k == KD - 1))
            mm.then_inc(kpe_summed, 1)
            pe.wait_ge(sem_kv["logged"], 1)
            latent_norm(nc, c, pe, "tensor", m.cq, NQL, QL, gql, sq, rstd[:, 1, :], sem_q)
            pe.wait_ge(sem_kv["done"], NKV)
            for tt in range(QT + 1):
                rows = P if tt < QT else NS
                if tt >= 2:
                    pe.wait_ge(v_drained, tt - 1)
                for k in range(NKV):
                    mm = nc.tensor.matmul(c.ps[0:rows, 6 + tt % 2, :], m.ckv[:, k, tt * P:tt * P + rows],
                                          m.wuv[:, k, :], start=(k == 0), stop=(k == NKV - 1))
                mm.then_inc(v_summed, 1)

        @block.scalar
        def _(act):
            latent_norm(nc, c, act, "scalar", m.ckv, NKV, KVL, gkv, sq, rstd[:, 0, :], sem_kv)
            latent_norm(nc, c, act, "scalar", m.cq, NQL, QL, gql, sq, rstd[:, 1, :], sem_q)
            for tt in range(QT + 1):
                rows = P if tt < QT else NS
                act.wait_ge(v_summed, tt + 1)
                nc.scalar.activation(m.v[0:rows, tt, :], c.ps[0:rows, 6 + tt % 2, :], ACT.Copy) \
                  .then_inc(v_drained, 1)
            for k in range(NG):
                nc.scalar.activation(m.gate[:, k, :], m.gate[:, k, :], ACT.Silu)

        @block.vector
        def _(dve):
            dve.wait_ge(loads, 16 * 5)
            latent_norm(nc, c, dve, "vector", m.ckv, NKV, KVL, gkv, sq, rstd[:, 0, :], sem_kv)
            dve.wait_ge(kpe_summed, 1)
            nc.vector.tensor_tensor(split_tiles(rot[NOPE:QK, 0, :]), c.ps[NOPE:QK, 0:NT, 0:TT],
                                    split_tiles(m.trig[NOPE:QK, :]), ALU.mult).then_inc(kpe_parts, 1)
            nc.vector.tensor_tensor(split_tiles(rot[NOPE:QK, 1, :]), c.ps[QK:P, 0:NT, 0:TT],
                                    split_tiles(m.trig[QK:P, :]), ALU.mult).then_inc(kpe_parts, 1)
            dve.wait_ge(kpe_parts, 2)
            nc.vector.tensor_tensor(m.kraw[NOPE:QK, :], rot[NOPE:QK, 0, :], rot[NOPE:QK, 1, :],
                                    ALU.add).then_inc(kpe_done, 1)
            latent_norm(nc, c, dve, "vector", m.cq, NQL, QL, gql, sq, rstd[:, 1, :], sem_q)


def mla_prompt_attention(c, m, j, o_tok):
    nc, dram = c.nc, c.dram
    with Stage(c) as st:
        wq = st.sb("w_q", [P, 2, NQL, P])
        wk = st.sb("w_k", [P, 2, NKV, NOPE])
        q = st.sb("q", [P, 2, T])
        kn = st.sb("kn", [P, 2, T])
        qraw = st.sb("qraw", [P, T])
        rot = st.sb("rotated", [P, 2, TT])
        sq_q = st.sb("sq_q", [P, T])
        sq_k = st.sb("sq_k", [P, T])
        rk = st.sb("rk", [P, T])
        probs = st.sb("probs", [P, 2, SEQ])
        probs_t = st.sb("probs_t", [P, 2, 512])
        causal = st.sb("causal", [P, P])
        gq = st.sb("g_q", [QK, 2])
        gqk = st.sb("g_qk", [QK, 1])
        rq = st.sb("rq", [P, 2, 2 * QT])
        nmax = st.sb("nmax", [P, 2])
        bias = st.sb("bias", [P, 2])
        rowsum = st.sb("rowsum", [P, 2])
        inv = st.sb("inv", [P, 2])
        prod = st.sb("prod", [QK, NS])
        qs_now = st.sb("qs_now", [QK, NS])
        S = [c.ps[:, 0:2, :].rearrange("p a n -> p (a n)"), c.ps[:, 2:4, :].rearrange("p a n -> p (a n)")]
        X = c.ps[:, 7, :]

        loads = st.sem("loads")
        w_landed = [st.sem("w_landed0"), st.sem("w_landed1")]
        gains_done = st.sem("gains_done")
        x_summed = st.sem("x_summed")
        q_parts = st.sem("q_parts")
        qraw_done = st.sem("qraw_done")
        kraw_done = st.sem("kraw_done")
        sq_q_done = st.sem("sq_q_done")
        sq_k_done = st.sem("sq_k_done")
        q_done = st.sem("q_done")
        rk_logged = st.sem("rk_logged")
        rk_done = st.sem("rk_done")
        kn_done = st.sem("kn_done")
        rq_logged = st.sem("rq_logged")
        rq_done = st.sem("rq_done")
        qs_done = st.sem("qs_done")
        prod_done = st.sem("prod_done")
        scored = st.sem("scored")
        masked = st.sem("masked")
        maxed = st.sem("maxed")
        snew_done = st.sem("snew_done")
        bias_done = st.sem("bias_done")
        exped = st.sem("exped")
        turned = st.sem("turned")
        pt_ready = st.sem("pt_ready")
        pv_read = st.sem("pv_read")
        inverted = st.sem("inverted")
        o_stored = st.sem("o_stored")
        block = st.block()

        NX = 11
        batches = [(qt, b) for qt in range(QT) for b in range(qt // 4 + 1)]
        NB = len(batches)
        of_tile = [[(n, b) for n, (q_, b) in enumerate(batches) if q_ == qt] for qt in range(QT)]

        def heads(engine, attend):
            attend(0, 0, 1)
            with engine.Fori(0, (H - 2) // 2) as i:
                attend(2 * i + 1, 1, 2 * i + 2)
                attend(2 * i + 2, 0, 2 * i + 3)
            attend(H - 1, 1, None)

        @block.sync
        def _(sp):
            sp.dma_start(causal[:, :], dram["causal"]).then_inc(loads, 16)
            sp.dma_start(gq[:, :], dram["g_qk"][j]).then_inc(loads, 16)

            def load(h, u):
                for slot, w in ((wq, dram["w_uq"][j]), (wk, dram["w_uk"][j])):
                    sp.dma_start(slot[:, u, :, :], w[bass.ds(h, 1)].rearrange("a p k m -> p (a k) m")) \
                      .then_inc(w_landed[u], 16)

            for u in range(2):
                load(u, u)
            with sp.Fori(1, H // 2) as i:
                for u in range(2):
                    sp.wait_ge(x_summed, 2 * NX * i + (NX * u - 2 * NX + 2 * NT))
                    load(2 * i + u, u)

        @block.gpsimd
        def _(pool):
            def scale_q(h, u):
                pool.wait_ge(qraw_done, NT * h + NT)
                wait(pool, scored, QT * h - QT)
                nc.gpsimd.tensor_tensor(q[0:QK, u, :], qraw[0:QK, :], gqk[:, 0:1].broadcast_to([QK, T]),
                                        ALU.mult).then_inc(q_done, 1)

            pool.wait_ge(gains_done, 1)
            scale_q(0, 0)
            scale_q(1, 1)
            with pool.Fori(1, H // 2) as i:
                for u in range(2):
                    scale_q(2 * i + u, u)

        @block.tensor
        def _(pe):
            def prep(h, u):
                def q_tile(t, cols):
                    def f():
                        if t == 0:
                            wait(pe, snew_done, h)
                            pe.wait_ge(w_landed[u], 16 * h + (32 - 16 * u))
                        else:
                            pe.wait_ge(qraw_done, NT * h + t)
                        for k in range(NQL):
                            mm = nc.tensor.matmul(X[:, 0:TT], wq[:, u, k, :], m.cq[:, k, cols],
                                                  start=(k == 0), stop=(k == NQL - 1))
                        mm.then_inc(x_summed, 1)
                    return f

                def k_tile(t, cols):
                    def f():
                        if t == 0:
                            pe.wait_ge(qraw_done, NT * h + NT)
                        else:
                            pe.wait_ge(kraw_done, NT * h + t)
                        for k in range(NKV):
                            mm = nc.tensor.matmul(X[0:NOPE, 0:TT], wk[:, u, k, :], m.ckv[:, k, cols],
                                                  start=(k == 0), stop=(k == NKV - 1))
                        mm.then_inc(x_summed, 1)
                    return f

                def k_sums(t, cols):
                    def f():
                        if t == 0:
                            pe.wait_ge(sq_k_done, h + 1)
                        else:
                            pe.wait_ge(rk_logged, NT * h + t)
                        nc.tensor.matmul(X[0:QK, 0:TT], c.ones[0:QK, 0:QK], sq_k[0:QK, cols],
                                         start=True, stop=True).then_inc(x_summed, 1)
                    return f

                def q_sums():
                    pe.wait_ge(rk_logged, NT * h + NT)
                    pe.wait_ge(sq_q_done, h + 1)
                    for qt in range(QT):
                        nc.tensor.matmul(X[:, qt:qt + 1], sq_q[0:QK, qt * P:(qt + 1) * P], c.ones[0:QK, 0:1],
                                         start=True, stop=True)
                    nc.tensor.matmul(X[:, QT:QT + NS], c.ones[0:QK, :], sq_q[0:QK, SEQ:T],
                                     start=True, stop=True).then_inc(x_summed, 1)

                def new_scores():
                    pe.wait_ge(prod_done, h + 1)
                    nc.tensor.matmul(X[:, 0:NS], c.ones[0:QK, :], prod[:, :],
                                     start=True, stop=True).then_inc(x_summed, 1)

                qs = [q_tile(*x) for x in tiles()]
                ks = [k_tile(*x) for x in tiles()]
                rs = [k_sums(*x) for x in tiles()]
                return {0: qs[0], 1: qs[1], 2: qs[2], 3: ks[0], 4: ks[1], 5: ks[2],
                        7: rs[0], 8: rs[1], 9: rs[2], 10: q_sums, 13: new_scores}

            def attend(h, u, following):
                steps = {} if following is None else prep(following, 1 - u)

                def place(n):
                    if n in steps:
                        steps[n]()

                def scores(qt):
                    if qt == 0:
                        pe.wait_ge(q_done, h + 1)
                        pe.wait_ge(kn_done, h + 1)
                    wait(pe, exped, QT * h + (qt - 1))
                    n = (qt + 1) * P
                    for lo in range(0, n, 512):
                        hi = min(n, lo + 512)
                        mm = nc.tensor.matmul(S[qt % 2][:, lo:hi], q[0:QK, u, qt * P:(qt + 1) * P],
                                              kn[0:QK, u, lo:hi], start=True, stop=True)
                    mm.then_inc(scored, 1)

                scores(0)
                for qt in range(QT):
                    if qt + 1 < QT:
                        scores(qt + 1)
                    place(2 * qt)
                    pe.wait_ge(exped, QT * h + (qt + 1))
                    for n, b in of_tile[qt]:
                        wait(pe, pt_ready, NB * h + (n - 1))
                        for kt in range(4 * b, min(4 * b + 4, qt + 1)):
                            mm = nc.tensor.transpose(c.ps[:, 4 + n % 2, (kt % 4) * P:(kt % 4 + 1) * P],
                                                     probs[:, qt % 2, kt * P:(kt + 1) * P], c.ident[:, :])
                        mm.then_inc(turned, 1)
                    place(2 * qt + 1)
                    wait(pe, o_stored, QT * h + qt)
                    for n, b in of_tile[qt]:
                        pe.wait_ge(pt_ready, NB * h + (n + 1))
                        for kt in range(4 * b, min(4 * b + 4, qt + 1)):
                            mm = nc.tensor.matmul(c.ps[:, 6, 0:DV],
                                                  probs_t[:, n % 2, (kt % 4) * P:(kt % 4 + 1) * P],
                                                  m.v[:, kt, bass.ds(h * DV, DV)],
                                                  start=(kt == 0), stop=(kt == qt))
                        mm.then_inc(pv_read, 1)

            pe.wait_ge(loads, 32)
            for f in prep(0, 0).values():
                f()
            heads(pe, attend)

        @block.vector
        def _(dve):
            def prep(h, u):
                def q_tile(t, cols):
                    def f():
                        dve.wait_ge(x_summed, NX * h + (t + 1))
                        if t == 0:
                            wait(dve, q_done, h)
                            wait(dve, sq_q_done, h)
                        nc.vector.tensor_copy(qraw[0:NOPE, cols], X[0:NOPE, 0:TT]).then_inc(q_parts, 1)
                        nc.vector.tensor_tensor(rot[NOPE:QK, 0, :], X[NOPE:QK, 0:TT], m.trig[NOPE:QK, cols],
                                                ALU.mult).then_inc(q_parts, 1)
                        nc.vector.tensor_tensor(rot[NOPE:QK, 1, :], X[QK:P, 0:TT], m.trig[QK:P, cols],
                                                ALU.mult).then_inc(q_parts, 1)
                        dve.wait_ge(q_parts, 3 * NT * h + 3 * (t + 1))
                        nc.vector.tensor_tensor(qraw[NOPE:QK, cols], rot[NOPE:QK, 0, :], rot[NOPE:QK, 1, :],
                                                ALU.add).then_inc(qraw_done, 1)
                    return f

                def k_tile(t, cols):
                    def f():
                        dve.wait_ge(x_summed, NX * h + (NT + t + 1))
                        if t == 0:
                            wait(dve, kn_done, h)
                            wait(dve, sq_k_done, h)
                        nc.vector.tensor_copy(m.kraw[0:NOPE, cols], X[0:NOPE, 0:TT]).then_inc(kraw_done, 1)
                    return f

                def keys():
                    dve.wait_ge(rk_done, h + 1)
                    wait(dve, scored, QT * h - QT)
                    nc.vector.tensor_tensor(kn[0:QK, u, :], m.kraw[0:QK, :], rk[0:QK, :], ALU.mult) \
                      .then_inc(kn_done, 1)

                def sample_queries():
                    dve.wait_ge(rq_done, h + 1)
                    dve.wait_ge(q_done, h + 1)
                    wait(dve, x_summed, NX * h)
                    nc.vector.tensor_tensor(qs_now[:, :], q[0:QK, u, SEQ:T], rq[0:QK, u, QT:QT + NS],
                                            ALU.mult).then_inc(qs_done, 1)
                    dve.wait_ge(qs_done, 2 * h + 1)
                    dve.wait_ge(kn_done, h + 1)
                    nc.vector.tensor_tensor(prod[:, :], qs_now[:, :], kn[0:QK, u, SEQ:T],
                                            ALU.mult).then_inc(prod_done, 1)
                    nc.vector.tensor_copy(m.qs[:, bass.ds(h, 1), :].rearrange("p a n -> p (a n)"), qs_now[:, :]) \
                      .then_inc(qs_done, 1)

                def new_scores():
                    dve.wait_ge(x_summed, NX * h + NX)
                    dve.wait_ge(qs_done, 2 * h + 2)
                    nc.vector.tensor_copy(m.snew[:, :, bass.ds(h, 1)].rearrange("p n a -> p (n a)"),
                                          X[:, 0:NS]).then_inc(snew_done, 1)

                qs = [q_tile(*x) for x in tiles()]
                ks = [k_tile(*x) for x in tiles()]
                return {0: qs[0], 1: qs[1], 2: qs[2], 3: ks[0], 4: ks[1], 5: ks[2],
                        10: keys, 12: sample_queries, 14: new_scores}

            def attend(h, u, following):
                steps = {} if following is None else prep(following, 1 - u)

                def place(n):
                    if n in steps:
                        steps[n]()

                def row_max(qt):
                    b = qt % 2
                    diag = S[b][:, qt * P:(qt + 1) * P]
                    dve.wait_ge(scored, QT * h + (qt + 1))
                    nc.vector.tensor_tensor(diag, diag, causal[:, :], ALU.add).then_inc(masked, 1)
                    dve.wait_ge(masked, QT * h + (qt + 1))
                    nc.vector.tensor_reduce(nmax[:, b:b + 1], S[b][:, 0:(qt + 1) * P], AX.X, ALU.max,
                                            negate=True).then_inc(maxed, 1)
                    dve.wait_ge(maxed, QT * h + (qt + 1))
                    wait(dve, exped, QT * h + (qt - 1))
                    nc.vector.tensor_tensor(bias[:, b:b + 1], nmax[:, b:b + 1], rq[:, u, qt:qt + 1],
                                            ALU.mult).then_inc(bias_done, 1)

                row_max(0)
                for qt in range(QT):
                    if qt + 1 < QT:
                        row_max(qt + 1)
                    place(2 * qt)
                    for n, b in of_tile[qt]:
                        width = (min(4 * b + 4, qt + 1) - 4 * b) * P
                        dve.wait_ge(turned, NB * h + (n + 1))
                        wait(dve, pv_read, NB * h + (n - 1))
                        nc.vector.tensor_copy(probs_t[:, n % 2, 0:width], c.ps[:, 4 + n % 2, 0:width]) \
                          .then_inc(pt_ready, 1)
                    place(2 * qt + 1)
                    dve.wait_ge(exped, QT * h + (qt + 1))
                    nc.vector.reciprocal(inv[:, qt % 2:qt % 2 + 1], rowsum[:, qt % 2:qt % 2 + 1]) \
                      .then_inc(inverted, 1)
                    dve.wait_ge(inverted, QT * h + (qt + 1))
                    dve.wait_ge(pv_read, NB * h + (of_tile[qt][-1][0] + 1))
                    nc.vector.tensor_scalar(o_tok[:, qt, bass.ds(h * DV, DV)], c.ps[:, 6, 0:DV],
                                            inv[:, qt % 2:qt % 2 + 1], None, op0=ALU.mult) \
                      .then_inc(o_stored, 1)

            dve.wait_ge(loads, 32)
            nc.vector.tensor_tensor(gqk[:, :], gq[:, 0:1], gq[:, 1:2], ALU.mult).then_inc(gains_done, 1)
            for f in prep(0, 0).values():
                f()
            heads(dve, attend)

        @block.scalar
        def _(act):
            def prep(h, u):
                def q_squares():
                    act.wait_ge(qraw_done, NT * h + NT)
                    wait(act, x_summed, NX * h)
                    nc.scalar.activation(sq_q[0:QK, :], qraw[0:QK, :], ACT.Square).then_inc(sq_q_done, 1)

                def k_squares():
                    act.wait_ge(kraw_done, NT * h + NT)
                    nc.scalar.activation(sq_k[0:QK, :], m.kraw[0:QK, :], ACT.Square).then_inc(sq_k_done, 1)

                def k_log(t, cols):
                    def f():
                        act.wait_ge(x_summed, NX * h + (2 * NT + t + 1))
                        if t == 0:
                            wait(act, kn_done, h)
                        nc.scalar.activation(rk[0:QK, cols], X[0:QK, 0:TT], ACT.Ln, scale=1.0 / QK,
                                             bias=c.eps(QK)).then_inc(rk_logged, 1)
                    return f

                def k_exp():
                    act.wait_ge(rk_logged, NT * h + NT)
                    nc.scalar.activation(rk[0:QK, :], rk[0:QK, :], ACT.Exp, scale=-0.5).then_inc(rk_done, 1)

                def q_log():
                    act.wait_ge(x_summed, NX * h + (NX - 1))
                    wait(act, exped, QT * h - QT)
                    wait(act, qs_done, 2 * h - 2)
                    nc.scalar.activation(rq[:, u, :], X[:, 0:2 * QT], ACT.Ln, scale=1.0 / QK,
                                         bias=c.eps()).then_inc(rq_logged, 1)

                def q_exp():
                    act.wait_ge(rq_logged, h + 1)
                    nc.scalar.activation(rq[:, u, :], rq[:, u, :], ACT.Exp, scale=-0.5,
                                         bias=c.const[:, C_LNSCALE:C_LNSCALE + 1]).then_inc(rq_done, 1)

                rs = [k_log(*x) for x in tiles()]
                return {3: [q_squares], 6: [k_squares], 7: [rs[0]], 8: [rs[1]], 9: [rs[2], k_exp],
                        10: [q_log], 11: [q_exp]}

            def attend(h, u, following):
                steps = {} if following is None else prep(following, 1 - u)
                for qt in range(QT):
                    act.wait_ge(bias_done, QT * h + (qt + 1))
                    if qt >= 2:
                        act.wait_ge(turned, NB * h + (of_tile[qt - 2][-1][0] + 1))
                        act.wait_ge(inverted, QT * h + (qt - 1))
                    else:
                        wait(act, turned, NB * h + (of_tile[QT - 2 + qt][-1][0] + 1 - NB))
                        wait(act, inverted, QT * h + (qt - 1))
                    n = (qt + 1) * P
                    nc.scalar.activation(probs[:, qt % 2, 0:n], S[qt % 2][:, 0:n], ACT.Exp,
                                         scale=rq[:, u, qt:qt + 1], bias=bias[:, qt % 2:qt % 2 + 1],
                                         accum_out=rowsum[:, qt % 2:qt % 2 + 1]).then_inc(exped, 1)
                    for n in (2 * qt, 2 * qt + 1):
                        for f in steps.get(n, []):
                            f()

            for fs in prep(0, 0).values():
                for f in fs:
                    f()
            heads(act, attend)


def mla_sample_attention(c, m, j):
    nc, dram = c.nc, c.dram
    with Stage(c) as st:
        nat = st.sb("pages", [P, 2, PAGES, NAT])
        RING = 4
        lat_t = st.sb("latents_t", [P, RING, NKV, PAGE])
        kpe_t = st.sb("kpe_t", [ROPE, RING, PAGE])
        wukt = st.sb("w_uk_t", [NOPE, H, KVL])
        wuk = st.sb("w_uk_all", [P, NKV, H * NOPE])
        table = st.sb("page_table", [1, NS * PAGES], I32)
        qlat = st.sb("latent_queries", [P, NKV, NS, H])
        qpe = st.sb("rope_queries", [ROPE, NS, H])
        sq = st.sb("key_squares", [P, 2, H * NOPE])
        kk = st.sb("kpe_squares", [P, 2, PAGES, ROPE])
        kks = st.sb("kpe_sums", [P, 2, PAGES])
        ss = st.sb("sums", [P, 2, PAGES, H])
        rk = st.sb("rk", [P, PAGES, H])
        sc = st.sb("scores", [P, PAGES, H])
        pr = st.sb("probs", [P, PAGES, H])
        mx = st.sb("max", [P, H])
        top = st.sb("top", [H, 1])
        diag = st.sb("diag", [H, H])
        mall = st.sb("max_all", [P, H])
        pnew = st.sb("new_prob", [P, H])
        lsum = st.sb("row_sums", [P, H])
        ltot = st.sb("total", [P, H])
        part = st.sb("new_part", [P, NKV, H])
        ckvs = st.sb("new_latents", [P, NS, NKV])

        loads = st.sem("loads")
        wk_landed = st.sem("wk_landed")
        nat_landed = [st.sem("nat_landed0"), st.sem("nat_landed1")]
        ring_landed = [st.sem(f"ring_landed{r}") for r in range(RING)]
        q_summed = st.sem("q_summed")
        q_ready = st.sem("q_ready")
        expanded = st.sem("expanded")
        squared = st.sem("squared")
        scored = st.sem("scored")
        ssum = st.sem("ssum")
        kk_done = st.sem("kk_done")
        kks_done = st.sem("kks_done")
        ss_done = st.sem("ss_done")
        rk_logged = st.sem("rk_logged")
        rk_done = st.sem("rk_done")
        sc_done = st.sem("sc_done")
        mx_done = st.sem("mx_done")
        mx_turned = st.sem("mx_turned")
        top_done = st.sem("top_done")
        diag_done = st.sem("diag_done")
        m_summed = st.sem("m_summed")
        m_done = st.sem("m_done")
        pn_done = st.sem("pn_done")
        pr_done = st.sem("pr_done")
        l_done = st.sem("l_done")
        l_summed = st.sem("l_summed")
        inv_done = st.sem("inv_done")
        weighted = st.sem("weighted")
        part_done = st.sem("part_done")
        acc_done = st.sem("acc_done")
        block = st.block()
        KEYS = [c.ps[:, 0, :], c.ps[:, 1, :]]
        SC = [c.ps[:, 2, 0:PAGES * H], c.ps[:, 3, 0:PAGES * H]]
        SMALL = c.ps[:, 4, :]
        ACC = c.ps[:, 5, 0:NKV * H]
        tok = dram["pages"][j]
        tok_t = dram["pages_t"][j]
        kp_t = dram["pages_kpe_t"][j]

        def sequences(engine, pages, tail):
            pages(0, 0, None)
            with engine.Fori(0, (NS - 2) // 2) as i:
                pages(2 * i + 1, 1, tail(2 * i, 0))
                pages(2 * i + 2, 0, tail(2 * i + 1, 1))
            pages(NS - 1, 1, tail(NS - 2, 0))
            for f in tail(NS - 1, 1).values():
                f()

        def run(steps, p):
            if steps is not None and p in steps:
                steps[p]()

        @block.sync
        def _(sp):
            sp.dma_start(table[:, :], dram["page_table"]).then_inc(loads, 16)
            sp.dma_start(wukt[:, :, :], dram["w_uk_t"][j]).then_inc(wk_landed, 16)
            sp.dma_start(wuk[:, :, :], dram["w_uk_all"][j]).then_inc(wk_landed, 16)
            sp.wait_ge(loads, 16)

            def pages(b, u, steps):
                wait(sp, weighted, b - 1)
                for p in range(PAGES):
                    r = p % RING
                    page = sp.value_load(table[0:1, bass.ds(b * PAGES + p, 1)], min_val=0,
                                         max_val=tok.shape[0] - 1)
                    wait(sp, scored, PAGES * b + (p + 1 - RING))
                    sp.dma_start(lat_t[:, r, :, :], tok_t[bass.ds(page, 1)].rearrange("a p k t -> p (a k) t")) \
                      .then_inc(ring_landed[r], 16)
                    sp.dma_start(kpe_t[:, r, :], kp_t[bass.ds(page, 1)].rearrange("a p t -> p (a t)")) \
                      .then_inc(ring_landed[r], 16)
                    sp.dma_start(nat[:, u, p, :], tok[bass.ds(page, 1)].rearrange("a p f -> p (a f)")) \
                      .then_inc(nat_landed[u], 16)

            pages(0, 0, None)
            pages(1, 1, None)
            with sp.Fori(1, NS // 2) as i:
                for u in range(2):
                    pages(2 * i + u, u, None)

        @block.gpsimd
        def _(pool):
            def kpe_squares(b, u):
                pool.wait_ge(nat_landed[u], 16 * PAGES * ((b - u) // 2 + 1) if isinstance(b, int)
                             else 8 * PAGES * b + (16 * PAGES - 8 * PAGES * u))
                wait(pool, kks_done, b - 1)
                nc.gpsimd.tensor_tensor(kk[:, u, :, :], nat[:, u, :, KVL:NAT], nat[:, u, :, KVL:NAT],
                                        ALU.mult).then_inc(kk_done, 1)

            kpe_squares(0, 0)
            kpe_squares(1, 1)
            with pool.Fori(1, NS // 2) as i:
                for u in range(2):
                    kpe_squares(2 * i + u, u)

        @block.tensor
        def _(pe):
            def tail(b, u):
                def turn_max():
                    pe.wait_ge(mx_done, 2 * b + 2)
                    wait(pe, inv_done, 2 * b)
                    nc.tensor.transpose(SMALL[0:H, 0:P], mx[:, :], c.ident[:, :]).then_inc(mx_turned, 1)

                def spread_max():
                    pe.wait_ge(diag_done, b + 1)
                    nc.tensor.matmul(SMALL[:, P:P + H], c.ones[0:H, :], diag[:, :],
                                     start=True, stop=True).then_inc(m_summed, 1)

                def weighted_sums():
                    pe.wait_ge(l_done, b + 1)
                    nc.tensor.matmul(SMALL[:, 2 * P:2 * P + H], c.ones[:, :], lsum[:, :],
                                     start=True, stop=True).then_inc(l_summed, 1)
                    wait(pe, acc_done, NKV * b)
                    for k in range(NKV):
                        for p in range(PAGES):
                            mm = nc.tensor.matmul(ACC[:, k * H:(k + 1) * H], nat[:, u, p, k * P:(k + 1) * P],
                                                  pr[:, p, :], start=(p == 0), stop=(p == PAGES - 1))
                    mm.then_inc(weighted, 1)

                return {4: turn_max, 6: spread_max, 9: weighted_sums}

            def pages(b, u, steps):
                for p in range(PAGES):
                    r, e = p % RING, p % 2
                    pe.wait_ge(ring_landed[r], 32 * (PAGES // RING) * b + 32 * (p // RING + 1))
                    wait(pe, squared, PAGES * b + (p - 1))
                    for k in range(NKV):
                        mm = nc.tensor.matmul(KEYS[e], lat_t[:, r, k, :], wuk[:, k, :],
                                              start=(k == 0), stop=(k == NKV - 1))
                    mm.then_inc(expanded, 1)
                    if p == 0:
                        wait(pe, sc_done, 2 * b - 2)
                    cols = slice(p * H, (p + 1) * H)
                    for k in range(NKV):
                        nc.tensor.matmul(SC[u][:, cols], lat_t[:, r, k, :],
                                         qlat[:, k, bass.ds(b, 1), :].rearrange("p a h -> p (a h)"),
                                         start=(k == 0), stop=False)
                    nc.tensor.matmul(SC[u][:, cols], kpe_t[:, r, :],
                                     qpe[:, bass.ds(b, 1), :].rearrange("p a h -> p (a h)"),
                                     start=False, stop=True).then_inc(scored, 1)
                    run(steps, p)

            pe.wait_ge(wk_landed, 32)
            for h in range(H):
                for k in range(NKV):
                    mm = nc.tensor.matmul(c.ps[:, 4 + k, h * NS:(h + 1) * NS], wukt[:, h, k * P:(k + 1) * P],
                                          m.qs[0:NOPE, h, :], start=True, stop=True)
            mm.then_inc(q_summed, 1)
            pe.wait_ge(q_ready, NKV + 1)
            sequences(pe, pages, tail)

        @block.scalar
        def _(act):
            def tail(b, u):
                def key_factor():
                    act.wait_ge(ss_done, b + 1)
                    wait(act, sc_done, 2 * b)
                    nc.scalar.activation(rk[:, :, :], ss[:, u, :, :], ACT.Ln, scale=1.0 / QK, bias=c.eps()) \
                      .then_inc(rk_logged, 1)
                    act.wait_ge(rk_logged, b + 1)
                    nc.scalar.activation(rk[:, :, :], rk[:, :, :], ACT.Exp, scale=-0.5).then_inc(rk_done, 1)

                def probabilities():
                    act.wait_ge(pn_done, b + 1)
                    wait(act, inv_done, 2 * b)
                    nc.scalar.activation(pnew[:, :], pnew[:, :], ACT.Exp).then_inc(pr_done, 1)
                    act.wait_ge(sc_done, 2 * b + 2)
                    wait(act, weighted, b)
                    nc.scalar.activation(pr[:, :, :], sc[:, :, :], ACT.Exp).then_inc(pr_done, 1)

                return {0: key_factor, 7: probabilities}

            def pages(b, u, steps):
                for p in range(PAGES):
                    e = p % 2
                    act.wait_ge(expanded, PAGES * b + (p + 1))
                    wait(act, ssum, PAGES * b + (p - 1))
                    nc.scalar.activation(sq[:, e, :], KEYS[e], ACT.Square).then_inc(squared, 1)
                    run(steps, p)

            sequences(act, pages, tail)

        @block.vector
        def _(dve):
            def tail(b, u):
                def finish_scores():
                    dve.wait_ge(rk_done, b + 1)
                    dve.wait_ge(scored, PAGES * b + PAGES)
                    wait(dve, pr_done, 2 * b)
                    nc.vector.tensor_tensor(sc[:, :, :], SC[u].rearrange("p (a h) -> p a h", a=PAGES),
                                            rk[:, :, :], ALU.mult).then_inc(sc_done, 1)
                    dve.wait_ge(sc_done, 2 * b + 1)
                    nc.vector.tensor_reduce(mx[:, :], sc[:, :, :].rearrange("p a h -> p h a"), AX.X, ALU.max) \
                      .then_inc(mx_done, 1)
                    dve.wait_ge(mx_done, 2 * b + 1)
                    nc.vector.tensor_tensor(mx[:, :], mx[:, :],
                                            m.snew[:, bass.ds(b, 1), :].rearrange("p a h -> p (a h)"),
                                            ALU.max).then_inc(mx_done, 1)

                def top_score():
                    dve.wait_ge(mx_turned, b + 1)
                    nc.vector.tensor_reduce(top[:, :], SMALL[0:H, 0:P], AX.X, ALU.max).then_inc(top_done, 1)
                    dve.wait_ge(top_done, b + 1)
                    nc.vector.tensor_scalar(diag[:, :], c.ident[0:H, 0:H], top[:, 0:1], None, op0=ALU.mult) \
                      .then_inc(diag_done, 1)

                def less_max():
                    dve.wait_ge(m_summed, b + 1)
                    nc.vector.tensor_copy(mall[:, :], SMALL[:, P:P + H]).then_inc(m_done, 1)
                    dve.wait_ge(m_done, b + 1)
                    nc.vector.tensor_tensor(pnew[:, :], m.snew[:, bass.ds(b, 1), :].rearrange("p a h -> p (a h)"),
                                            mall[:, :], ALU.subtract).then_inc(pn_done, 1)
                    nc.vector.tensor_tensor(sc[:, :, :], sc[:, :, :],
                                            mall[:, :].unsqueeze(1).broadcast_to([P, PAGES, H]),
                                            ALU.subtract).then_inc(sc_done, 1)

                def page_sums():
                    dve.wait_ge(pr_done, 2 * b + 2)
                    nc.vector.tensor_reduce(lsum[:, :], pr[:, :, :].rearrange("p a h -> p h a"), AX.X, ALU.add) \
                      .then_inc(l_done, 1)

                def divide():
                    dve.wait_ge(l_summed, b + 1)
                    nc.vector.tensor_tensor(ltot[:, :], SMALL[:, 2 * P:2 * P + H], pnew[:, :], ALU.add) \
                      .then_inc(inv_done, 1)
                    dve.wait_ge(inv_done, 2 * b + 1)
                    for k in range(NKV):
                        nc.vector.tensor_tensor(part[:, k, :], pnew[:, :],
                                                ckvs[:, bass.ds(b, 1), k:k + 1].rearrange("p a k -> p (a k)")
                                                .broadcast_to([P, H]), ALU.mult).then_inc(part_done, 1)
                    nc.vector.reciprocal(ltot[:, :], ltot[:, :]).then_inc(inv_done, 1)
                    dve.wait_ge(weighted, b + 1)
                    dve.wait_ge(part_done, 2 * NKV * b + NKV)
                    for k in range(NKV):
                        nc.vector.tensor_tensor(part[:, k, :], ACC[:, k * H:(k + 1) * H], part[:, k, :],
                                                ALU.add).then_inc(part_done, 1)
                    dve.wait_ge(part_done, 2 * NKV * b + 2 * NKV)
                    dve.wait_ge(inv_done, 2 * b + 2)
                    for k in range(NKV):
                        nc.vector.tensor_tensor(m.accn[:, k, :, bass.ds(b, 1)].rearrange("p h a -> p (h a)"),
                                                part[:, k, :], ltot[:, :], ALU.mult).then_inc(acc_done, 1)

                return {2: finish_scores, 4: top_score, 6: less_max, 8: page_sums, 12: divide}

            def pages(b, u, steps):
                for p in range(PAGES):
                    dve.wait_ge(squared, PAGES * b + (p + 1))
                    if p == 0:
                        wait(dve, rk_logged, b - 1)
                    nc.vector.tensor_reduce(ss[:, u, p, :], sq[:, p % 2, :].rearrange("p (h d) -> p h d", h=H),
                                            AX.X, ALU.add).then_inc(ssum, 1)
                    run(steps, p)
                dve.wait_ge(kk_done, b + 1)
                nc.vector.tensor_reduce(kks[:, u, :], kk[:, u, :, :], AX.X, ALU.add).then_inc(kks_done, 1)
                dve.wait_ge(kks_done, b + 1)
                dve.wait_ge(ssum, PAGES * b + PAGES)
                nc.vector.tensor_tensor(ss[:, u, :, :], ss[:, u, :, :],
                                        kks[:, u, :].unsqueeze(2).broadcast_to([P, PAGES, H]),
                                        ALU.add).then_inc(ss_done, 1)

            dve.wait_ge(q_summed, 1)
            for k in range(NKV):
                nc.vector.tensor_copy(qlat[:, k, :, :].rearrange("p n h -> p h n"),
                                      c.ps[:, 4 + k, 0:H * NS].rearrange("p (h n) -> p h n", h=H)) \
                  .then_inc(q_ready, 1)
                nc.vector.tensor_copy(ckvs[:, :, k], m.ckv[:, k, SEQ:T])
            nc.vector.tensor_copy(qpe[:, :, :].rearrange("p n h -> p h n"), m.qs[NOPE:QK, :, :]) \
              .then_inc(q_ready, 1)
            sequences(dve, pages, tail)


def mla_gated_values(c, m, o_tok):
    nc = c.nc
    with Stage(c) as st:
        summed = st.sem("summed")
        gated = st.sem("gated")
        s_summed = st.sem("s_summed")
        block = st.block()
        rounds = [(f, b) for f in range(NG) for b in range(QT // 4)]

        @block.tensor
        def _(pe):
            for n, (f, b) in enumerate(rounds):
                wait(pe, gated, n - 1)
                for t in range(4):
                    mm = nc.tensor.transpose(c.ps[:, n % 2, t * P:(t + 1) * P],
                                             o_tok[:, 4 * b + t, f * P:(f + 1) * P], c.ident[:, :])
                mm.then_inc(summed, 1)
            for f in range(NG):
                for k in range(NKV):
                    mm = nc.tensor.matmul(c.ps[:, 2, f * 2 * NS:(f + 1) * 2 * NS], m.wuv[:, k, f * P:(f + 1) * P],
                                          m.accn[:, k, 2 * f:2 * f + 2, :].rearrange("p h n -> p (h n)"),
                                          start=(k == 0), stop=(k == NKV - 1))
            mm.then_inc(s_summed, 1)

        @block.vector
        def _(dve):
            for n, (f, b) in enumerate(rounds):
                dve.wait_ge(summed, n + 1)
                g = m.gate[:, f, b * 512:(b + 1) * 512]
                nc.vector.tensor_tensor(g, c.ps[:, n % 2, :], g, ALU.mult).then_inc(gated, 1)
            dve.wait_ge(s_summed, 1)
            for f in range(NG):
                for e in range(2):
                    rows = slice(e * DV, (e + 1) * DV)
                    lo = f * 2 * NS + e * NS
                    nc.vector.tensor_tensor(m.gate[rows, f, SEQ:T], c.ps[rows, 2, lo:lo + NS],
                                            m.gate[rows, f, SEQ:T], ALU.mult)


def mla_layer(c, layer, j):
    rms_norm(c, layer)
    with Stage(c) as st:
        m = Mla(st)
        streamed_projection(c, c.dram["w_mla_in"][j], NQL + NKV + NG, KD, c.h,
                            lambda b, psum: c.nc.vector.tensor_copy(block_of(m.z, b), psum))
        mla_latents(c, m, j)
        o_tok = c.h[:, :, :].rearrange("p k t -> p (k t)")[:, 0:QT * H * DV].rearrange("p (q n) -> p q n", q=QT)
        mla_prompt_attention(c, m, j, o_tok)
        mla_sample_attention(c, m, j)
        mla_gated_values(c, m, o_tok)
        output_projection(c, c.dram["w_mla_out"][j], NG, m.gate)



CHUNKS = SEQ // P
KINDS = ("f", "q", "i", "g")


def heads_in_pairs(engine, head):
    head(0, 0, 1)
    with engine.Fori(0, (H - 2) // 2) as i:
        head(2 * i + 1, 1, 2 * i + 2)
        head(2 * i + 2, 0, 2 * i + 3)
    head(H - 1, 1, None)


def hgrn_lower_bound(c, layer, lb, olb):
    nc, dram = c.nc, c.dram
    with Stage(c) as st:
        raw = st.sb("bounds", [P, 4, KD])
        top = st.sb("top", [P, KD])
        tot = st.sb("tot", [P, KD])
        inv = st.sb("inv", [P, KD])
        loads = st.sem("loads")
        steps = st.sem("steps")
        exped = st.sem("exped")
        block = st.block()

        @block.sync
        def _(sp):
            sp.dma_start(raw[:, :, :], dram["hgrn_bounds"]).then_inc(loads, 16)

        @block.vector
        def _(dve):
            n = 0

            def step(ins):
                nonlocal n
                n += 1
                ins.then_inc(steps, 1)
                dve.wait_ge(steps, n)

            dve.wait_ge(loads, 16)
            step(nc.vector.tensor_reduce(top[:, :], raw[:, :, :].rearrange("p l k -> p k l"), AX.X, ALU.max))
            step(nc.vector.tensor_tensor(raw[:, :, :], raw[:, :, :],
                                         top[:, :].unsqueeze(1).broadcast_to([P, 4, KD]), ALU.subtract))
            dve.wait_ge(exped, 1)
            step(nc.vector.tensor_reduce(tot[:, :], raw[:, :, :].rearrange("p l k -> p k l"), AX.X, ALU.add))
            step(nc.vector.reciprocal(inv[:, :], tot[:, :]))
            step(nc.vector.tensor_reduce(tot[:, :], raw[:, 1:layer + 1, :].rearrange("p l k -> p k l"),
                                         AX.X, ALU.add))
            step(nc.vector.tensor_tensor(lb[:, :], tot[:, :], inv[:, :], ALU.mult))
            step(nc.vector.tensor_scalar(olb[:, :], lb[:, :], -1.0, 1.0, op0=ALU.mult, op1=ALU.add))

        @block.scalar
        def _(act):
            act.wait_ge(steps, 2)
            nc.scalar.activation(raw[:, :, :], raw[:, :, :], ACT.Exp).then_inc(exped, 1)


def hgrn_heads(c, out, lb, olb):
    nc, dram = c.nc, c.dram
    NU = 12
    QSCALE = P ** -0.5
    with Stage(c) as st:
        ws = st.sb("w_slots", [P, 4, KD, P])
        raw = st.sb("raw", [P, 3, T])
        sg = st.sb("decay", [P, T])
        k = st.sb("k", [P, T])
        q = st.sb("q", [P, T])
        gs = st.sb("gate", [P, T])
        gl = st.sb("log_decay", [P, T])
        b = st.sb("decay_sums", [P, SEQ])
        o = st.sb("o", [P, T])
        dd = st.sb("differences", [P, 2, T])
        z = st.sb("factors", [P, 2, T])
        v = st.sb("v", [P, 2, QT + 1, P])
        att = st.sb("att", [P, CHUNKS, P])
        states = st.sb("states", [P, CHUNKS, P])
        last = st.sb("chunk_decay", [P, CHUNKS])
        masks = st.sb("masks", [P, LEVELS + 1, P], mybir.dt.uint8)
        sel = st.sb("sel", [NS, NS, P])
        sin = st.sb("sample_in", [P, NS, P])
        ns = st.sb("sample_out", [P, NS, P])
        gn = st.sb("g_norm", [P, 1])
        kbt = dd[:, 1, 0:SEQ].rearrange("p (a n) -> p a n", a=CHUNKS)
        rs = z[:, 0, :]

        loads = st.sem("loads")
        w_landed = [st.sem(f"w_landed_{x}") for x in KINDS]
        sin_landed = st.sem("sin_landed")
        masks_done = st.sem("masks_done")
        unit_summed = st.sem("unit_summed")
        unit_drained = st.sem("unit_drained")
        acts = st.sem("acts")
        a_done = st.sem("a_done")
        k_done = st.sem("k_done")
        ln_done = st.sem("ln_done")
        scanned = st.sem("scanned")
        d_done = st.sem("d_done")
        exped = st.sem("exped")
        z_done = st.sem("z_done")
        zp_done = st.sem("zp_done")
        att_summed = st.sem("att_summed")
        att_copied = st.sem("att_copied")
        kb_turned = st.sem("kb_turned")
        kbt_done = st.sem("kbt_done")
        ds_summed = st.sem("ds_summed")
        state_done = st.sem("state_done")
        o_summed = st.sem("o_summed")
        o_done = st.sem("o_done")
        vb_summed = st.sem("vb_summed")
        sin_scaled = st.sem("sin_scaled")
        outer = st.sem("outer")
        ns_done = st.sem("ns_done")
        os_summed = st.sem("os_summed")
        os_done = st.sem("os_done")
        sqo_done = st.sem("sqo_done")
        ss_summed = st.sem("ss_summed")
        rs_logged = st.sem("rs_logged")
        rs_done = st.sem("rs_done")
        normed = st.sem("normed")
        og_done = st.sem("og_done")
        state_out = st.sem("state_out")
        ns_out = st.sem("ns_out")
        block = st.block()
        PAIR = [c.ps[:, 0:2, :].rearrange("p a n -> p (a n)").rearrange("p (a n) -> p a n", a=CHUNKS),
                c.ps[:, 2:4, :].rearrange("p a n -> p (a n)").rearrange("p (a n) -> p a n", a=CHUNKS)]

        def halves(buf, half):
            return buf.rearrange("p (n e h) -> p n e h", e=2, h=half)

        def chunks(buf):
            return buf.rearrange("p (a n) -> p a n", a=CHUNKS)

        @block.sync
        def _(sp):
            sp.dma_start(att[:, :, :], dram["hgrn_masks"]).then_inc(loads, 16)
            sp.dma_start(sel[:, :, :], dram["sel"]).then_inc(loads, 16)
            sp.dma_start(gn[:, :], dram["hgrn_g_norm"]).then_inc(loads, 16)

            def weights(h, first=False):
                for n in range(4):
                    if not first:
                        sp.wait_ge(unit_summed, NU * h + (3 * n + 3 - NU))
                    sp.dma_start(ws[:, n, :, :], dram["w_hgrn"][n][bass.ds(h, 1)].rearrange("a p k m -> p (a k) m")) \
                      .then_inc(w_landed[n], 16)

            def head(h, following):
                if following is not None:
                    weights(following)
                sin_before, states_now = 16 * h, CHUNKS * h + CHUNKS
                if not isinstance(h, int):
                    sin_before, states_now = sp.snap(sin_before), sp.snap(states_now)
                wait(sp, sin_landed, sin_before)
                wait(sp, ns_done, h)
                sp.dma_start(sin[:, :, :], dram["state_hgrn"][bass.ds(h, 1)].rearrange("a k n v -> k (a n) v")) \
                  .then_inc(sin_landed, 16)
                sp.wait_ge(ns_done, h + 1)
                sp.dma_start(dram["o_hgrn_s"][bass.ds(h, 1)].rearrange("a k n v -> k (a n) v"), ns[:, :, :]) \
                  .then_inc(ns_out, 16)
                sp.wait_ge(state_done, states_now)
                sp.dma_start(dram["o_hgrn_p"][bass.ds(h, 1)].rearrange("a k v -> k (a v)"),
                             states[:, CHUNKS - 1, :]).then_inc(state_out, 16)

            weights(0, first=True)
            head(0, 1)
            with sp.Fori(1, H - 1) as h:
                head(h, h + 1)
            head(H - 1, None)
            sp.wait_ge(ns_out, 16 * H)
            sp.wait_ge(state_out, 16 * H)

        @block.tensor
        def _(pe):
            def unit(h, n):
                kind, t = divmod(n, 3)
                bank = c.ps[:, 4 + n % 2, :]
                wait(pe, unit_drained, NU * h + (n - 1))
                if t == 0:
                    pe.wait_ge(w_landed[kind], 16 * h + 16)
                if KINDS[kind] != "i":
                    for kk in range(KD):
                        mm = nc.tensor.matmul(bank[:, 0:TT], ws[:, kind, kk, :], c.h[:, kk, t * TT:(t + 1) * TT],
                                              start=(kk == 0), stop=(kk == KD - 1))
                else:
                    for e in range(3):
                        tt = 3 * t + e
                        rows = P if tt < QT else NS
                        for kk in range(KD):
                            mm = nc.tensor.matmul(bank[0:rows, e * P:(e + 1) * P],
                                                  c.h[:, kk, tt * P:tt * P + rows], ws[:, kind, kk, :],
                                                  start=(kk == 0), stop=(kk == KD - 1))
                mm.then_inc(unit_summed, 1)

            def head(h, u, following):
                units = iter(range(NU) if following is not None else [])

                def fill(count=1):
                    for _ in range(count):
                        n = next(units, None)
                        if n is not None:
                            unit(following, n)

                def pair(n):
                    return PAIR[(n + u) % 2]

                fill(2)
                wait(pe, state_done, CHUNKS * h)
                pe.wait_ge(acts, 4 * h + 3)
                pe.wait_ge(k_done, h + 1)
                for a in range(CHUNKS):
                    cols = slice(a * P, (a + 1) * P)
                    mm = nc.tensor.matmul(pair(0)[:, a, :], k[:, cols], q[:, cols], start=True, stop=True)
                mm.then_inc(att_summed, 1)
                wait(pe, rs_logged, NT * h)
                for n in range(NS):
                    mm = nc.tensor.matmul(c.ps[:, 6 + n // 4, (n % 4) * P:(n % 4 + 1) * P], sel[:, n, :],
                                          v[0:NS, u, QT, :], start=True, stop=True)
                mm.then_inc(vb_summed, 1)
                for l in range(LEVELS):
                    n = l + 1
                    if n == 1:
                        wait(pe, o_done, h)
                    else:
                        pe.wait_ge(att_copied, 8 * h + (n - 1))
                    pe.wait_ge(z_done, 8 * h + (l + 1))
                    pe.wait_ge(zp_done, 8 * h + (l + 1))
                    for a in range(CHUNKS):
                        zc = z[:, l % 2, a * P:(a + 1) * P]
                        mm = nc.tensor.matmul(pair(n)[:, a, :], zc, zc, start=True, stop=True)
                    mm.then_inc(att_summed, 1)
                    if l:
                        fill()
                    if l == 4:
                        pe.wait_ge(ns_done, h + 1)
                        pe.wait_ge(outer, 2 * h + 2)
                        for n in range(NS):
                            mm = nc.tensor.matmul(c.ps[:, 6, n:n + 1], ns[:, n, :], q[:, SEQ + n:SEQ + n + 1],
                                                  start=True, stop=True)
                        mm.then_inc(os_summed, 1)
                pe.wait_ge(zp_done, 8 * h + 8)
                pe.wait_ge(att_copied, 8 * h + 7)
                for a in range(CHUNKS):
                    mm = nc.tensor.transpose(pair(8)[:, a, :], z[:, 1, a * P:(a + 1) * P], c.ident[:, :])
                mm.then_inc(kb_turned, 1)
                fill()
                pe.wait_ge(kbt_done, h + 1)
                pe.wait_ge(att_copied, 8 * h + 8)
                for a in range(CHUNKS):
                    mm = nc.tensor.matmul(pair(9)[:, a, :], kbt[:, a, :], v[:, u, a, :], start=True, stop=True)
                mm.then_inc(ds_summed, 1)
                fill(2)
                pe.wait_ge(z_done, 8 * h + 8)
                pe.wait_ge(state_done, CHUNKS * h + (CHUNKS - 1))
                for a in range(CHUNKS):
                    mm = nc.tensor.matmul(pair(10)[:, a, :], v[:, u, a, :], att[:, a, :], start=True, stop=(a == 0))
                    if a:
                        mm = nc.tensor.matmul(pair(10)[:, a, :], states[:, a - 1, :], dd[:, 0, a * P:(a + 1) * P],
                                              start=False, stop=True)
                mm.then_inc(o_summed, 1)
                fill()
                pe.wait_ge(sqo_done, h + 1)
                pe.wait_ge(os_done, h + 1)
                for t, cols in tiles():
                    if t == 2:
                        pe.wait_ge(rs_logged, NT * h + 1)
                    nc.tensor.matmul(c.ps[:, 6 + t % 2, 0:TT], c.ones[:, :], gl[:, cols],
                                     start=True, stop=True).then_inc(ss_summed, 1)

            pe.wait_ge(loads, 48)
            for n in range(NU):
                unit(0, n)
            heads_in_pairs(pe, head)

        @block.scalar
        def _(act):
            def drain_unit(h, u, n):
                kind, t = divmod(n, 3)
                bank = c.ps[:, 4 + n % 2, :]
                act.wait_ge(unit_summed, NU * h + (n + 1))
                if KINDS[kind] != "i":
                    place = {"f": 0, "q": 1, "g": 2}[KINDS[kind]]
                    nc.scalar.activation(raw[:, place, t * TT:(t + 1) * TT], bank[:, 0:TT], ACT.Copy) \
                      .then_inc(unit_drained, 1)
                    return
                if t == 2:
                    nc.scalar.activation(v[0:NS, u, QT, :], bank[0:NS, 2 * P:3 * P], ACT.Copy)
                full = 3 if t < 2 else 2
                nc.scalar.activation(v[:, u, 3 * t:3 * t + full, :],
                                     bank[:, 0:full * P].rearrange("p (a n) -> p a n", a=full), ACT.Copy) \
                  .then_inc(unit_drained, 1)

            def head(h, u, following):
                units = iter(range(NU) if following is not None else [])

                def fill(count=1):
                    for _ in range(count):
                        n = next(units, None)
                        if n is not None:
                            drain_unit(following, 1 - u, n)

                act.wait_ge(unit_drained, NU * h + NU)
                wait(act, og_done, h)
                nc.scalar.activation(sg[:, :], raw[:, 0, :], ACT.Sigmoid).then_inc(acts, 1)
                nc.scalar.activation(k[:, :], raw[:, 0, :], ACT.Sigmoid, scale=-1.0).then_inc(acts, 1)
                nc.scalar.activation(q[:, :], raw[:, 1, :], ACT.Silu).then_inc(acts, 1)
                nc.scalar.activation(gs[:, :], raw[:, 2, :], ACT.Silu).then_inc(acts, 1)
                act.wait_ge(acts, 4 * h + 4)
                act.wait_ge(a_done, h + 1)
                nc.scalar.activation(gl[:, 0:SEQ], sg[:, 0:SEQ], ACT.Ln).then_inc(ln_done, 1)
                fill(2)
                for l in range(LEVELS):
                    half = P >> (l + 1)
                    act.wait_ge(d_done, 8 * h + (l + 1))
                    both = halves(dd[:, l % 2, 0:SEQ], half)
                    nc.scalar.activation(both[:, :, 1, :], both[:, :, 1, :], ACT.Exp).then_inc(exped, 1)
                    nc.scalar.activation(both[:, :, 0, :], both[:, :, 0, :], ACT.Exp, scale=-1.0).then_inc(exped, 1)
                    if l:
                        fill()
                act.wait_ge(d_done, 8 * h + 8)
                nc.scalar.activation(dd[:, 1, 0:SEQ], dd[:, 1, 0:SEQ], ACT.Exp, scale=-1.0).then_inc(exped, 1)
                act.wait_ge(z_done, 8 * h + 7)
                act.wait_ge(zp_done, 8 * h + 7)
                nc.scalar.activation(dd[:, 0, 0:SEQ], b[:, :], ACT.Exp).then_inc(exped, 1)
                nc.scalar.activation(last[:, :], chunks(b[:, :])[:, :, P - 1], ACT.Exp).then_inc(exped, 1)
                act.wait_ge(os_summed, h + 1)
                nc.scalar.activation(o[:, SEQ:T], c.ps[:, 6, 0:NS], ACT.Copy, scale=QSCALE).then_inc(os_done, 1)
                act.wait_ge(kb_turned, h + 1)
                nc.scalar.activation(kbt, PAIR[u % 2], ACT.Copy).then_inc(kbt_done, 1)
                fill(3)
                act.wait_ge(o_summed, h + 1)
                nc.scalar.activation(chunks(o[:, 0:SEQ]), PAIR[u % 2], ACT.Copy, scale=QSCALE).then_inc(o_done, 1)
                act.wait_ge(o_done, h + 1)
                act.wait_ge(os_done, h + 1)
                nc.scalar.activation(gl[:, :], o[:, :], ACT.Square).then_inc(sqo_done, 1)
                fill()
                for t, cols in tiles():
                    act.wait_ge(ss_summed, NT * h + (t + 1))
                    nc.scalar.activation(rs[:, cols], c.ps[:, 6 + t % 2, 0:TT], ACT.Ln, scale=1.0 / P,
                                         bias=c.eps()).then_inc(rs_logged, 1)
                act.wait_ge(rs_logged, NT * h + NT)
                nc.scalar.activation(rs, rs, ACT.Exp, scale=-0.5).then_inc(rs_done, 1)

            for n in range(NU):
                drain_unit(0, 0, n)
            heads_in_pairs(act, head)

        @block.gpsimd
        def _(pool):
            def head(h, u, following):
                pool.wait_ge(sin_landed, 16 * h + 16)
                pool.wait_ge(a_done, h + 1)
                nc.gpsimd.tensor_tensor(sin[:, :, :], sin[:, :, :],
                                        sg[:, SEQ:T].unsqueeze(2).broadcast_to([P, NS, P]),
                                        ALU.mult).then_inc(sin_scaled, 1)
                for l in range(LEVELS):
                    if l == 2:
                        pool.wait_ge(outer, 2 * h + 2)
                        pool.wait_ge(sin_scaled, h + 1)
                        nc.gpsimd.tensor_tensor(ns[:, :, :], ns[:, :, :], sin[:, :, :], ALU.add) \
                          .then_inc(ns_done, 1)
                    half = P >> (l + 1)
                    pool.wait_ge(exped, 17 * h + (2 * l + 2))
                    if l >= 2:
                        pool.wait_ge(att_summed, 8 * h + l)
                    nc.gpsimd.tensor_tensor(halves(z[:, l % 2, 0:SEQ], half)[:, :, 0, :],
                                            halves(dd[:, l % 2, 0:SEQ], half)[:, :, 0, :],
                                            halves(k[:, 0:SEQ], half)[:, :, 0, :], ALU.mult).then_inc(zp_done, 1)
                pool.wait_ge(exped, 17 * h + 15)
                pool.wait_ge(att_summed, 8 * h + 7)
                nc.gpsimd.tensor_tensor(z[:, 1, 0:SEQ], dd[:, 1, 0:SEQ], k[:, 0:SEQ], ALU.mult) \
                  .then_inc(zp_done, 1)

            heads_in_pairs(pool, head)

        @block.vector
        def _(dve):
            def head(h, u, following):
                dve.wait_ge(acts, 4 * h + 1)
                nc.vector.tensor_scalar(sg[:, :], sg[:, :], olb[:, bass.ds(h, 1)], lb[:, bass.ds(h, 1)],
                                        op0=ALU.mult, op1=ALU.add).then_inc(a_done, 1)
                dve.wait_ge(acts, 4 * h + 2)
                nc.vector.tensor_scalar(k[:, :], k[:, :], olb[:, bass.ds(h, 1)], None, op0=ALU.mult) \
                  .then_inc(k_done, 1)
                dve.wait_ge(ln_done, h + 1)
                for a in range(CHUNKS):
                    cols = slice(a * P, (a + 1) * P)
                    nc.vector.tensor_tensor_scan(b[:, cols], c.ones[:, :], gl[:, cols], 0.0,
                                                 op0=ALU.mult, op1=ALU.add).then_inc(scanned, 1)
                dve.wait_ge(scanned, CHUNKS * h + CHUNKS)

                def difference(l):
                    half = P >> (l + 1)
                    if l >= 2:
                        dve.wait_ge(z_done, 8 * h + (l - 1))
                        dve.wait_ge(zp_done, 8 * h + (l - 1))
                    ref = halves(b[:, :], half)[:, :, 0:1, half - 1:half]
                    nc.vector.tensor_tensor(halves(dd[:, l % 2, 0:SEQ], half), halves(b[:, :], half),
                                            ref.broadcast_to([P, SEQ // (2 * half), 2, half]), ALU.subtract) \
                      .then_inc(d_done, 1)

                def upper(l):
                    half = P >> (l + 1)
                    dve.wait_ge(exped, 17 * h + (2 * l + 1))
                    dve.wait_ge(acts, 4 * h + 3)
                    if l >= 2:
                        dve.wait_ge(att_summed, 8 * h + l)
                    nc.vector.tensor_tensor(halves(z[:, l % 2, 0:SEQ], half)[:, :, 1, :],
                                            halves(dd[:, l % 2, 0:SEQ], half)[:, :, 1, :],
                                            halves(q[:, 0:SEQ], half)[:, :, 1, :], ALU.mult).then_inc(z_done, 1)

                def pick(n):
                    dve.wait_ge(masks_done, 2)
                    if n:
                        dve.wait_ge(att_copied, 8 * h + n)
                    dve.wait_ge(att_summed, 8 * h + (n + 1))
                    nc.vector.copy_predicated(att[:, :, :], masks[:, n:n + 1, :].broadcast_to([P, CHUNKS, P]),
                                              PAIR[(n + u) % 2]).then_inc(att_copied, 1)

                dve.wait_ge(scanned, 8 * h + 1)
                difference(0)
                pick(0)
                dve.wait_ge(k_done, h + 1)
                dve.wait_ge(vb_summed, h + 1)
                wait(dve, ns_out, 16 * h)
                for e in range(2):
                    nc.vector.tensor_tensor(ns[:, 4 * e:4 * e + 4, :],
                                            c.ps[:, 6 + e, :].rearrange("p (a n) -> p a n", a=4),
                                            k[:, SEQ + 4 * e:SEQ + 4 * e + 4].unsqueeze(2)
                                            .broadcast_to([P, 4, P]), ALU.mult).then_inc(outer, 1)
                for l in range(LEVELS):
                    if l + 1 < LEVELS:
                        difference(l + 1)
                    dve.wait_ge(scanned, 8 * h + (l + 1))
                    upper(l)
                    if l:
                        pick(l)
                dve.wait_ge(scanned, 8 * h + 8)
                dve.wait_ge(z_done, 8 * h + 6)
                dve.wait_ge(zp_done, 8 * h + 6)
                nc.vector.tensor_tensor(chunks(dd[:, 1, 0:SEQ]), chunks(b[:, :]),
                                        chunks(b[:, :])[:, :, P - 1:P].broadcast_to([P, CHUNKS, P]),
                                        ALU.subtract).then_inc(d_done, 1)
                pick(LEVELS)
                dve.wait_ge(exped, 17 * h + 16)
                nc.vector.tensor_tensor(dd[:, 0, 0:SEQ], dd[:, 0, 0:SEQ], q[:, 0:SEQ], ALU.mult) \
                  .then_inc(z_done, 1)
                dve.wait_ge(ds_summed, h + 1)
                dve.wait_ge(exped, 17 * h + 17)
                wait(dve, state_out, 16 * h)
                pair = PAIR[(9 + u) % 2]
                nc.vector.tensor_copy(states[:, 0, :], pair[:, 0, :]).then_inc(state_done, 1)
                for a in range(1, CHUNKS):
                    dve.wait_ge(state_done, CHUNKS * h + a)
                    nc.vector.scalar_tensor_tensor(states[:, a, :], states[:, a - 1, :], last[:, a:a + 1],
                                                   pair[:, a, :], op0=ALU.mult, op1=ALU.add) \
                      .then_inc(state_done, 1)
                dve.wait_ge(rs_done, h + 1)
                nc.vector.scalar_tensor_tensor(o[:, :], o[:, :], gn[:, 0:1], rs, op0=ALU.mult, op1=ALU.mult) \
                  .then_inc(normed, 1)
                dve.wait_ge(normed, h + 1)
                dve.wait_ge(acts, 4 * h + 4)
                nc.vector.tensor_tensor(out[:, bass.ds(h, 1), :].rearrange("p a t -> p (a t)"), o[:, :], gs[:, :],
                                        ALU.mult).then_inc(og_done, 1)

            dve.wait_ge(loads, 48)
            nc.vector.tensor_copy(masks[:, :, :], att[:, :, :]).then_inc(masks_done, 1)
            dve.wait_ge(masks_done, 1)
            nc.vector.memset(att[:, :, :], 0.0).then_inc(masks_done, 1)
            heads_in_pairs(dve, head)


def hgrn_layer(c, layer):
    rms_norm(c, layer)
    with Stage(c) as st:
        out = st.sb("heads_out", [P, KD, T])
        lb = st.sb("lb", [P, KD])
        olb = st.sb("one_less_lb", [P, KD])
        hgrn_lower_bound(c, layer, lb, olb)
        hgrn_heads(c, out, lb, olb)
        output_projection(c, c.dram["w_hgrn_out"], KD, out)


CONV = 4


def rglru_decay_rate(c, m8, p8):
    nc, dram = c.nc, c.dram
    with Stage(c) as st:
        lam = st.sb("lam", [P, KD])
        neg = st.sb("neg", [P, KD])
        z = st.sb("z", [P, KD])
        s = st.sb("s", [P, KD])
        s2 = st.sb("s2", [P, KD])
        p = st.sb("p", [P, KD])
        loads = st.sem("loads")
        steps = st.sem("steps")
        exped = st.sem("exped")
        block = st.block()

        @block.sync
        def _(sp):
            sp.dma_start(lam[:, :], dram["rg_lam"]).then_inc(loads, 16)

        @block.scalar
        def _(act):
            act.wait_ge(steps, 2)
            nc.scalar.activation(z[:, :], z[:, :], ACT.Exp, scale=-1.0).then_inc(exped, 1)

        @block.vector
        def _(dve):
            n = 0

            def step(ins):
                nonlocal n
                n += 1
                ins.then_inc(steps, 1)
                dve.wait_ge(steps, n)

            dve.wait_ge(loads, 16)
            step(nc.vector.tensor_scalar(neg[:, :], lam[:, :], -1.0, None, op0=ALU.mult))
            step(nc.vector.tensor_tensor(z[:, :], neg[:, :], lam[:, :], ALU.max))
            dve.wait_ge(exped, 1)
            step(nc.vector.tensor_scalar(s[:, :], z[:, :], 2.0, None, op0=ALU.add))
            step(nc.vector.reciprocal(s[:, :], s[:, :]))
            step(nc.vector.tensor_tensor(s[:, :], s[:, :], z[:, :], ALU.mult))
            step(nc.vector.tensor_tensor(s2[:, :], s[:, :], s[:, :], ALU.mult))
            step(nc.vector.tensor_scalar(p[:, :], s2[:, :], 1.0 / 17, 1.0 / 15, op0=ALU.mult, op1=ALU.add))
            for d in (13, 11, 9, 7, 5, 3, 1):
                step(nc.vector.tensor_tensor(p[:, :], p[:, :], s2[:, :], ALU.mult))
                step(nc.vector.tensor_scalar(p[:, :], p[:, :], 1.0 / d, None, op0=ALU.add))
            step(nc.vector.tensor_tensor(p[:, :], p[:, :], s[:, :], ALU.mult))
            step(nc.vector.tensor_scalar(neg[:, :], neg[:, :], 0.0, None, op0=ALU.max))
            step(nc.vector.scalar_tensor_tensor(p[:, :], p[:, :], 2.0, neg[:, :], op0=ALU.mult, op1=ALU.add))
            step(nc.vector.tensor_scalar(m8[:, :], p[:, :], -8.0, None, op0=ALU.mult))
            step(nc.vector.tensor_scalar(p8[:, :], p[:, :], 8.0, None, op0=ALU.mult))


def rglru_heads(c, out, m8, p8):
    nc, dram = c.nc, c.dram
    NU = 6
    PRE = CONV - 1
    with Stage(c) as st:
        ws = st.sb("w_slots", [P, 2, KD, P])
        wg = st.sb("w_gates", [P, 2, 2, P])
        xb = st.sb("xb", [P, 2, PRE + T])
        graw = st.sb("gate_raw", [P, 2, T])
        gs = st.sb("gate", [P, T])
        y = st.sb("y", [P, T])
        r = st.sb("r", [P, T])
        iy = st.sb("i", [P, T])
        a = st.sb("a", [P, T])
        th = st.sb("tanh", [P, T])
        a2 = st.sb("a2", [P, T])
        hs = st.sb("hs", [P, T])
        convw = st.sb("conv_w", [P, KD, CONV + 3])
        sconv = st.sb("state_conv", [P, KD, PRE, NS])
        slru = st.sb("state_lru", [P, KD, NS])
        oconvp = st.sb("o_conv_p", [P, KD, PRE])
        oconvs = st.sb("o_conv_s", [P, KD, PRE, NS])
        olrup = st.sb("o_lru_p", [P, KD])
        olrus = st.sb("o_lru_s", [P, KD, NS])

        loads = st.sem("loads")
        w_landed = [st.sem("w_landed_x"), st.sem("w_landed_g")]
        wg_landed = [st.sem("wg_landed0"), st.sem("wg_landed1")]
        zeroed = st.sem("zeroed")
        unit_summed = st.sem("unit_summed")
        unit_drained = st.sem("unit_drained")
        y_parts = st.sem("y_parts")
        ri_summed = st.sem("ri_summed")
        gs_done = st.sem("gs_done")
        r_done = st.sem("r_done")
        i_done = st.sem("i_done")
        iy_done = st.sem("iy_done")
        a_done = st.sem("a_done")
        th_done = st.sem("th_done")
        a2_done = st.sem("a2_done")
        m_done = st.sem("m_done")
        root_done = st.sem("root_done")
        u_done = st.sem("u_done")
        h_done = st.sem("h_done")
        kept = st.sem("kept")
        og_done = st.sem("og_done")
        stored = st.sem("stored")
        block = st.block()
        R, I = c.ps[:, 2:2 + NT, 0:TT], c.ps[:, 5:5 + NT, 0:TT]

        @block.sync
        def _(sp):
            sp.dma_start(convw[:, :, :], dram["rg_small"]).then_inc(loads, 16)
            sp.dma_start(sconv[:, :, :, :], dram["state_conv"]).then_inc(loads, 16)
            sp.dma_start(slru[:, :, :], dram["state_lru"]).then_inc(loads, 16)

            def weights(h, u, first=False):
                for n in range(2):
                    if not first:
                        sp.wait_ge(unit_summed, NU * h + (3 * n + 3 - NU))
                    sp.dma_start(ws[:, n, :, :], dram["w_rg"][n][bass.ds(h, 1)].rearrange("a p k m -> p (a k) m")) \
                      .then_inc(w_landed[n], 16)
                wait(sp, ri_summed, 2 * h - 2)
                sp.dma_start(wg[:, u, :, :], dram["w_rg_gates"][bass.ds(h, 1)].rearrange("a p k m -> p (a k) m")) \
                  .then_inc(wg_landed[u], 16)

            weights(0, 0, first=True)
            weights(1, 1)
            with sp.Fori(1, H // 2) as i:
                for u in range(2):
                    weights(2 * i + u, u)
            sp.wait_ge(kept, 5 * H)
            sp.dma_start(dram["o_conv_p"], oconvp[:, :, :]).then_inc(stored, 16)
            sp.dma_start(dram["o_conv_s"], oconvs[:, :, :, :]).then_inc(stored, 16)
            sp.dma_start(dram["o_lru_p"], olrup[:, :]).then_inc(stored, 16)
            sp.dma_start(dram["o_lru_s"], olrus[:, :, :]).then_inc(stored, 16)
            sp.wait_ge(stored, 64)

        @block.tensor
        def _(pe):
            def unit(h, n):
                kind, t = divmod(n, 3)
                wait(pe, unit_drained, NU * h + (n - 1))
                if t == 0:
                    pe.wait_ge(w_landed[kind], 16 * h + 16)
                for kk in range(KD):
                    mm = nc.tensor.matmul(c.ps[:, n % 2, 0:TT], ws[:, kind, kk, :], c.h[:, kk, t * TT:(t + 1) * TT],
                                          start=(kk == 0), stop=(kk == KD - 1))
                mm.then_inc(unit_summed, 1)

            def head(h, u, following):
                if following is not None:
                    for n in range(3):
                        unit(following, n)
                pe.wait_ge(y_parts, 7 * h + 7)
                pe.wait_ge(wg_landed[u], 8 * h + (16 - 8 * u))
                for e, done in enumerate((r_done, i_done)):
                    wait(pe, done, h)
                    for t, cols in tiles():
                        mm = nc.tensor.matmul(c.ps[:, 2 + NT * e + t, 0:TT], wg[:, u, e, :], y[:, cols],
                                              start=True, stop=True)
                    mm.then_inc(ri_summed, 1)
                if following is not None:
                    for n in range(3, NU):
                        unit(following, n)

            for n in range(NU):
                unit(0, n)
            heads_in_pairs(pe, head)

        @block.scalar
        def _(act):
            def drain_unit(h, u, n):
                kind, t = divmod(n, 3)
                act.wait_ge(unit_summed, NU * h + (n + 1))
                if n == 0:
                    wait(act, kept, 5 * h - 5)
                    wait(act, y_parts, 7 * h - 7)
                lo = PRE if kind == 0 else 0
                dst = (xb if kind == 0 else graw)[:, u, lo + t * TT:lo + (t + 1) * TT]
                nc.scalar.activation(dst, c.ps[:, n % 2, 0:TT], ACT.Copy).then_inc(unit_drained, 1)

            def head(h, u, following):
                act.wait_ge(unit_drained, NU * h + NU)
                wait(act, og_done, h)
                nc.scalar.activation(gs[:, :], graw[:, u, :], ACT.Silu).then_inc(gs_done, 1)
                if following is not None:
                    for n in range(3):
                        drain_unit(following, 1 - u, n)
                act.wait_ge(loads, 48)
                act.wait_ge(ri_summed, 2 * h + 1)
                nc.scalar.activation(split_tiles(r[:, :]), R, ACT.Sigmoid,
                                     bias=convw[:, bass.ds(h, 1), CONV + 1:CONV + 2].rearrange("p a k -> p (a k)")) \
                  .then_inc(r_done, 1)
                act.wait_ge(ri_summed, 2 * h + 2)
                wait(act, u_done, h)
                nc.scalar.activation(split_tiles(iy[:, :]), I, ACT.Sigmoid,
                                     bias=convw[:, bass.ds(h, 1), CONV + 2:CONV + 3].rearrange("p a k -> p (a k)")) \
                  .then_inc(i_done, 1)
                act.wait_ge(r_done, h + 1)
                wait(act, h_done, 3 * h)
                nc.scalar.activation(a[:, :], r[:, :], ACT.Exp, scale=m8[:, bass.ds(h, 1)]).then_inc(a_done, 1)
                nc.scalar.activation(th[:, :], r[:, :], ACT.Tanh, scale=p8[:, bass.ds(h, 1)]).then_inc(th_done, 1)
                act.wait_ge(a_done, h + 1)
                nc.scalar.activation(a2[:, :], a[:, :], ACT.Square).then_inc(a2_done, 1)
                act.wait_ge(m_done, h + 1)
                nc.scalar.activation(a2[:, :], a2[:, :], ACT.Sqrt).then_inc(root_done, 1)
                if following is not None:
                    for n in range(3, NU):
                        drain_unit(following, 1 - u, n)

            act.wait_ge(zeroed, 1)
            for n in range(NU):
                drain_unit(0, 0, n)
            heads_in_pairs(act, head)

        @block.gpsimd
        def _(pool):
            def head(h, u, following):
                pool.wait_ge(i_done, h + 1)
                nc.gpsimd.tensor_tensor(iy[:, :], iy[:, :], y[:, :], ALU.mult).then_inc(iy_done, 1)
                pool.wait_ge(root_done, h + 1)
                pool.wait_ge(iy_done, h + 1)
                nc.gpsimd.tensor_tensor(a2[:, :], a2[:, :], iy[:, :], ALU.mult).then_inc(u_done, 1)
                pool.wait_ge(h_done, 3 * h + 3)
                pool.wait_ge(gs_done, h + 1)
                nc.gpsimd.tensor_tensor(out[:, bass.ds(h, 1), :].rearrange("p a t -> p (a t)"), hs[:, :], gs[:, :],
                                        ALU.mult).then_inc(og_done, 1)

            heads_in_pairs(pool, head)

        @block.vector
        def _(dve):
            def one(buf, h, k):
                return buf[:, bass.ds(h, 1), k:k + 1].rearrange("p a k -> p (a k)")

            def head(h, u, following):
                dve.wait_ge(unit_drained, NU * h + 3)
                wait(dve, iy_done, h)
                wait(dve, ri_summed, 2 * h)
                nc.vector.tensor_scalar(y[:, :], xb[:, u, PRE:PRE + T], one(convw, h, PRE), one(convw, h, CONV),
                                        op0=ALU.mult, op1=ALU.add).then_inc(y_parts, 1)
                for n in range(PRE):
                    dve.wait_ge(y_parts, 7 * h + (2 * n + 1))
                    nc.vector.scalar_tensor_tensor(y[:, 0:SEQ], xb[:, u, n:n + SEQ], one(convw, h, n), y[:, 0:SEQ],
                                                   op0=ALU.mult, op1=ALU.add).then_inc(y_parts, 1)
                    nc.vector.scalar_tensor_tensor(
                        y[:, SEQ:T], sconv[:, bass.ds(h, 1), n, :].rearrange("p a s -> p (a s)"), one(convw, h, n),
                        y[:, SEQ:T], op0=ALU.mult, op1=ALU.add).then_inc(y_parts, 1)
                nc.vector.tensor_copy(oconvp[:, bass.ds(h, 1), :].rearrange("p a k -> p (a k)"),
                                      xb[:, u, SEQ:SEQ + PRE]).then_inc(kept, 1)
                nc.vector.tensor_copy(oconvs[:, bass.ds(h, 1), 0:PRE - 1, :].rearrange("p a k s -> p (a k) s"),
                                      sconv[:, bass.ds(h, 1), 1:PRE, :].rearrange("p a k s -> p (a k) s")) \
                  .then_inc(kept, 1)
                nc.vector.tensor_copy(oconvs[:, bass.ds(h, 1), PRE - 1, :].rearrange("p a s -> p (a s)"),
                                      xb[:, u, PRE + SEQ:PRE + T]).then_inc(kept, 1)
                dve.wait_ge(a2_done, h + 1)
                dve.wait_ge(th_done, h + 1)
                nc.vector.scalar_tensor_tensor(a2[:, :], a2[:, :], 1.0, th[:, :], op0=ALU.add, op1=ALU.mult) \
                  .then_inc(m_done, 1)
                dve.wait_ge(u_done, h + 1)
                wait(dve, og_done, h)
                wait(dve, kept, 5 * h)
                nc.vector.tensor_tensor_scan(hs[:, 0:SEQ], a[:, 0:SEQ], a2[:, 0:SEQ], 0.0,
                                             op0=ALU.mult, op1=ALU.add).then_inc(h_done, 1)
                nc.vector.tensor_tensor(hs[:, SEQ:T], a[:, SEQ:T],
                                        slru[:, bass.ds(h, 1), :].rearrange("p a s -> p (a s)"),
                                        ALU.mult).then_inc(h_done, 1)
                dve.wait_ge(h_done, 3 * h + 2)
                nc.vector.tensor_tensor(hs[:, SEQ:T], hs[:, SEQ:T], a2[:, SEQ:T], ALU.add).then_inc(h_done, 1)
                dve.wait_ge(h_done, 3 * h + 3)
                nc.vector.tensor_copy(olrup[:, bass.ds(h, 1)], hs[:, SEQ - 1:SEQ]).then_inc(kept, 1)
                nc.vector.tensor_copy(olrus[:, bass.ds(h, 1), :].rearrange("p a s -> p (a s)"), hs[:, SEQ:T]) \
                  .then_inc(kept, 1)

            nc.vector.memset(xb[:, :, 0:PRE], 0.0).then_inc(zeroed, 1)
            dve.wait_ge(zeroed, 1)
            dve.wait_ge(loads, 48)
            heads_in_pairs(dve, head)


def rglru_layer(c, layer):
    rms_norm(c, layer)
    with Stage(c) as st:
        out = st.sb("heads_out", [P, KD, T])
        m8 = st.sb("m8", [P, KD])
        p8 = st.sb("p8", [P, KD])
        rglru_decay_rate(c, m8, p8)
        rglru_heads(c, out, m8, p8)
        output_projection(c, c.dram["w_rg_out"], KD, out)


def store_residual(c):
    nc, dram = c.nc, c.dram
    with Stage(c) as st:
        stored = st.sem("stored")
        block = st.block()

        @block.sync
        def _(sp):
            sp.dma_start(dram["o_x"], c.x[:, :, :]).then_inc(stored, 16)
            sp.wait_ge(stored, 16)


LAYERS = 4


def program(nc, dram):
    with ExitStack() as ctx:
        Stage.used = []
        c = Chip(nc, ctx, dram)
        load_inputs(c)
        if LAYERS >= 1:
            mla_layer(c, 0, 0)
        if LAYERS >= 2:
            hgrn_layer(c, 1)
        if LAYERS >= 3:
            rglru_layer(c, 2)
        if LAYERS >= 4:
            mla_layer(c, 3, 1)
        store_residual(c)



def feature_tiles(a):
    return np.moveaxis(a.reshape(*a.shape[:-1], a.shape[-1] // P, P), -1, -2)


def weight_blocks(w, width=P):
    k, n = w.shape
    return w.reshape(k // P, P, n // width, width).transpose(2, 1, 0, 3)


def stack(f, w):
    return np.stack([f(x) for x in w])


def shape_constants(past):
    pos = np.concatenate([np.arange(SEQ), np.full(NS, past)]).astype(np.float32)
    inv = (1.0 / (np.float32(10000.0) ** (np.arange(0, ROPE, 2, dtype=np.float32) / ROPE))).astype(np.float32)
    ang = (pos[None, :] * inv[:, None]).astype(np.float32)
    trig = np.zeros((P, T), np.float32)
    trig[NOPE:QK] = np.concatenate([np.cos(ang), np.cos(ang)])
    trig[QK:P] = np.concatenate([-np.sin(ang), np.sin(ang)])
    r = np.arange(P)
    s, t = r[:, None], r[None, :]
    masks = [s == t] + [(s // (2 * hf) == t // (2 * hf)) & (s // hf + 1 == t // hf)
                        for hf in (P >> (l + 1) for l in range(LEVELS))]
    return {
        "hgrn_masks": np.stack(masks, axis=1).astype(np.float32),
        "sel": np.repeat(np.eye(NS, dtype=np.float32)[:, :, None], P, axis=2),
        "ident": np.eye(P, dtype=np.float32), "ones": np.ones((P, P), np.float32),
        "const": np.tile(np.array(TINY, np.float32), (P, 1)), "trig": trig,
        "causal": np.where(r[None, :] <= r[:, None], 0.0, -1e30).astype(np.float32),
    }


def layouts(i):
    a = {k: np.asarray(v) for k, v in i.items()}
    x = np.concatenate([a["x_prompt"].reshape(SEQ, D), a["x_sample"].reshape(NS, D)])
    pages = np.concatenate([a["cache_ckv"], a["cache_kpe"]], axis=-1)
    nl, pool = pages.shape[:2]
    win = a["mla_w_in"]
    z = np.concatenate([win[:, :, :QL + KVL], win[:, :, QL + KVL + ROPE:]], axis=2)
    kpe = win[:, :, QL + KVL:QL + KVL + ROPE]
    half = ROPE // 2
    kpe = np.concatenate([kpe, kpe[:, :, half:], kpe[:, :, :half]], axis=2)
    uq = a["mla_w_uq"].reshape(nl, QL, H, QK)
    uq = np.concatenate([uq, uq[..., NOPE + half:], uq[..., NOPE:NOPE + half]], axis=3).reshape(nl, QL, H * P)
    ukv = a["mla_w_ukv"].reshape(nl, KVL, H, NOPE + DV)
    uk, uv = ukv[..., :NOPE].reshape(nl, KVL, H * NOPE), ukv[..., NOPE:].reshape(nl, KVL, H * DV)
    out = {
        "x": feature_tiles(x).transpose(1, 2, 0),
        "norm_g": feature_tiles(a["norm_g"]).transpose(1, 0, 2),
        "w_mla_in": stack(weight_blocks, z),
        "w_kpe": stack(lambda w: weight_blocks(w, 2 * ROPE)[0], kpe),
        "g_q_lora": feature_tiles(a["mla_g_q_lora"]),
        "g_kv": feature_tiles(a["mla_g_kv"]),
        "w_uq": stack(weight_blocks, uq),
        "w_uk": stack(lambda w: weight_blocks(w, NOPE), uk),
        "w_uk_all": stack(lambda w: weight_blocks(w, H * NOPE)[0], uk),
        "w_uk_t": uk.reshape(nl, KVL, H, NOPE).transpose(0, 3, 2, 1),
        "w_uv": stack(lambda w: weight_blocks(w, H * DV)[0], uv),
        "g_qk": np.stack([a["mla_g_q"], a["mla_g_k"]], axis=-1),
        "w_mla_out": stack(weight_blocks, a["mla_w_out"]),
        "page_table": a["page_table"].reshape(1, NS * PAGES),
        "pages": pages,
        "pages_t": a["cache_ckv"].transpose(0, 1, 3, 2).reshape(nl, pool, NKV, P, PAGE).transpose(0, 1, 3, 2, 4),
        "pages_kpe_t": a["cache_kpe"].transpose(0, 1, 3, 2),
    }
    w4 = a["hgrn_w_in"][0].reshape(D, 4, H, P)
    q_, f_, i_, g_ = (w4[:, n].reshape(D, H * P) for n in range(4))
    out["w_hgrn"] = np.stack([weight_blocks(w) for w in (f_, q_, i_, g_)])
    out["w_hgrn_out"] = weight_blocks(a["hgrn_w_out"][0])
    out["hgrn_bounds"] = feature_tiles(a["hgrn_lower_bounds"]).transpose(1, 0, 2)
    out["hgrn_g_norm"] = a["hgrn_g_norm"][0].reshape(P, 1)
    out["state_hgrn"] = a["state_hgrn"][0].transpose(1, 2, 0, 3)
    rg = a["rglru_w_in"][0]
    out["w_rg"] = np.stack([weight_blocks(rg[:, :D]), weight_blocks(rg[:, D:])])
    out["w_rg_gates"] = np.stack([a["rglru_w_a"][0], a["rglru_w_x"][0]], axis=2)
    out["w_rg_out"] = weight_blocks(a["rglru_w_out"][0])
    small = np.concatenate([a["rglru_conv_w"][0], a["rglru_conv_b"], a["rglru_b_a"], a["rglru_b_x"]])
    out["rg_small"] = feature_tiles(small).transpose(1, 2, 0)
    out["rg_lam"] = feature_tiles(a["rglru_L"][0])
    out["state_conv"] = feature_tiles(a["state_conv"][0]).transpose(2, 3, 1, 0)
    out["state_lru"] = feature_tiles(a["state_lru"][0]).transpose(1, 2, 0)
    out.update(shape_constants(PAGES * PAGE))
    return {k: np.ascontiguousarray(v) for k, v in out.items()}


def kernel(**inputs):
    import concourse.bacc as bacc
    from concourse.bass_utils import run_bass_kernel_spmd

    nl = inputs["cache_ckv"].shape[0]
    outs = {"o_x": (P, KD, T), "o_ckv": (nl, P, NKV, T), "o_kpe": (nl, ROPE, T),
            "o_hgrn_p": (H, P, P), "o_hgrn_s": (H, P, NS, P),
            "o_conv_p": (P, KD, CONV - 1), "o_conv_s": (P, KD, CONV - 1, NS), "o_lru_p": (P, KD),
            "o_lru_s": (P, KD, NS)}
    nc = bacc.Bacc("TRN2", target_bir_lowering=False, num_devices=1)
    arrays, dram = layouts(inputs), {}
    for name, a in arrays.items():
        dram[name] = nc.dram_tensor("in_" + name, a.shape, mybir.dt.from_np(a.dtype), kind="ExternalInput").ap()
    for name, shape in outs.items():
        dram[name] = nc.dram_tensor(name, shape, F32, kind="ExternalOutput").ap()
    program(nc, dram)
    r = run_bass_kernel_spmd(nc, [{"in_" + k: v for k, v in arrays.items()}], core_ids=[0]).results[0]

    x = r["o_x"].transpose(2, 1, 0).reshape(T, D)
    ckv = r["o_ckv"].transpose(0, 3, 2, 1).reshape(nl, T, KVL)
    kpe = r["o_kpe"].transpose(0, 2, 1)
    return (x[:SEQ].reshape(1, SEQ, D), x[SEQ:].reshape(NS, 1, D),
            ckv[:, :SEQ].reshape(nl, 1, SEQ, KVL), kpe[:, :SEQ].reshape(nl, 1, SEQ, ROPE),
            ckv[:, SEQ:].reshape(nl, NS, 1, KVL), kpe[:, SEQ:].reshape(nl, NS, 1, ROPE),
            r["o_hgrn_p"].reshape(1, 1, H, P, P), r["o_hgrn_s"].transpose(2, 0, 1, 3)[None],
            r["o_conv_p"].transpose(2, 1, 0).reshape(1, 1, CONV - 1, D),
            r["o_conv_s"].transpose(3, 2, 1, 0).reshape(1, NS, CONV - 1, D),
            r["o_lru_p"].T.reshape(1, 1, D), r["o_lru_s"].transpose(2, 1, 0).reshape(1, NS, D))
```

```python
from contextlib import ExitStack

import concourse.bass as bass
import numpy as np
from concourse import mybir

F32 = mybir.dt.float32
F32R = mybir.dt.float32r
I32 = mybir.dt.int32
ACT = mybir.ActivationFunctionType
ALU = mybir.AluOpType
AX = mybir.AxisListType

P = 128
D = 1024
KD = D // P
SEQ = 1024
NS = 8
T = SEQ + NS
NT = 3
TT = T // NT
QT = SEQ // P
EPS = 1e-6

H = 8
NOPE, ROPE, DV = 64, 32, 64
QK = NOPE + ROPE
QL, KVL = 384, 256
NQL, NKV = QL // P, KVL // P
NG = H * DV // P
PAGES, PAGE = 16, 128
NAT = KVL + ROPE
SCALE = QK ** -0.5

LEVELS = 7
C_ONE, C_EPS, C_LNSCALE = 0, 1, 2
TINY = [1.0, EPS, float(np.log(SCALE))]


def wait(engine, sem, count):
    if not (isinstance(count, int) and count <= 0):
        engine.wait_ge(sem, count)


def tiles(n=NT):
    return [(t, slice(t * TT, (t + 1) * TT)) for t in range(n)]


LAYERS = 4


def following(layer):
    return layer + 1 if layer + 1 < LAYERS else None


class Chip:

    def __init__(self, nc, ctx, dram):
        self.nc, self.dram = nc, dram

        def sb(name, shape, dt=F32):
            return ctx.enter_context(nc.sbuf_tensor(name, shape, dt))

        self.x = sb("residual", [P, KD, T])
        self.h = sb("normed", [P, KD, T])
        self.ident = sb("ident", [P, P])
        self.ones = sb("ones", [P, P])
        self.const = sb("const", [P, len(TINY)])
        self.gains = sb("gains", [P, 4, KD])
        self.ps = ctx.enter_context(nc.psum_tensor("ps", [P, 8, 512], F32))

    def eps(self, rows=P):
        return self.const[0:rows, C_EPS:C_EPS + 1]


MOST_SEMS = 64


LN_EXP_SET = 6


def load_ln_exp(nc):
    nc.scalar.add_instruction(mybir.InstLoadActFuncSet(name=nc.get_next_instruction_name(),
                                                       engine=mybir.EngineType.Activation,
                                                       act_func_set_id=LN_EXP_SET))


class Stage:

    count = 0
    used = []

    def __init__(self, c):
        self.nc = c.nc
        self.ctx = ExitStack()
        self.sems = []
        self.tag = f"_{Stage.count}"
        Stage.count += 1

    def __enter__(self):
        self.ctx.__enter__()
        return self

    def __exit__(self, *a):
        done = self.ctx.__exit__(*a)
        Stage.used += self.sems
        if len(self.nc.free_semaphores) < MOST_SEMS:
            self.nc.clear_and_free_semaphores(Stage.used)
            self.nc.all_engine_barrier()
            Stage.used = []
        return done

    def sb(self, name, shape, dt=F32):
        return self.ctx.enter_context(self.nc.sbuf_tensor(name + self.tag, shape, dt))

    def sem(self, name):
        self.sems.append(self.nc.alloc_semaphore(name + self.tag))
        return self.sems[-1]

    def block(self):
        return self.ctx.enter_context(self.nc.Block())


class Norm:

    BY_POOL = 3

    def __init__(self, c, st, layer):
        self.c, self.layer = c, layer
        self.sq = st.sb("squares", [P, 2, T])
        self.acc = st.sb("square_sums", [P, T])
        self.rstd = st.sb("rstd", [P, T])
        self.squared = st.sem("squared")
        self.accumulated = st.sem("accumulated")
        self.gain_in = st.sem("gain_in")
        self.summed = st.sem("summed")
        self.logged = st.sem("logged")
        self.rstd_ready = st.sem("rstd_ready")

    def square(self, act, m, u):
        if not isinstance(m, int) or m >= 2:
            act.wait_ge(self.accumulated, m - 1)
        self.c.nc.scalar.activation(self.sq[:, u, :], self.c.x[:, bass.ds(m, 1), :].rearrange("p a t -> p (a t)"),
                                    ACT.Square).then_inc(self.squared, 1)

    def accumulate_first(self, pool):
        pool.wait_ge(self.squared, 2)
        self.c.nc.gpsimd.tensor_tensor(self.acc[:, :], self.sq[:, 0, :], self.sq[:, 1, :], ALU.add) \
            .then_inc(self.accumulated, 1)

    def accumulate(self, pool, m, u):
        pool.wait_ge(self.squared, m + 1)
        pool.wait_ge(self.accumulated, m - 1)
        self.c.nc.gpsimd.tensor_tensor(self.acc[:, :], self.acc[:, :], self.sq[:, u, :], ALU.add) \
            .then_inc(self.accumulated, 1)

    def sum(self, pe):
        nc, c = self.c.nc, self.c
        for buf, sem, count in ((self.acc, self.accumulated, KD - 2), (self.sq[:, (KD - 1) % 2, :], self.squared, KD)):
            pe.wait_ge(sem, count)
            for t, cols in tiles():
                mm = nc.tensor.matmul(c.ps[:, t, 0:TT], c.ones[:, :], buf[:, cols],
                                      start=(buf is self.acc), stop=(buf is not self.acc))
        mm.then_inc(self.summed, 1)

    def root(self, act):
        nc, c = self.c.nc, self.c
        for k in range(self.BY_POOL):
            nc.scalar.activation(c.h[:, k, :], c.x[:, k, :], ACT.Copy, scale=c.gains[:, self.layer, k:k + 1]) \
              .then_inc(self.gain_in, 1)
        act.wait_ge(self.summed, 1)
        nc.scalar.activation(split_tiles(self.rstd[:, :]), c.ps[:, 0:NT, 0:TT], ACT.Ln,
                             scale=1.0 / D, bias=c.eps()).then_inc(self.logged, 1)
        act.wait_ge(self.logged, 1)
        nc.scalar.activation(self.rstd[:, :], self.rstd[:, :], ACT.Exp, scale=-0.5).then_inc(self.rstd_ready, 1)

    def scale_first(self, pool):
        pool.wait_ge(self.rstd_ready, 1)
        pool.wait_ge(self.gain_in, self.BY_POOL)
        for k in range(self.BY_POOL):
            self.c.nc.gpsimd.tensor_tensor(self.c.h[:, k, :], self.c.h[:, k, :], self.rstd[:, :], ALU.mult)

    def scale_rest(self, dve):
        c = self.c
        dve.wait_ge(self.rstd_ready, 1)
        for k in range(self.BY_POOL, KD):
            c.nc.vector.scalar_tensor_tensor(c.h[:, k, :], c.x[:, k, :], c.gains[:, self.layer, k:k + 1],
                                             self.rstd[:, :], op0=ALU.mult, op1=ALU.mult)


def load_inputs(c):
    nc, dram = c.nc, c.dram
    with Stage(c) as st:
        norm = Norm(c, st, 0)
        x_landed = [st.sem(f"x_landed{n}") for n in range(KD // 2)]
        landed = st.sem("constants_landed")
        block = st.block()

        @block.sync
        def _(sp):
            for n, sem in enumerate(x_landed):
                sp.dma_start(c.x[:, 2 * n:2 * n + 2, :], dram["x"][:, 2 * n:2 * n + 2, :]).then_inc(sem, 16)
                if n == 0:
                    sp.dma_start(c.ident[:, :], dram["ident"]).then_inc(landed, 16)
                    sp.dma_start(c.ones[:, :], dram["ones"]).then_inc(landed, 16)
                    sp.dma_start(c.const[:, :], dram["const"]).then_inc(landed, 16)
                    sp.dma_start(c.gains[:, :, :], dram["norm_g"]).then_inc(landed, 16)

        @block.scalar
        def _(act):
            load_ln_exp(nc)
            for m in range(KD):
                act.wait_ge(x_landed[m // 2], 16)
                norm.square(act, m, m % 2)
            act.wait_ge(landed, 64)
            norm.root(act)

        @block.gpsimd
        def _(pool):
            norm.accumulate_first(pool)
            for m in range(2, KD - 1):
                norm.accumulate(pool, m, m % 2)
            norm.scale_first(pool)

        @block.tensor
        def _(pe):
            pe.wait_ge(landed, 64)
            norm.sum(pe)

        @block.vector
        def _(dve):
            dve.wait_ge(landed, 64)
            for sem in x_landed:
                dve.wait_ge(sem, 16)
            norm.scale_rest(dve)


def streamed_projection(c, w, blocks, kt, src, drain, norm_layer=None):
    nc = c.nc
    with Stage(c) as st:
        ws = st.sb("w_slots", [P, 2, kt, P])
        w_hi = st.sb("w_hi", [P, 2, kt, P], F32R)
        w_lo = st.sb("w_lo", [P, 2, kt, P], F32R)
        src_hi = st.sb("src_hi", [P, kt, T], F32R)
        src_lo = st.sb("src_lo", [P, kt, T], F32R)
        w_landed = [st.sem("w_landed0"), st.sem("w_landed1")]
        w_hi_done = st.sem("w_hi_done")
        w_lo_done = st.sem("w_lo_done")
        src_hi_done = st.sem("src_hi_done")
        src_lo_done = st.sem("src_lo_done")
        summed = st.sem("block_summed")
        drained = st.sem("block_drained")
        norm = None if norm_layer is None else Norm(c, st, norm_layer)
        block = st.block()
        pairs = blocks // 2

        @block.sync
        def _(sp):
            for u in range(2):
                sp.dma_start(ws[:, u, :, :], w[u]).then_inc(w_landed[u], 16)
            with sp.Fori(1, pairs) as i:
                for u in range(2):
                    sp.wait_ge(w_lo_done, 2 * i + (u - 1))
                    sp.dma_start(ws[:, u, :, :], w[bass.ds(2 * i + u, 1)].rearrange("a p k m -> p (a k) m")) \
                      .then_inc(w_landed[u], 16)
            if blocks % 2:
                sp.wait_ge(w_lo_done, blocks - 2)
                sp.dma_start(ws[:, 0, :, :], w[blocks - 1]).then_inc(w_landed[0], 16)

        @block.scalar
        def _(act):
            def weight_hi(m, u, landed):
                act.wait_ge(w_landed[u], landed)
                wait(act, summed, m - 1)
                nc.scalar.activation(w_hi[:, u, :, :], ws[:, u, :, :], ACT.Copy).then_inc(w_hi_done, 1)

            def square(m, u):
                if norm:
                    act.wait_ge(drained, m + 1)
                    norm.square(act, m, u)

            load_ln_exp(nc)
            for k in range(kt):
                nc.scalar.activation(src_hi[:, k, :], src[:, k, :], ACT.Copy).then_inc(src_hi_done, 1)
                if k == 1:
                    weight_hi(0, 0, 16)
            weight_hi(1, 1, 16)
            for u in range(2):
                weight_hi(2 + u, u, 32)
                square(u, u)
            with act.Fori(2, pairs) as i:
                for u in range(2):
                    weight_hi(2 * i + u, u, 16 * i + 16)
                    square(2 * i + (u - 2), u)
            if blocks % 2:
                weight_hi(blocks - 1, 0, 16 * (pairs + 1))
            if norm:
                for u in range(2):
                    square(blocks - 2 + u, u)
                norm.root(act)

        @block.gpsimd
        def _(pool):
            def weight_lo(m, u):
                pool.wait_ge(w_hi_done, m + 1)
                nc.gpsimd.tensor_tensor(w_lo[:, u, :, :], ws[:, u, :, :], w_hi[:, u, :, :].bitcast(F32),
                                        ALU.subtract).then_inc(w_lo_done, 1)

            for m in range(4):
                weight_lo(m, m % 2)
            if norm:
                norm.accumulate_first(pool)
            with pool.Fori(2, pairs) as i:
                for u in range(2):
                    weight_lo(2 * i + u, u)
                    if norm:
                        norm.accumulate(pool, 2 * i + (u - 2), u)
            if blocks % 2:
                weight_lo(blocks - 1, 0)
            if norm:
                norm.accumulate(pool, blocks - 2, 0)
                norm.scale_first(pool)

        @block.tensor
        def _(pe):
            def one(m, u, first=False):
                pe.wait_ge(w_lo_done, m + 1)
                if not first:
                    pe.wait_ge(drained, m - 1)
                for k in range(kt):
                    if first and u == 0:
                        pe.wait_ge(src_lo_done, k + 1)
                    for n, (a, b) in enumerate(((w_hi, src_hi), (w_hi, src_lo), (w_lo, src_hi))):
                        for t, cols in tiles():
                            mm = nc.tensor.matmul(c.ps[:, NT * u + t, 0:TT], a[:, u, k, :], b[:, k, cols],
                                                  start=(k == 0 and n == 0), stop=(k == kt - 1 and n == 2))
                mm.then_inc(summed, 1)

            for u in range(2):
                one(u, u, first=True)
            with pe.Fori(1, pairs) as i:
                for u in range(2):
                    one(2 * i + u, u)
            if blocks % 2:
                one(blocks - 1, 0)
            if norm:
                pe.wait_ge(drained, blocks - 1)
                norm.sum(pe)

        @block.vector
        def _(dve):
            def one(m, u):
                dve.wait_ge(summed, m + 1)
                drain(m, c.ps[:, NT * u:NT * u + NT, 0:TT]).then_inc(drained, 1)

            for k in range(kt):
                dve.wait_ge(src_hi_done, k + 1)
                nc.vector.tensor_tensor(src_lo[:, k, :], src[:, k, :], src_hi[:, k, :].bitcast(F32),
                                        ALU.subtract).then_inc(src_lo_done, 1)
            with dve.Fori(0, pairs) as i:
                for u in range(2):
                    one(2 * i + u, u)
            if blocks % 2:
                one(blocks - 1, 0)
            if norm:
                norm.scale_rest(dve)


def split_tiles(ap):
    return ap.rearrange("p (a t) -> p a t", a=NT)


def block_of(buf, m):
    return buf[:, bass.ds(m, 1), :].rearrange("p b (a t) -> p (b a) t", a=NT)


def output_projection(c, w, kt, src, next_layer):
    streamed_projection(c, w, KD, kt, src, lambda m, psum: c.nc.vector.tensor_tensor(
        block_of(c.x, m), psum, block_of(c.x, m), ALU.add), next_layer)



class Mla:

    def __init__(self, st, z):
        self.z = z
        self.cq = self.z[:, 0:NQL, :]
        self.ckv = self.z[:, NQL:NQL + NKV, :]
        self.gate = self.z[:, NQL + NKV:, :]
        self.trig = st.sb("trig", [P, T])
        self.kraw = st.sb("kraw", [P, T])
        self.v = st.sb("values", [P, QT + 1, H * DV])
        self.wuv = st.sb("w_uv", [P, NKV, H * DV])
        self.qs = st.sb("sample_queries", [QK, H, NS])
        self.snew = st.sb("new_token_scores", [P, NS, H])
        self.accn = st.sb("sample_latents", [P, NKV, H, NS])


def latent_norm(nc, c, engine, which, buf, n, width, gain, sq, rstd, s):
    if which == "scalar":
        for k in range(n):
            if k >= 2:
                engine.wait_ge(s["summed"], k - 1)
            nc.scalar.activation(sq[:, k % 2, :], buf[:, k, :], ACT.Square).then_inc(s["squared"], 1)
        engine.wait_ge(s["summed"], n)
        nc.scalar.activation(split_tiles(rstd[:, :]), c.ps[:, NT:2 * NT, 0:TT], ACT.Ln,
                             scale=1.0 / width, bias=c.eps()).then_inc(s["logged"], 1)
        engine.wait_ge(s["logged"], 1)
        nc.scalar.activation(rstd[:, :], rstd[:, :], ACT.Exp, scale=-0.5).then_inc(s["rstd"], 1)
    elif which == "tensor":
        for k in range(n):
            engine.wait_ge(s["squared"], k + 1)
            for t, cols in tiles():
                mm = nc.tensor.matmul(c.ps[:, NT + t, 0:TT], c.ones[:, :], sq[:, k % 2, cols],
                                      start=(k == 0), stop=(k == n - 1))
            mm.then_inc(s["summed"], 1)
    else:
        engine.wait_ge(s["rstd"], 1)
        for k in range(n):
            nc.vector.scalar_tensor_tensor(buf[:, k, :], buf[:, k, :], gain[:, k:k + 1], rstd[:, :],
                                           op0=ALU.mult, op1=ALU.mult).then_inc(s["done"], 1)


def mla_latents(c, m, j):
    nc, dram = c.nc, c.dram
    with Stage(c) as st:
        wkpe = st.sb("w_kpe", [P, KD, 2 * ROPE])
        gql = st.sb("g_q_lora", [P, NQL])
        gkv = st.sb("g_kv", [P, NKV])
        sq = st.sb("squares", [P, 2, T])
        rstd = st.sb("rstd", [P, 2, T])
        rot = st.sb("rotated", [P, 2, T])
        loads = st.sem("loads")
        kpe_summed = st.sem("kpe_summed")
        kpe_parts = st.sem("kpe_parts")
        kpe_done = st.sem("kpe_done")
        sem_kv = {k: st.sem("ckv_" + k) for k in ("squared", "summed", "logged", "rstd", "done")}
        sem_q = {k: st.sem("cq_" + k) for k in ("squared", "summed", "logged", "rstd", "done")}
        v_summed = st.sem("v_summed")
        v_drained = st.sem("v_drained")
        stored = st.sem("stored")
        block = st.block()

        @block.sync
        def _(sp):
            sp.dma_start(wkpe[:, :, :], dram["w_kpe"][j]).then_inc(loads, 16)
            sp.dma_start(m.trig[:, :], dram["trig"]).then_inc(loads, 16)
            sp.dma_start(gql[:, :], dram["g_q_lora"][j]).then_inc(loads, 16)
            sp.dma_start(gkv[:, :], dram["g_kv"][j]).then_inc(loads, 16)
            sp.dma_start(m.wuv[:, :, :], dram["w_uv"][j]).then_inc(loads, 16)
            sp.wait_ge(sem_kv["done"], NKV)
            sp.dma_start(dram["o_ckv"][j], m.ckv).then_inc(stored, 16)
            sp.wait_ge(kpe_done, 1)
            sp.dma_start(dram["o_kpe"][j], m.kraw[NOPE:QK, :]).then_inc(stored, 16)
            sp.wait_ge(stored, 32)

        @block.tensor
        def _(pe):
            latent_norm(nc, c, pe, "tensor", m.ckv, NKV, KVL, gkv, sq, rstd[:, 0, :], sem_kv)
            pe.wait_ge(loads, 16 * 5)
            for t, cols in tiles():
                for k in range(KD):
                    mm = nc.tensor.matmul(c.ps[NOPE:P, t, 0:TT], wkpe[:, k, :], c.h[:, k, cols],
                                          start=(k == 0), stop=(k == KD - 1))
            mm.then_inc(kpe_summed, 1)
            pe.wait_ge(sem_kv["logged"], 1)
            latent_norm(nc, c, pe, "tensor", m.cq, NQL, QL, gql, sq, rstd[:, 1, :], sem_q)
            pe.wait_ge(sem_kv["done"], NKV)
            for tt in range(QT + 1):
                rows = P if tt < QT else NS
                if tt >= 2:
                    pe.wait_ge(v_drained, tt - 1)
                for k in range(NKV):
                    mm = nc.tensor.matmul(c.ps[0:rows, 6 + tt % 2, :], m.ckv[:, k, tt * P:tt * P + rows],
                                          m.wuv[:, k, :], start=(k == 0), stop=(k == NKV - 1))
                mm.then_inc(v_summed, 1)

        @block.scalar
        def _(act):
            load_ln_exp(nc)
            latent_norm(nc, c, act, "scalar", m.ckv, NKV, KVL, gkv, sq, rstd[:, 0, :], sem_kv)
            latent_norm(nc, c, act, "scalar", m.cq, NQL, QL, gql, sq, rstd[:, 1, :], sem_q)
            for tt in range(QT + 1):
                rows = P if tt < QT else NS
                act.wait_ge(v_summed, tt + 1)
                nc.scalar.activation(m.v[0:rows, tt, :], c.ps[0:rows, 6 + tt % 2, :], ACT.Copy) \
                  .then_inc(v_drained, 1)
            for k in range(NG):
                nc.scalar.activation(m.gate[:, k, :], m.gate[:, k, :], ACT.Silu)

        @block.vector
        def _(dve):
            dve.wait_ge(loads, 16 * 5)
            latent_norm(nc, c, dve, "vector", m.ckv, NKV, KVL, gkv, sq, rstd[:, 0, :], sem_kv)
            dve.wait_ge(kpe_summed, 1)
            nc.vector.tensor_tensor(split_tiles(rot[NOPE:QK, 0, :]), c.ps[NOPE:QK, 0:NT, 0:TT],
                                    split_tiles(m.trig[NOPE:QK, :]), ALU.mult).then_inc(kpe_parts, 1)
            nc.vector.tensor_tensor(split_tiles(rot[NOPE:QK, 1, :]), c.ps[QK:P, 0:NT, 0:TT],
                                    split_tiles(m.trig[QK:P, :]), ALU.mult).then_inc(kpe_parts, 1)
            dve.wait_ge(kpe_parts, 2)
            nc.vector.tensor_tensor(m.kraw[NOPE:QK, :], rot[NOPE:QK, 0, :], rot[NOPE:QK, 1, :],
                                    ALU.add).then_inc(kpe_done, 1)
            latent_norm(nc, c, dve, "vector", m.cq, NQL, QL, gql, sq, rstd[:, 1, :], sem_q)


def mla_prompt_attention(c, m, j, o_tok):
    nc, dram = c.nc, c.dram
    with Stage(c) as st:
        wq = st.sb("w_q", [P, 2, NQL, P])
        wk = st.sb("w_k", [P, 2, NKV, NOPE])
        q = st.sb("q", [P, 2, T])
        kn = st.sb("kn", [P, 2, T])
        qraw = st.sb("qraw", [P, T])
        rot = st.sb("rotated", [P, T])
        sq_q = st.sb("sq_q", [P, T])
        sq_k = st.sb("sq_k", [P, T])
        rk = st.sb("rk", [P, T])
        probs = st.sb("probs", [P, 2, SEQ])
        probs_t = st.sb("probs_t", [P, 4, 512])
        causal = st.sb("causal", [P, P])
        gq = st.sb("g_q", [QK, 2])
        gqk = st.sb("g_qk", [QK, 1])
        rq = st.sb("rq", [P, 2, 2 * QT])
        nmax = st.sb("nmax", [P, 2])
        bias = st.sb("bias", [P, 2])
        rowsum = st.sb("rowsum", [P, 4])
        inv = st.sb("inv", [P, 2])
        prod = st.sb("prod", [QK, NS])
        qs_now = st.sb("qs_now", [QK, NS])
        S = [c.ps[:, 0:2, :].rearrange("p a n -> p (a n)"), c.ps[:, 2:4, :].rearrange("p a n -> p (a n)")]
        X = c.ps[:, 7, :]

        def wait_taken(engine, h, n):
            engine.wait_ge(x_taken[n % 2], NT * h + (n // 2 + 1))

        def bank(h, n):
            return c.ps[:, n if isinstance(h, int) and h == 0 else 7, :]

        loads = st.sem("loads")
        w_landed = [st.sem("w_landed0"), st.sem("w_landed1")]
        gains_done = st.sem("gains_done")
        x_summed = st.sem("x_summed")
        x_taken = [st.sem("x_taken_by_vector"), st.sem("x_taken_by_scalar")]
        q_parts = st.sem("q_parts")
        qraw_done = st.sem("qraw_done")
        sq_q_done = st.sem("sq_q_done")
        sq_k_done = st.sem("sq_k_done")
        q_done = st.sem("q_done")
        rk_logged = st.sem("rk_logged")
        rk_done = st.sem("rk_done")
        kn_done = st.sem("kn_done")
        rq_logged = st.sem("rq_logged")
        rq_done = st.sem("rq_done")
        qs_done = st.sem("qs_done")
        prod_done = st.sem("prod_done")
        scored = st.sem("scored")
        masked = st.sem("masked")
        maxed = st.sem("maxed")
        snew_done = st.sem("snew_done")
        bias_done = st.sem("bias_done")
        exped = st.sem("exped")
        turned = st.sem("turned")
        pt_ready = st.sem("pt_ready")
        pv_read = st.sem("pv_read")
        inverted = st.sem("inverted")
        o_stored = st.sem("o_stored")
        block = st.block()

        NX = 11
        batches = [(qt, b) for qt in range(QT) for b in range(qt // 4 + 1)]
        NB = len(batches)
        of_tile = [[(n, b) for n, (q_, b) in enumerate(batches) if q_ == qt] for qt in range(QT)]

        def heads(engine, attend):
            attend(0, 0, 1)
            with engine.Fori(0, (H - 2) // 2) as i:
                attend(2 * i + 1, 1, 2 * i + 2)
                attend(2 * i + 2, 0, 2 * i + 3)
            attend(H - 1, 1, None)

        def ahead(part, h, u, following, qt):
            if qt < QT:
                part(h, u, qt)
            elif following is not None:
                part(following, 1 - u, qt - QT)

        def place(steps, n):
            if n in steps:
                steps[n]()

        def take_tiles(engine, copy, h):
            def step(n, t, cols):
                def f():
                    engine.wait_ge(x_summed, NX * h + (n + 1))
                    if n == 0:
                        wait(engine, kn_done, h)
                        wait(engine, sq_k_done, h)
                    if n == NT:
                        wait(engine, q_done, h)
                        wait(engine, sq_q_done, h)
                    if n < NT:
                        copy(m.kraw[0:NOPE, cols], bank(h, n)[0:NOPE, 0:TT]).then_inc(x_taken[n % 2], 1)
                    else:
                        copy(qraw[:, cols], bank(h, n)[:, 0:TT]).then_inc(x_taken[n % 2], 1)
                return f
            return [step(n, *tiles()[n % NT]) for n in range(2 * NT)]

        @block.sync
        def _(sp):
            def load(h, u):
                for slot, w in ((wq, dram["w_uq"][j]), (wk, dram["w_uk"][j])):
                    sp.dma_start(slot[:, u, :, :], w[bass.ds(h, 1)].rearrange("a p k m -> p (a k) m")) \
                      .then_inc(w_landed[u], 16)

            load(0, 0)
            sp.dma_start(gq[:, :], dram["g_qk"][j]).then_inc(loads, 16)
            sp.dma_start(causal[:, :], dram["causal"]).then_inc(loads, 16)
            load(1, 1)
            with sp.Fori(1, H // 2) as i:
                for u in range(2):
                    sp.wait_ge(x_summed, 2 * NX * i + (NX * u - 2 * NX + 2 * NT))
                    load(2 * i + u, u)

        @block.gpsimd
        def _(pool):
            def scale_q(h, u):
                wait_taken(pool, h, 2 * NT - 2)
                wait_taken(pool, h, 2 * NT - 1)
                wait(pool, sq_q_done, h)
                nc.gpsimd.tensor_tensor(rot[NOPE:QK, :], qraw[QK:P, :], m.trig[QK:P, :], ALU.mult) \
                  .then_inc(q_parts, 1)
                nc.gpsimd.tensor_tensor(qraw[NOPE:QK, :], qraw[NOPE:QK, :], m.trig[NOPE:QK, :], ALU.mult) \
                  .then_inc(q_parts, 1)
                pool.wait_ge(q_parts, 2 * h + 2)
                nc.gpsimd.tensor_tensor(qraw[NOPE:QK, :], qraw[NOPE:QK, :], rot[NOPE:QK, :], ALU.add) \
                  .then_inc(qraw_done, 1)
                pool.wait_ge(qraw_done, h + 1)
                wait(pool, scored, QT * h - QT)
                nc.gpsimd.tensor_tensor(q[0:QK, u, :], qraw[0:QK, :], gqk[:, 0:1].broadcast_to([QK, T]),
                                        ALU.mult).then_inc(q_done, 1)

            pool.wait_ge(gains_done, 1)
            scale_q(0, 0)
            scale_q(1, 1)
            with pool.Fori(1, H // 2) as i:
                for u in range(2):
                    scale_q(2 * i + u, u)

        @block.tensor
        def _(pe):
            def prep(h, u):
                first = isinstance(h, int) and h == 0

                def q_tile(t, cols):
                    def f():
                        if not first:
                            wait_taken(pe, h, NT + t - 1)
                        for k in range(NQL):
                            mm = nc.tensor.matmul(bank(h, NT + t)[:, 0:TT], wq[:, u, k, :], m.cq[:, k, cols],
                                                  start=(k == 0), stop=(k == NQL - 1))
                        mm.then_inc(x_summed, 1)
                    return f

                def k_tile(t, cols):
                    def f():
                        if t == 0:
                            wait(pe, snew_done, h)
                            pe.wait_ge(w_landed[u], 16 * h + (32 - 16 * u))
                        elif not first:
                            wait_taken(pe, h, t - 1)
                        for k in range(NKV):
                            mm = nc.tensor.matmul(bank(h, t)[0:NOPE, 0:TT], wk[:, u, k, :], m.ckv[:, k, cols],
                                                  start=(k == 0), stop=(k == NKV - 1))
                        mm.then_inc(x_summed, 1)
                    return f

                def k_sums(t, cols):
                    def f():
                        if t == 0:
                            pe.wait_ge(sq_k_done, h + 1)
                            wait_taken(pe, h, 2 * NT - 1)
                        else:
                            pe.wait_ge(rk_logged, NT * h + t)
                        nc.tensor.matmul(X[0:QK, 0:TT], c.ones[0:QK, 0:QK], sq_k[0:QK, cols],
                                         start=True, stop=True).then_inc(x_summed, 1)
                    return f

                def q_sums():
                    pe.wait_ge(rk_logged, NT * h + NT)
                    pe.wait_ge(sq_q_done, h + 1)
                    for qt in range(QT):
                        nc.tensor.matmul(X[:, qt:qt + 1], sq_q[0:QK, qt * P:(qt + 1) * P], c.ones[0:QK, 0:1],
                                         start=True, stop=True)
                    nc.tensor.matmul(X[:, QT:QT + NS], c.ones[0:QK, :], sq_q[0:QK, SEQ:T],
                                     start=True, stop=True).then_inc(x_summed, 1)

                def new_scores():
                    pe.wait_ge(prod_done, h + 1)
                    nc.tensor.matmul(X[:, 0:NS], c.ones[0:QK, :], prod[:, :],
                                     start=True, stop=True).then_inc(x_summed, 1)

                qs = [q_tile(*x) for x in tiles()]
                ks = [k_tile(*x) for x in tiles()]
                rs = [k_sums(*x) for x in tiles()]
                return {0: ks[0], 1: ks[1], 2: ks[2], 3: qs[0], 4: qs[1], 5: qs[2],
                        6: rs[0], 7: rs[1], 8: rs[2], 10: q_sums, 13: new_scores}

            def scores(h, u, qt):
                if qt == 0:
                    pe.wait_ge(q_done, h + 1)
                    pe.wait_ge(kn_done, h + 1)
                wait(pe, exped, QT * h + (qt - 1))
                n = (qt + 1) * P
                for lo in range(0, n, 512):
                    hi = min(n, lo + 512)
                    mm = nc.tensor.matmul(S[qt % 2][:, lo:hi], q[0:QK, u, qt * P:(qt + 1) * P],
                                          kn[0:QK, u, lo:hi], start=True, stop=True)
                mm.then_inc(scored, 1)

            def turn(h, qt):
                pe.wait_ge(exped, QT * h + (qt + 1))
                for n, b in of_tile[qt]:
                    wait(pe, pt_ready, NB * h + (n - 1))
                    for kt in range(4 * b, min(4 * b + 4, qt + 1)):
                        mm = nc.tensor.transpose(c.ps[:, 4 + n % 2, (kt % 4) * P:(kt % 4 + 1) * P],
                                                 probs[:, qt % 2, kt * P:(kt + 1) * P], c.ident[:, :])
                    mm.then_inc(turned, 1)

            def weigh(h, qt):
                wait(pe, o_stored, QT * h + qt)
                for n, b in of_tile[qt]:
                    pe.wait_ge(pt_ready, NB * h + (n + 1))
                    for kt in range(4 * b, min(4 * b + 4, qt + 1)):
                        mm = nc.tensor.matmul(c.ps[:, 6, 0:DV],
                                              probs_t[:, n % 4, (kt % 4) * P:(kt % 4 + 1) * P],
                                              m.v[:, kt, bass.ds(h * DV, DV)],
                                              start=(kt == 0), stop=(kt == qt))
                    mm.then_inc(pv_read, 1)

            def attend(h, u, following):
                steps = {} if following is None else prep(following, 1 - u)
                for qt in range(QT):
                    ahead(scores, h, u, following, qt + 2)
                    place(steps, 2 * qt)
                    ahead(lambda h, u, qt: turn(h, qt), h, u, following, qt + 1)
                    place(steps, 2 * qt + 1)
                    weigh(h, qt)

            for f in prep(0, 0).values():
                f()
            scores(0, 0, 0)
            scores(0, 0, 1)
            turn(0, 0)
            heads(pe, attend)

        @block.vector
        def _(dve):
            def prep(h, u):
                def keys():
                    dve.wait_ge(rk_done, h + 1)
                    wait(dve, scored, QT * h - QT)
                    nc.vector.tensor_tensor(kn[0:QK, u, :], m.kraw[0:QK, :], rk[0:QK, :], ALU.mult) \
                      .then_inc(kn_done, 1)

                def sample_queries():
                    dve.wait_ge(rq_done, h + 1)
                    dve.wait_ge(q_done, h + 1)
                    wait(dve, x_summed, NX * h)
                    nc.vector.tensor_tensor(qs_now[:, :], q[0:QK, u, SEQ:T], rq[0:QK, u, QT:QT + NS],
                                            ALU.mult).then_inc(qs_done, 1)
                    dve.wait_ge(qs_done, 2 * h + 1)
                    dve.wait_ge(kn_done, h + 1)
                    nc.vector.tensor_tensor(prod[:, :], qs_now[:, :], kn[0:QK, u, SEQ:T],
                                            ALU.mult).then_inc(prod_done, 1)
                    nc.vector.tensor_copy(m.qs[:, bass.ds(h, 1), :].rearrange("p a n -> p (a n)"), qs_now[:, :]) \
                      .then_inc(qs_done, 1)

                def new_scores():
                    dve.wait_ge(x_summed, NX * h + NX)
                    dve.wait_ge(qs_done, 2 * h + 2)
                    nc.vector.tensor_copy(m.snew[:, :, bass.ds(h, 1)].rearrange("p n a -> p (n a)"),
                                          X[:, 0:NS]).then_inc(snew_done, 1)

                takes = take_tiles(dve, nc.vector.tensor_copy, h)
                return {0: takes[0], 2: takes[2], 4: takes[4], 10: keys, 12: sample_queries, 14: new_scores}

            def row_max(h, u, qt):
                b = qt % 2
                diag = S[b][:, qt * P:(qt + 1) * P]
                if qt == 0:
                    dve.wait_ge(rq_done, h + 1)
                dve.wait_ge(scored, QT * h + (qt + 1))
                nc.vector.tensor_tensor(diag, diag, causal[:, :], ALU.add).then_inc(masked, 1)
                dve.wait_ge(masked, QT * h + (qt + 1))
                nc.vector.tensor_reduce(nmax[:, b:b + 1], S[b][:, 0:(qt + 1) * P], AX.X, ALU.max,
                                        negate=True).then_inc(maxed, 1)
                dve.wait_ge(maxed, QT * h + (qt + 1))
                wait(dve, exped, QT * h + (qt - 1))
                nc.vector.tensor_tensor(bias[:, b:b + 1], nmax[:, b:b + 1], rq[:, u, qt:qt + 1],
                                        ALU.mult).then_inc(bias_done, 1)

            def take_turned(h, qt):
                for n, b in of_tile[qt]:
                    width = (min(4 * b + 4, qt + 1) - 4 * b) * P
                    dve.wait_ge(turned, NB * h + (n + 1))
                    wait(dve, pv_read, NB * h + (n - 3))
                    nc.vector.tensor_copy(probs_t[:, n % 4, 0:width], c.ps[:, 4 + n % 2, 0:width]) \
                      .then_inc(pt_ready, 1)

            def attend(h, u, following):
                steps = {} if following is None else prep(following, 1 - u)
                for qt in range(QT):
                    ahead(row_max, h, u, following, qt + 2)
                    place(steps, 2 * qt)
                    ahead(lambda h, u, qt: take_turned(h, qt), h, u, following, qt + 1)
                    place(steps, 2 * qt + 1)
                    dve.wait_ge(exped, QT * h + (qt + 1))
                    nc.vector.reciprocal(inv[:, qt % 2:qt % 2 + 1], rowsum[:, qt % 4:qt % 4 + 1]) \
                      .then_inc(inverted, 1)
                    dve.wait_ge(inverted, QT * h + (qt + 1))
                    dve.wait_ge(pv_read, NB * h + (of_tile[qt][-1][0] + 1))
                    nc.vector.tensor_scalar(o_tok[:, qt, bass.ds(h * DV, DV)], c.ps[:, 6, 0:DV],
                                            inv[:, qt % 2:qt % 2 + 1], None, op0=ALU.mult) \
                      .then_inc(o_stored, 1)

            dve.wait_ge(loads, 32)
            nc.vector.tensor_tensor(gqk[:, :], gq[:, 0:1], gq[:, 1:2], ALU.mult).then_inc(gains_done, 1)
            for f in prep(0, 0).values():
                f()
            row_max(0, 0, 0)
            row_max(0, 0, 1)
            take_turned(0, 0)
            heads(dve, attend)

        @block.scalar
        def _(act):
            load_ln_exp(nc)
            def prep(h, u):
                def q_squares():
                    act.wait_ge(qraw_done, h + 1)
                    wait(act, x_summed, NX * h)
                    nc.scalar.activation(sq_q[0:QK, :], qraw[0:QK, :], ACT.Square).then_inc(sq_q_done, 1)

                def k_squares():
                    wait_taken(act, h, NT - 2)
                    wait_taken(act, h, NT - 1)
                    nc.scalar.activation(sq_k[0:QK, :], m.kraw[0:QK, :], ACT.Square).then_inc(sq_k_done, 1)

                def k_log(t, cols):
                    def f():
                        act.wait_ge(x_summed, NX * h + (2 * NT + t + 1))
                        if t == 0:
                            wait(act, kn_done, h)
                        nc.scalar.activation(rk[0:QK, cols], X[0:QK, 0:TT], ACT.Ln, scale=1.0 / QK,
                                             bias=c.eps(QK)).then_inc(rk_logged, 1)
                    return f

                def k_exp():
                    act.wait_ge(rk_logged, NT * h + NT)
                    nc.scalar.activation(rk[0:QK, :], rk[0:QK, :], ACT.Exp, scale=-0.5).then_inc(rk_done, 1)

                def q_log():
                    act.wait_ge(x_summed, NX * h + (NX - 1))
                    wait(act, exped, QT * h - QT)
                    wait(act, qs_done, 2 * h - 2)
                    nc.scalar.activation(rq[:, u, :], X[:, 0:2 * QT], ACT.Ln, scale=1.0 / QK,
                                         bias=c.eps()).then_inc(rq_logged, 1)

                def q_exp():
                    act.wait_ge(rq_logged, h + 1)
                    nc.scalar.activation(rq[:, u, :], rq[:, u, :], ACT.Exp, scale=-0.5,
                                         bias=c.const[:, C_LNSCALE:C_LNSCALE + 1]).then_inc(rq_done, 1)

                takes = take_tiles(act, lambda out, x: nc.scalar.activation(out, x, ACT.Copy), h)
                rs = [k_log(*x) for x in tiles()]
                return {1: [takes[1]], 3: [takes[3]], 4: [k_squares], 5: [takes[5]], 6: [rs[0]], 7: [rs[1]],
                        8: [rs[2], k_exp], 9: [q_squares], 10: [q_log], 11: [q_exp]}

            def exponentials(h, u, qt):
                act.wait_ge(bias_done, QT * h + (qt + 1))
                if qt >= 2:
                    act.wait_ge(turned, NB * h + (of_tile[qt - 2][-1][0] + 1))
                else:
                    wait(act, turned, NB * h + (of_tile[QT - 2 + qt][-1][0] + 1 - NB))
                wait(act, inverted, QT * h + (qt - 3))
                n = (qt + 1) * P
                nc.scalar.activation(probs[:, qt % 2, 0:n], S[qt % 2][:, 0:n], ACT.Exp,
                                     scale=rq[:, u, qt:qt + 1], bias=bias[:, qt % 2:qt % 2 + 1],
                                     accum_out=rowsum[:, qt % 4:qt % 4 + 1]).then_inc(exped, 1)

            def attend(h, u, following):
                steps = {} if following is None else prep(following, 1 - u)
                for qt in range(QT):
                    ahead(exponentials, h, u, following, qt + 2)
                    for n in (2 * qt, 2 * qt + 1):
                        for f in steps.get(n, []):
                            f()

            for fs in prep(0, 0).values():
                for f in fs:
                    f()
            exponentials(0, 0, 0)
            exponentials(0, 0, 1)
            heads(act, attend)


def mla_sample_attention(c, m, j):
    nc, dram = c.nc, c.dram
    with Stage(c) as st:
        nat = st.sb("pages", [P, 2, PAGES, NAT])
        RING = 4
        lat_t = st.sb("latents_t", [P, RING, NKV, PAGE])
        kpe_t = st.sb("kpe_t", [ROPE, RING, PAGE])
        wukt = st.sb("w_uk_t", [NOPE, H, KVL])
        wuk_hi = st.sb("w_uk_hi", [P, NKV, H * NOPE], F32R)
        wuk_lo = st.sb("w_uk_lo", [P, NKV, H * NOPE], F32R)
        lat_hi = st.sb("latents_t_hi", [P, 2, NKV, PAGE], F32R)
        lat_lo = st.sb("latents_t_lo", [P, 2, NKV, PAGE], F32R)
        table = st.sb("page_table", [1, NS * PAGES], I32)
        qlat = st.sb("latent_queries", [P, NKV, NS, H])
        qpe = st.sb("rope_queries", [ROPE, NS, H])
        sq = st.sb("key_squares", [P, 2, H * NOPE])
        wuk = sq
        kk = st.sb("kpe_squares", [P, PAGES, ROPE])
        kks = st.sb("kpe_sums", [P, 2, PAGES])
        ss = st.sb("sums", [P, 2, PAGES, H])
        rk = st.sb("rk", [P, PAGES, H])
        sc = st.sb("scores", [P, PAGES, H])
        pr = st.sb("probs", [P, PAGES, H])
        mx = st.sb("max", [P, H])
        top = st.sb("top", [H, 1])
        diag = st.sb("diag", [H, H])
        mall = st.sb("max_all", [P, H])
        pnew = st.sb("new_prob", [P, H])
        lsum = st.sb("row_sums", [P, H])
        ltot = st.sb("total", [P, H])
        part = st.sb("new_part", [P, NKV, H])
        acc = st.sb("weighted_latents", [H, KVL])
        ckvs = st.sb("new_latents", [P, NS, NKV])

        loads = st.sem("loads")
        wk_landed = st.sem("wk_landed")
        nat_landed = [st.sem("nat_landed0"), st.sem("nat_landed1")]
        ring_landed = [st.sem(f"ring_landed{r}") for r in range(RING)]
        q_summed = st.sem("q_summed")
        q_ready = st.sem("q_ready")
        wuk_split = st.sem("wuk_split")
        hi_done = st.sem("hi_done")
        lo_done = st.sem("lo_done")
        expanded = st.sem("expanded")
        squared = st.sem("squared")
        scored = st.sem("scored")
        ssum = st.sem("ssum")
        kk_done = st.sem("kk_done")
        kks_done = st.sem("kks_done")
        ss_done = st.sem("ss_done")
        rk_logged = st.sem("rk_logged")
        rk_done = st.sem("rk_done")
        sc_done = st.sem("sc_done")
        mx_done = st.sem("mx_done")
        mx_turned = st.sem("mx_turned")
        top_done = st.sem("top_done")
        diag_done = st.sem("diag_done")
        m_summed = st.sem("m_summed")
        m_done = st.sem("m_done")
        pn_done = st.sem("pn_done")
        pr_done = st.sem("pr_done")
        l_done = st.sem("l_done")
        l_summed = st.sem("l_summed")
        inv_done = st.sem("inv_done")
        weighted = st.sem("weighted")
        acc_taken = st.sem("acc_taken")
        acc_turned = st.sem("acc_turned")
        part_done = st.sem("part_done")
        acc_done = st.sem("acc_done")
        block = st.block()
        KEYS = [c.ps[:, 0, :], c.ps[:, 1, :]]
        SC = [c.ps[:, 2, 0:PAGES * H], c.ps[:, 3, 0:PAGES * H]]
        ACC = c.ps[:, 6, 0:NKV * H]
        SMALL = c.ps[:, 4, :]
        tok = dram["pages"][j]
        tok_t = dram["pages_t"][j]
        kp_t = dram["pages_kpe_t"][j]

        def sequences(engine, pages, tail):
            pages(0, 0, None)
            pages(1, 1, tail(0, 0))
            pages(2, 0, tail(1, 1))
            with engine.Fori(1, (NS - 2) // 2) as i:
                pages(2 * i + 1, 1, tail(2 * i, 0))
                pages(2 * i + 2, 0, tail(2 * i + 1, 1))
            pages(NS - 1, 1, tail(NS - 2, 0))
            for f in tail(NS - 1, 1).values():
                f()

        def run(steps, p):
            if steps is not None and p in steps:
                steps[p]()

        @block.sync
        def _(sp):
            sp.dma_start(table[:, :], dram["page_table"]).then_inc(loads, 16)
            sp.dma_start(wukt[:, :, :], dram["w_uk_t"][j]).then_inc(wk_landed, 16)
            sp.dma_start(wuk[:, :, :], dram["w_uk_all"][j]).then_inc(wk_landed, 16)
            sp.wait_ge(loads, 16)

            def pages(b, u, steps):
                wait(sp, weighted, b - 1)
                for p in range(PAGES):
                    r = p % RING
                    page = sp.value_load(table[0:1, bass.ds(b * PAGES + p, 1)], min_val=0,
                                         max_val=tok.shape[0] - 1)
                    wait(sp, scored, PAGES * b + (p + 1 - RING))
                    sp.dma_start(lat_t[:, r, :, :], tok_t[bass.ds(page, 1)].rearrange("a p k t -> p (a k) t")) \
                      .then_inc(ring_landed[r], 16)
                    sp.dma_start(kpe_t[:, r, :], kp_t[bass.ds(page, 1)].rearrange("a p t -> p (a t)")) \
                      .then_inc(ring_landed[r], 16)
                    sp.dma_start(nat[:, u, p, :], tok[bass.ds(page, 1)].rearrange("a p f -> p (a f)")) \
                      .then_inc(nat_landed[u], 16)

            pages(0, 0, None)
            pages(1, 1, None)
            with sp.Fori(1, NS // 2) as i:
                for u in range(2):
                    pages(2 * i + u, u, None)

        @block.gpsimd
        def _(pool):
            def kpe_squares(b, u):
                pool.wait_ge(nat_landed[u], 16 * PAGES * ((b - u) // 2 + 1) if isinstance(b, int)
                             else 8 * PAGES * b + (16 * PAGES - 8 * PAGES * u))
                wait(pool, kks_done, b)
                nc.gpsimd.tensor_tensor(kk[:, :, :], nat[:, u, :, KVL:NAT], nat[:, u, :, KVL:NAT],
                                        ALU.mult).then_inc(kk_done, 1)

            def latents_lo(b, p):
                pool.wait_ge(hi_done, PAGES * b + (p + 1))
                nc.gpsimd.tensor_tensor(lat_lo[:, p % 2, :, :], lat_t[:, p % RING, :, :],
                                        lat_hi[:, p % 2, :, :].bitcast(F32), ALU.subtract).then_inc(lo_done, 1)

            def sequence(b, u):
                for p in range(PAGES):
                    latents_lo(b, p)
                kpe_squares(b, u)

            pool.wait_ge(wuk_split, 1)
            nc.gpsimd.tensor_tensor(wuk_lo[:, :, :], wuk[:, :, :], wuk_hi[:, :, :].bitcast(F32), ALU.subtract) \
              .then_inc(wuk_split, 1)
            sequence(0, 0)
            sequence(1, 1)
            with pool.Fori(1, NS // 2) as i:
                for u in range(2):
                    sequence(2 * i + u, u)

        @block.tensor
        def _(pe):
            def tail(b, u):
                def turn_max():
                    pe.wait_ge(mx_done, 2 * b + 2)
                    wait(pe, inv_done, 2 * b)
                    nc.tensor.transpose(SMALL[0:H, 0:P], mx[:, :], c.ident[:, :]).then_inc(mx_turned, 1)

                def spread_max():
                    pe.wait_ge(diag_done, b + 1)
                    nc.tensor.matmul(SMALL[:, P:P + H], c.ones[0:H, :], diag[:, :],
                                     start=True, stop=True).then_inc(m_summed, 1)

                def total():
                    pe.wait_ge(l_done, b + 1)
                    nc.tensor.matmul(SMALL[:, 2 * P:2 * P + H], c.ones[:, :], lsum[:, :],
                                     start=True, stop=True).then_inc(l_summed, 1)

                def weighted_sums(part):
                    def f():
                        if part == 0:
                            pe.wait_ge(pr_done, 2 * b + 2)
                            wait(pe, acc_taken, b)
                        for p in range(part * PAGES // 4, (part + 1) * PAGES // 4):
                            mm = nc.tensor.matmul(c.ps[0:H, 5, 0:KVL], pr[:, p, :], nat[:, u, p, 0:KVL],
                                                  start=(p == 0), stop=(p == PAGES - 1))
                        if part == 3:
                            mm.then_inc(weighted, 1)
                    return f

                def turn_sums():
                    pe.wait_ge(acc_taken, b + 1)
                    wait(pe, acc_done, NKV * b)
                    for k in range(NKV):
                        mm = nc.tensor.matmul(ACC[:, k * H:(k + 1) * H], acc[:, k * P:(k + 1) * P],
                                              c.ident[0:H, 0:H], start=True, stop=True)
                    mm.then_inc(acc_turned, 1)

                w = [weighted_sums(n) for n in range(4)]
                return {4: turn_max, 6: spread_max, 8: w[0], 9: w[1], 10: w[2], 11: w[3], 12: total, 13: turn_sums}

            def pages(b, u, steps):
                for p in range(PAGES):
                    r, e = p % RING, p % 2
                    pe.wait_ge(ring_landed[r], 32 * (PAGES // RING) * b + 32 * (p // RING + 1))
                    pe.wait_ge(lo_done, PAGES * b + (p + 1))
                    wait(pe, squared, PAGES * b + (p - 1))
                    products = [(x, y, k) for k in range(NKV)
                                for x, y in ((lat_hi, wuk_hi), (lat_hi, wuk_lo), (lat_lo, wuk_hi))]
                    for n, (x, y, k) in enumerate(products):
                        mm = nc.tensor.matmul(KEYS[e], x[:, e, k, :], y[:, k, :],
                                              start=(n == 0), stop=(n == len(products) - 1))
                    mm.then_inc(expanded, 1)
                    if p == 0:
                        wait(pe, sc_done, 2 * b - 2)
                    cols = slice(p * H, (p + 1) * H)
                    for k in range(NKV):
                        nc.tensor.matmul(SC[u][:, cols], lat_t[:, r, k, :],
                                         qlat[:, k, bass.ds(b, 1), :].rearrange("p a h -> p (a h)"),
                                         start=(k == 0), stop=False)
                    nc.tensor.matmul(SC[u][:, cols], kpe_t[:, r, :],
                                     qpe[:, bass.ds(b, 1), :].rearrange("p a h -> p (a h)"),
                                     start=False, stop=True).then_inc(scored, 1)
                    run(steps, p)

            pe.wait_ge(wk_landed, 32)
            for h in range(H):
                for k in range(NKV):
                    mm = nc.tensor.matmul(c.ps[:, 4 + k, h * NS:(h + 1) * NS], wukt[:, h, k * P:(k + 1) * P],
                                          m.qs[0:NOPE, h, :], start=True, stop=True)
            mm.then_inc(q_summed, 1)
            pe.wait_ge(q_ready, NKV + 1)
            pe.wait_ge(wuk_split, 2)
            sequences(pe, pages, tail)

        @block.scalar
        def _(act):
            load_ln_exp(nc)
            def tail(b, u):
                def key_factor():
                    act.wait_ge(ss_done, b + 1)
                    wait(act, sc_done, 2 * b)
                    nc.scalar.activation(rk[:, :, :], ss[:, u, :, :], ACT.Ln, scale=1.0 / QK, bias=c.eps()) \
                      .then_inc(rk_logged, 1)
                    act.wait_ge(rk_logged, b + 1)
                    nc.scalar.activation(rk[:, :, :], rk[:, :, :], ACT.Exp, scale=-0.5).then_inc(rk_done, 1)

                def probabilities():
                    act.wait_ge(pn_done, b + 1)
                    wait(act, inv_done, 2 * b)
                    nc.scalar.activation(pnew[:, :], pnew[:, :], ACT.Exp).then_inc(pr_done, 1)
                    act.wait_ge(sc_done, 2 * b + 2)
                    wait(act, weighted, b)
                    nc.scalar.activation(pr[:, :, :], sc[:, :, :], ACT.Exp).then_inc(pr_done, 1)

                return {0: key_factor, 7: probabilities}

            def latents_hi(b, p):
                act.wait_ge(ring_landed[p % RING], 32 * (PAGES // RING) * b + 32 * (p // RING + 1))
                wait(act, expanded, PAGES * b + (p - 1))
                nc.scalar.activation(lat_hi[:, p % 2, :, :], lat_t[:, p % RING, :, :], ACT.Copy) \
                  .then_inc(hi_done, 1)

            def pages(b, u, steps):
                for p in range(PAGES):
                    e = p % 2
                    if p + 1 < PAGES:
                        latents_hi(b, p + 1)
                    elif not isinstance(b, int) or b + 1 < NS:
                        latents_hi(b + 1, 0)
                    act.wait_ge(expanded, PAGES * b + (p + 1))
                    wait(act, ssum, PAGES * b + (p - 1))
                    nc.scalar.activation(sq[:, e, :], KEYS[e], ACT.Square).then_inc(squared, 1)
                    run(steps, p)

            act.wait_ge(wk_landed, 32)
            nc.scalar.activation(wuk_hi[:, :, :], wuk[:, :, :], ACT.Copy).then_inc(wuk_split, 1)
            latents_hi(0, 0)
            sequences(act, pages, tail)

        @block.vector
        def _(dve):
            def tail(b, u):
                def finish_scores():
                    dve.wait_ge(rk_done, b + 1)
                    dve.wait_ge(scored, PAGES * b + PAGES)
                    wait(dve, pr_done, 2 * b)
                    nc.vector.tensor_tensor(sc[:, :, :], SC[u].rearrange("p (a h) -> p a h", a=PAGES),
                                            rk[:, :, :], ALU.mult).then_inc(sc_done, 1)
                    dve.wait_ge(sc_done, 2 * b + 1)
                    nc.vector.tensor_reduce(mx[:, :], sc[:, :, :].rearrange("p a h -> p h a"), AX.X, ALU.max) \
                      .then_inc(mx_done, 1)
                    dve.wait_ge(mx_done, 2 * b + 1)
                    nc.vector.tensor_tensor(mx[:, :], mx[:, :],
                                            m.snew[:, bass.ds(b, 1), :].rearrange("p a h -> p (a h)"),
                                            ALU.max).then_inc(mx_done, 1)

                def top_score():
                    dve.wait_ge(mx_turned, b + 1)
                    nc.vector.tensor_reduce(top[:, :], SMALL[0:H, 0:P], AX.X, ALU.max).then_inc(top_done, 1)
                    dve.wait_ge(top_done, b + 1)
                    nc.vector.tensor_scalar(diag[:, :], c.ident[0:H, 0:H], top[:, 0:1], None, op0=ALU.mult) \
                      .then_inc(diag_done, 1)

                def less_max():
                    dve.wait_ge(m_summed, b + 1)
                    nc.vector.tensor_copy(mall[:, :], SMALL[:, P:P + H]).then_inc(m_done, 1)
                    dve.wait_ge(m_done, b + 1)
                    nc.vector.tensor_tensor(pnew[:, :], m.snew[:, bass.ds(b, 1), :].rearrange("p a h -> p (a h)"),
                                            mall[:, :], ALU.subtract).then_inc(pn_done, 1)
                    nc.vector.tensor_tensor(sc[:, :, :], sc[:, :, :],
                                            mall[:, :].unsqueeze(1).broadcast_to([P, PAGES, H]),
                                            ALU.subtract).then_inc(sc_done, 1)

                def page_sums():
                    dve.wait_ge(pr_done, 2 * b + 2)
                    nc.vector.tensor_reduce(lsum[:, :], pr[:, :, :].rearrange("p a h -> p h a"), AX.X, ALU.add) \
                      .then_inc(l_done, 1)

                def take_sums():
                    dve.wait_ge(weighted, b + 1)
                    wait(dve, acc_turned, b)
                    nc.vector.tensor_copy(acc[:, :], c.ps[0:H, 5, 0:KVL]).then_inc(acc_taken, 1)

                def divide():
                    dve.wait_ge(l_summed, b + 1)
                    nc.vector.tensor_tensor(ltot[:, :], SMALL[:, 2 * P:2 * P + H], pnew[:, :], ALU.add) \
                      .then_inc(inv_done, 1)
                    dve.wait_ge(inv_done, 2 * b + 1)
                    for k in range(NKV):
                        nc.vector.tensor_tensor(part[:, k, :], pnew[:, :],
                                                ckvs[:, bass.ds(b, 1), k:k + 1].rearrange("p a k -> p (a k)")
                                                .broadcast_to([P, H]), ALU.mult).then_inc(part_done, 1)
                    nc.vector.reciprocal(ltot[:, :], ltot[:, :]).then_inc(inv_done, 1)
                    dve.wait_ge(acc_turned, b + 1)
                    dve.wait_ge(part_done, 2 * NKV * b + NKV)
                    for k in range(NKV):
                        nc.vector.tensor_tensor(part[:, k, :], ACC[:, k * H:(k + 1) * H], part[:, k, :],
                                                ALU.add).then_inc(part_done, 1)
                    dve.wait_ge(part_done, 2 * NKV * b + 2 * NKV)
                    dve.wait_ge(inv_done, 2 * b + 2)
                    for k in range(NKV):
                        nc.vector.tensor_tensor(m.accn[:, k, :, bass.ds(b, 1)].rearrange("p h a -> p (h a)"),
                                                part[:, k, :], ltot[:, :], ALU.mult).then_inc(acc_done, 1)

                return {2: finish_scores, 4: top_score, 6: less_max, 8: page_sums, 12: take_sums, 14: divide}

            def pages(b, u, steps):
                for p in range(PAGES):
                    dve.wait_ge(squared, PAGES * b + (p + 1))
                    if p == 0:
                        wait(dve, rk_logged, b - 1)
                    nc.vector.tensor_reduce(ss[:, u, p, :], sq[:, p % 2, :].rearrange("p (h d) -> p h d", h=H),
                                            AX.X, ALU.add).then_inc(ssum, 1)
                    run(steps, p)
                dve.wait_ge(kk_done, b + 1)
                nc.vector.tensor_reduce(kks[:, u, :], kk[:, :, :], AX.X, ALU.add).then_inc(kks_done, 1)
                dve.wait_ge(kks_done, b + 1)
                dve.wait_ge(ssum, PAGES * b + PAGES)
                nc.vector.tensor_tensor(ss[:, u, :, :], ss[:, u, :, :],
                                        kks[:, u, :].unsqueeze(2).broadcast_to([P, PAGES, H]),
                                        ALU.add).then_inc(ss_done, 1)

            dve.wait_ge(q_summed, 1)
            for k in range(NKV):
                nc.vector.tensor_copy(qlat[:, k, :, :].rearrange("p n h -> p h n"),
                                      c.ps[:, 4 + k, 0:H * NS].rearrange("p (h n) -> p h n", h=H)) \
                  .then_inc(q_ready, 1)
                nc.vector.tensor_copy(ckvs[:, :, k], m.ckv[:, k, SEQ:T])
            nc.vector.tensor_copy(qpe[:, :, :].rearrange("p n h -> p h n"), m.qs[NOPE:QK, :, :]) \
              .then_inc(q_ready, 1)
            sequences(dve, pages, tail)


def mla_gated_values(c, m, o_tok):
    nc = c.nc
    with Stage(c) as st:
        summed = st.sem("summed")
        gated = st.sem("gated")
        s_summed = st.sem("s_summed")
        block = st.block()
        rounds = [(f, b) for f in range(NG) for b in range(QT // 4)]

        @block.tensor
        def _(pe):
            for n, (f, b) in enumerate(rounds):
                wait(pe, gated, n - 1)
                for t in range(4):
                    mm = nc.tensor.transpose(c.ps[:, n % 2, t * P:(t + 1) * P],
                                             o_tok[:, 4 * b + t, f * P:(f + 1) * P], c.ident[:, :])
                mm.then_inc(summed, 1)
            for f in range(NG):
                for k in range(NKV):
                    mm = nc.tensor.matmul(c.ps[:, 2, f * 2 * NS:(f + 1) * 2 * NS], m.wuv[:, k, f * P:(f + 1) * P],
                                          m.accn[:, k, 2 * f:2 * f + 2, :].rearrange("p h n -> p (h n)"),
                                          start=(k == 0), stop=(k == NKV - 1))
            mm.then_inc(s_summed, 1)

        @block.vector
        def _(dve):
            for n, (f, b) in enumerate(rounds):
                dve.wait_ge(summed, n + 1)
                g = m.gate[:, f, b * 512:(b + 1) * 512]
                nc.vector.tensor_tensor(g, c.ps[:, n % 2, :], g, ALU.mult).then_inc(gated, 1)
            dve.wait_ge(s_summed, 1)
            for f in range(NG):
                for e in range(2):
                    rows = slice(e * DV, (e + 1) * DV)
                    lo = f * 2 * NS + e * NS
                    nc.vector.tensor_tensor(m.gate[rows, f, SEQ:T], c.ps[rows, 2, lo:lo + NS],
                                            m.gate[rows, f, SEQ:T], ALU.mult)


def mla_layer(c, layer, j):
    with Stage(c) as st:
        z = st.sb("latents", [P, NQL + NKV + NG, T])
        streamed_projection(c, c.dram["w_mla_in"][j], NQL + NKV + NG, KD, c.h,
                            lambda b, psum: c.nc.vector.tensor_copy(block_of(z, b), psum))
        m = Mla(st, z)
        mla_latents(c, m, j)
        o_tok = c.h[:, :, :].rearrange("p k t -> p (k t)")[:, 0:QT * H * DV].rearrange("p (q n) -> p q n", q=QT)
        mla_prompt_attention(c, m, j, o_tok)
        mla_sample_attention(c, m, j)
        mla_gated_values(c, m, o_tok)
        output_projection(c, c.dram["w_mla_out"][j], NG, m.gate, following(layer))



CHUNKS = SEQ // P
KINDS = ("f", "q", "i", "g")


def heads_in_pairs(engine, head):
    head(0, 0, 1)
    with engine.Fori(0, (H - 2) // 2) as i:
        head(2 * i + 1, 1, 2 * i + 2)
        head(2 * i + 2, 0, 2 * i + 3)
    head(H - 1, 1, None)


def hgrn_lower_bound(c, layer, lb, olb):
    nc, dram = c.nc, c.dram
    with Stage(c) as st:
        raw = st.sb("bounds", [P, 4, KD])
        top = st.sb("top", [P, KD])
        tot = st.sb("tot", [P, KD])
        inv = st.sb("inv", [P, KD])
        loads = st.sem("loads")
        steps = st.sem("steps")
        exped = st.sem("exped")
        block = st.block()

        @block.sync
        def _(sp):
            sp.dma_start(raw[:, :, :], dram["hgrn_bounds"]).then_inc(loads, 16)

        @block.vector
        def _(dve):
            n = 0

            def step(ins):
                nonlocal n
                n += 1
                ins.then_inc(steps, 1)
                dve.wait_ge(steps, n)

            dve.wait_ge(loads, 16)
            step(nc.vector.tensor_reduce(top[:, :], raw[:, :, :].rearrange("p l k -> p k l"), AX.X, ALU.max))
            step(nc.vector.tensor_tensor(raw[:, :, :], raw[:, :, :],
                                         top[:, :].unsqueeze(1).broadcast_to([P, 4, KD]), ALU.subtract))
            dve.wait_ge(exped, 1)
            step(nc.vector.tensor_reduce(tot[:, :], raw[:, :, :].rearrange("p l k -> p k l"), AX.X, ALU.add))
            step(nc.vector.reciprocal(inv[:, :], tot[:, :]))
            step(nc.vector.tensor_reduce(tot[:, :], raw[:, 1:layer + 1, :].rearrange("p l k -> p k l"),
                                         AX.X, ALU.add))
            step(nc.vector.tensor_tensor(lb[:, :], tot[:, :], inv[:, :], ALU.mult))
            step(nc.vector.tensor_scalar(olb[:, :], lb[:, :], -1.0, 1.0, op0=ALU.mult, op1=ALU.add))

        @block.scalar
        def _(act):
            load_ln_exp(nc)
            act.wait_ge(steps, 2)
            nc.scalar.activation(raw[:, :, :], raw[:, :, :], ACT.Exp).then_inc(exped, 1)


def hgrn_heads(c, out, lb, olb):
    nc, dram = c.nc, c.dram
    NU = 12
    QSCALE = P ** -0.5
    with Stage(c) as st:
        ws = st.sb("w_slots", [P, 4, KD, P])
        raw = st.sb("raw", [P, 3, T])
        sg = st.sb("decay", [P, T])
        k = st.sb("k", [P, T])
        q = st.sb("q", [P, T])
        gs = st.sb("gate", [P, 2, T])
        gl = st.sb("log_decay", [P, T])
        b = st.sb("decay_sums", [P, SEQ])
        o = st.sb("o", [P, T])
        dd = st.sb("differences", [P, 2, T])
        z = st.sb("factors", [P, 2, T])
        v = st.sb("v", [P, 2, QT + 1, P])
        att = st.sb("att", [P, CHUNKS, P])
        states = st.sb("states", [P, CHUNKS, P])
        last = st.sb("chunk_decay", [P, CHUNKS])
        masks = st.sb("masks", [P, LEVELS + 1, P], mybir.dt.uint8)
        sel = st.sb("sel", [NS, NS, P])
        sin = st.sb("sample_in", [P, NS, P])
        ns = st.sb("sample_out", [P, NS, P])
        gn = st.sb("g_norm", [P, 1])
        kbt = dd[:, 1, 0:SEQ].rearrange("p (a n) -> p a n", a=CHUNKS)
        rs = z[:, 0, :]

        loads = st.sem("loads")
        w_landed = [st.sem(f"w_landed_{x}") for x in KINDS]
        sin_landed = st.sem("sin_landed")
        masks_done = st.sem("masks_done")
        unit_summed = st.sem("unit_summed")
        unit_drained = st.sem("unit_drained")
        acts = st.sem("acts")
        a_done = st.sem("a_done")
        k_done = st.sem("k_done")
        ln_done = st.sem("ln_done")
        scanned = st.sem("scanned")
        d_done = st.sem("d_done")
        exped = st.sem("exped")
        z_done = st.sem("z_done")
        zp_done = st.sem("zp_done")
        att_summed = st.sem("att_summed")
        att_copied = st.sem("att_copied")
        kb_turned = st.sem("kb_turned")
        kbt_done = st.sem("kbt_done")
        ds_summed = st.sem("ds_summed")
        state_done = st.sem("state_done")
        o_summed = st.sem("o_summed")
        o_done = st.sem("o_done")
        vb_summed = st.sem("vb_summed")
        sin_scaled = st.sem("sin_scaled")
        outer = st.sem("outer")
        ns_done = st.sem("ns_done")
        os_summed = st.sem("os_summed")
        os_done = st.sem("os_done")
        sqo_done = st.sem("sqo_done")
        ss_summed = st.sem("ss_summed")
        rs_logged = st.sem("rs_logged")
        rs_done = st.sem("rs_done")
        normed = st.sem("normed")
        og_done = st.sem("og_done")
        state_out = st.sem("state_out")
        ns_out = st.sem("ns_out")
        block = st.block()
        PAIR = [c.ps[:, 0:2, :].rearrange("p a n -> p (a n)").rearrange("p (a n) -> p a n", a=CHUNKS),
                c.ps[:, 2:4, :].rearrange("p a n -> p (a n)").rearrange("p (a n) -> p a n", a=CHUNKS)]

        def halves(buf, half):
            return buf.rearrange("p (n e h) -> p n e h", e=2, h=half)

        def chunks(buf):
            return buf.rearrange("p (a n) -> p a n", a=CHUNKS)

        @block.sync
        def _(sp):
            sp.dma_start(att[:, :, :], dram["hgrn_masks"]).then_inc(loads, 16)
            sp.dma_start(sel[:, :, :], dram["sel"]).then_inc(loads, 16)
            sp.dma_start(gn[:, :], dram["hgrn_g_norm"]).then_inc(loads, 16)

            def weights(h, first=False):
                for n in range(4):
                    if not first:
                        sp.wait_ge(unit_summed, NU * h + (3 * n + 3 - NU))
                    sp.dma_start(ws[:, n, :, :], dram["w_hgrn"][n][bass.ds(h, 1)].rearrange("a p k m -> p (a k) m")) \
                      .then_inc(w_landed[n], 16)

            def head(h, following):
                if following is not None:
                    weights(following)
                sin_before, states_now = 16 * h, CHUNKS * h + CHUNKS
                if not isinstance(h, int):
                    sin_before, states_now = sp.snap(sin_before), sp.snap(states_now)
                wait(sp, sin_landed, sin_before)
                wait(sp, ns_done, h)
                sp.dma_start(sin[:, :, :], dram["state_hgrn"][bass.ds(h, 1)].rearrange("a k n v -> k (a n) v")) \
                  .then_inc(sin_landed, 16)
                sp.wait_ge(ns_done, h + 1)
                sp.dma_start(dram["o_hgrn_s"][bass.ds(h, 1)].rearrange("a k n v -> k (a n) v"), ns[:, :, :]) \
                  .then_inc(ns_out, 16)
                sp.wait_ge(state_done, states_now)
                sp.dma_start(dram["o_hgrn_p"][bass.ds(h, 1)].rearrange("a k v -> k (a v)"),
                             states[:, CHUNKS - 1, :]).then_inc(state_out, 16)

            weights(0, first=True)
            head(0, 1)
            with sp.Fori(1, H - 1) as h:
                head(h, h + 1)
            head(H - 1, None)
            sp.wait_ge(ns_out, 16 * H)
            sp.wait_ge(state_out, 16 * H)

        @block.tensor
        def _(pe):
            def unit(h, n):
                kind, t = divmod(n, 3)
                bank = c.ps[:, 4 + n % 2, :]
                wait(pe, unit_drained, NU * h + (n - 1))
                if t == 0:
                    pe.wait_ge(w_landed[kind], 16 * h + 16)
                if KINDS[kind] != "i":
                    for kk in range(KD):
                        mm = nc.tensor.matmul(bank[:, 0:TT], ws[:, kind, kk, :], c.h[:, kk, t * TT:(t + 1) * TT],
                                              start=(kk == 0), stop=(kk == KD - 1))
                else:
                    for e in range(3):
                        tt = 3 * t + e
                        rows = P if tt < QT else NS
                        for kk in range(KD):
                            mm = nc.tensor.matmul(bank[0:rows, e * P:(e + 1) * P],
                                                  c.h[:, kk, tt * P:tt * P + rows], ws[:, kind, kk, :],
                                                  start=(kk == 0), stop=(kk == KD - 1))
                mm.then_inc(unit_summed, 1)

            def head(h, u, following):
                units = iter(range(NU) if following is not None else [])

                def fill(count=1):
                    for _ in range(count):
                        n = next(units, None)
                        if n is not None:
                            unit(following, n)

                def pair(n):
                    return PAIR[(n + u) % 2]

                fill()
                wait(pe, state_done, CHUNKS * h)
                pe.wait_ge(acts, 4 * h + 3)
                pe.wait_ge(k_done, h + 1)
                for a in range(CHUNKS):
                    cols = slice(a * P, (a + 1) * P)
                    mm = nc.tensor.matmul(pair(0)[:, a, :], k[:, cols], q[:, cols], start=True, stop=True)
                mm.then_inc(att_summed, 1)
                wait(pe, rs_logged, NT * h)
                for n in range(NS):
                    mm = nc.tensor.matmul(c.ps[:, 6 + n // 4, (n % 4) * P:(n % 4 + 1) * P], sel[:, n, :],
                                          v[0:NS, u, QT, :], start=True, stop=True)
                mm.then_inc(vb_summed, 1)
                fill()
                for l in range(LEVELS):
                    n = l + 1
                    if n == 1:
                        wait(pe, o_done, h)
                    else:
                        pe.wait_ge(att_copied, 8 * h + (n - 1))
                    pe.wait_ge(z_done, 8 * h + (l + 1))
                    pe.wait_ge(zp_done, 8 * h + (l + 1))
                    for a in range(CHUNKS):
                        zc = z[:, l % 2, a * P:(a + 1) * P]
                        mm = nc.tensor.matmul(pair(n)[:, a, :], zc, zc, start=True, stop=True)
                    mm.then_inc(att_summed, 1)
                    if l:
                        fill()
                    if l == 4:
                        pe.wait_ge(ns_done, h + 1)
                        pe.wait_ge(outer, 2 * h + 2)
                        for n in range(NS):
                            mm = nc.tensor.matmul(c.ps[:, 6, n:n + 1], ns[:, n, :], q[:, SEQ + n:SEQ + n + 1],
                                                  start=True, stop=True)
                        mm.then_inc(os_summed, 1)
                pe.wait_ge(zp_done, 8 * h + 8)
                pe.wait_ge(att_copied, 8 * h + 7)
                for a in range(CHUNKS):
                    mm = nc.tensor.transpose(pair(8)[:, a, :], z[:, 1, a * P:(a + 1) * P], c.ident[:, :])
                mm.then_inc(kb_turned, 1)
                fill()
                pe.wait_ge(kbt_done, h + 1)
                pe.wait_ge(att_copied, 8 * h + 8)
                for a in range(CHUNKS):
                    mm = nc.tensor.matmul(pair(9)[:, a, :], kbt[:, a, :], v[:, u, a, :], start=True, stop=True)
                mm.then_inc(ds_summed, 1)
                fill(2)
                pe.wait_ge(z_done, 8 * h + 8)
                pe.wait_ge(state_done, CHUNKS * h + (CHUNKS - 1))
                for a in range(CHUNKS):
                    mm = nc.tensor.matmul(pair(10)[:, a, :], v[:, u, a, :], att[:, a, :], start=True, stop=(a == 0))
                    if a:
                        mm = nc.tensor.matmul(pair(10)[:, a, :], states[:, a - 1, :], dd[:, 0, a * P:(a + 1) * P],
                                              start=False, stop=True)
                mm.then_inc(o_summed, 1)
                fill()
                pe.wait_ge(sqo_done, h + 1)
                pe.wait_ge(os_done, h + 1)
                for t, cols in tiles():
                    if t == 2:
                        pe.wait_ge(rs_logged, NT * h + 1)
                    nc.tensor.matmul(c.ps[:, 6 + t % 2, 0:TT], c.ones[:, :], gl[:, cols],
                                     start=True, stop=True).then_inc(ss_summed, 1)

            pe.wait_ge(loads, 48)
            for n in range(NU):
                unit(0, n)
            heads_in_pairs(pe, head)

        @block.scalar
        def _(act):
            def drain_unit(h, u, n):
                kind, t = divmod(n, 3)
                bank = c.ps[:, 4 + n % 2, :]
                act.wait_ge(unit_summed, NU * h + (n + 1))
                if KINDS[kind] != "i":
                    place = {"f": 0, "q": 1, "g": 2}[KINDS[kind]]
                    nc.scalar.activation(raw[:, place, t * TT:(t + 1) * TT], bank[:, 0:TT], ACT.Copy) \
                      .then_inc(unit_drained, 1)
                    return
                if t == 2:
                    nc.scalar.activation(v[0:NS, u, QT, :], bank[0:NS, 2 * P:3 * P], ACT.Copy)
                full = 3 if t < 2 else 2
                nc.scalar.activation(v[:, u, 3 * t:3 * t + full, :],
                                     bank[:, 0:full * P].rearrange("p (a n) -> p a n", a=full), ACT.Copy) \
                  .then_inc(unit_drained, 1)

            def level_exp(h, l):
                half = P >> (l + 1)
                act.wait_ge(d_done, 8 * h + (l + 1))
                both = halves(dd[:, l % 2, 0:SEQ], half)
                nc.scalar.activation(both[:, :, 1, :], both[:, :, 1, :], ACT.Exp).then_inc(exped, 1)
                nc.scalar.activation(both[:, :, 0, :], both[:, :, 0, :], ACT.Exp, scale=-1.0).then_inc(exped, 1)

            def forget_key_query(h):
                act.wait_ge(unit_drained, NU * h + 2 * NT)
                wait(act, sin_scaled, h)
                wait(act, zp_done, 8 * h)
                wait(act, outer, 2 * h)
                nc.scalar.activation(sg[:, :], raw[:, 0, :], ACT.Sigmoid).then_inc(acts, 1)
                nc.scalar.activation(k[:, :], raw[:, 0, :], ACT.Sigmoid, scale=-1.0).then_inc(acts, 1)
                wait(act, z_done, 8 * h)
                wait(act, os_summed, h)
                nc.scalar.activation(q[:, :], raw[:, 1, :], ACT.Silu).then_inc(acts, 1)

            def gate(h, u):
                act.wait_ge(unit_drained, NU * h + NU)
                wait(act, og_done, h - 1)
                nc.scalar.activation(gs[:, u, :], raw[:, 2, :], ACT.Silu).then_inc(acts, 1)
                load_ln_exp(nc)
                act.wait_ge(acts, 4 * h + 4)

            def head(h, u, following):
                units = iter(range(NU) if following is not None else [])

                def fill(count=1):
                    for _ in range(count):
                        n = next(units, None)
                        if n is not None:
                            drain_unit(following, 1 - u, n)

                act.wait_ge(a_done, h + 1)
                nc.scalar.activation(gl[:, 0:SEQ], sg[:, 0:SEQ], ACT.Ln).then_inc(ln_done, 1)
                wait(act, og_done, h)
                level_exp(h, 0)
                for l in range(LEVELS):
                    if l + 1 < LEVELS:
                        level_exp(h, l + 1)
                    else:
                        act.wait_ge(d_done, 8 * h + 8)
                        nc.scalar.activation(dd[:, 1, 0:SEQ], dd[:, 1, 0:SEQ], ACT.Exp, scale=-1.0) \
                          .then_inc(exped, 1)
                    fill(1 if l else 2)
                act.wait_ge(z_done, 8 * h + 7)
                act.wait_ge(zp_done, 8 * h + 7)
                nc.scalar.activation(dd[:, 0, 0:SEQ], b[:, :], ACT.Exp).then_inc(exped, 1)
                nc.scalar.activation(last[:, :], chunks(b[:, :])[:, :, P - 1], ACT.Exp).then_inc(exped, 1)
                act.wait_ge(os_summed, h + 1)
                nc.scalar.activation(o[:, SEQ:T], c.ps[:, 6, 0:NS], ACT.Copy, scale=QSCALE).then_inc(os_done, 1)
                act.wait_ge(kb_turned, h + 1)
                nc.scalar.activation(kbt, PAIR[u % 2], ACT.Copy).then_inc(kbt_done, 1)
                fill(3)
                act.wait_ge(o_summed, h + 1)
                nc.scalar.activation(chunks(o[:, 0:SEQ]), PAIR[u % 2], ACT.Copy, scale=QSCALE).then_inc(o_done, 1)
                act.wait_ge(o_done, h + 1)
                act.wait_ge(os_done, h + 1)
                nc.scalar.activation(gl[:, :], o[:, :], ACT.Square).then_inc(sqo_done, 1)
                if following is not None:
                    forget_key_query(following)
                    fill()
                    gate(following, 1 - u)
                for t, cols in tiles():
                    act.wait_ge(ss_summed, NT * h + (t + 1))
                    nc.scalar.activation(rs[:, cols], c.ps[:, 6 + t % 2, 0:TT], ACT.Ln, scale=1.0 / P,
                                         bias=c.eps()).then_inc(rs_logged, 1)
                act.wait_ge(rs_logged, NT * h + NT)
                nc.scalar.activation(rs, rs, ACT.Exp, scale=-0.5).then_inc(rs_done, 1)

            for n in range(NU):
                drain_unit(0, 0, n)
            forget_key_query(0)
            gate(0, 0)
            heads_in_pairs(act, head)

        @block.gpsimd
        def _(pool):
            def head(h, u, following):
                pool.wait_ge(sin_landed, 16 * h + 16)
                pool.wait_ge(a_done, h + 1)
                nc.gpsimd.tensor_tensor(sin[:, :, :], sin[:, :, :],
                                        sg[:, SEQ:T].unsqueeze(2).broadcast_to([P, NS, P]),
                                        ALU.mult).then_inc(sin_scaled, 1)
                for l in range(LEVELS):
                    if l == 2:
                        pool.wait_ge(outer, 2 * h + 2)
                        pool.wait_ge(sin_scaled, h + 1)
                        nc.gpsimd.tensor_tensor(ns[:, :, :], ns[:, :, :], sin[:, :, :], ALU.add) \
                          .then_inc(ns_done, 1)
                    half = P >> (l + 1)
                    pool.wait_ge(exped, 17 * h + (2 * l + 2))
                    if l >= 2:
                        pool.wait_ge(att_summed, 8 * h + l)
                    nc.gpsimd.tensor_tensor(halves(z[:, l % 2, 0:SEQ], half)[:, :, 0, :],
                                            halves(dd[:, l % 2, 0:SEQ], half)[:, :, 0, :],
                                            halves(k[:, 0:SEQ], half)[:, :, 0, :], ALU.mult).then_inc(zp_done, 1)
                pool.wait_ge(exped, 17 * h + 15)
                pool.wait_ge(att_summed, 8 * h + 7)
                nc.gpsimd.tensor_tensor(z[:, 1, 0:SEQ], dd[:, 1, 0:SEQ], k[:, 0:SEQ], ALU.mult) \
                  .then_inc(zp_done, 1)

            heads_in_pairs(pool, head)

        @block.vector
        def _(dve):
            def decay_and_key(h):
                dve.wait_ge(acts, 4 * h + 1)
                nc.vector.tensor_scalar(sg[:, :], sg[:, :], olb[:, bass.ds(h, 1)], lb[:, bass.ds(h, 1)],
                                        op0=ALU.mult, op1=ALU.add).then_inc(a_done, 1)
                dve.wait_ge(acts, 4 * h + 2)
                nc.vector.tensor_scalar(k[:, :], k[:, :], olb[:, bass.ds(h, 1)], None, op0=ALU.mult) \
                  .then_inc(k_done, 1)

            def head(h, u, following):
                dve.wait_ge(ln_done, h + 1)
                for a in range(CHUNKS):
                    cols = slice(a * P, (a + 1) * P)
                    nc.vector.tensor_tensor_scan(b[:, cols], c.ones[:, :], gl[:, cols], 0.0,
                                                 op0=ALU.mult, op1=ALU.add).then_inc(scanned, 1)
                dve.wait_ge(scanned, CHUNKS * h + CHUNKS)

                def difference(l):
                    half = P >> (l + 1)
                    if l >= 2:
                        dve.wait_ge(z_done, 8 * h + (l - 1))
                        dve.wait_ge(zp_done, 8 * h + (l - 1))
                    ref = halves(b[:, :], half)[:, :, 0:1, half - 1:half]
                    nc.vector.tensor_tensor(halves(dd[:, l % 2, 0:SEQ], half), halves(b[:, :], half),
                                            ref.broadcast_to([P, SEQ // (2 * half), 2, half]), ALU.subtract) \
                      .then_inc(d_done, 1)

                def upper(l):
                    half = P >> (l + 1)
                    dve.wait_ge(exped, 17 * h + (2 * l + 1))
                    dve.wait_ge(acts, 4 * h + 3)
                    if l >= 2:
                        dve.wait_ge(att_summed, 8 * h + l)
                    nc.vector.tensor_tensor(halves(z[:, l % 2, 0:SEQ], half)[:, :, 1, :],
                                            halves(dd[:, l % 2, 0:SEQ], half)[:, :, 1, :],
                                            halves(q[:, 0:SEQ], half)[:, :, 1, :], ALU.mult).then_inc(z_done, 1)

                def pick(n):
                    dve.wait_ge(masks_done, 2)
                    if n:
                        dve.wait_ge(att_copied, 8 * h + n)
                    dve.wait_ge(att_summed, 8 * h + (n + 1))
                    nc.vector.copy_predicated(att[:, :, :], masks[:, n:n + 1, :].broadcast_to([P, CHUNKS, P]),
                                              PAIR[(n + u) % 2]).then_inc(att_copied, 1)

                dve.wait_ge(scanned, 8 * h + 1)
                difference(0)
                pick(0)
                dve.wait_ge(k_done, h + 1)
                dve.wait_ge(vb_summed, h + 1)
                wait(dve, ns_out, 16 * h)
                for e in range(2):
                    nc.vector.tensor_tensor(ns[:, 4 * e:4 * e + 4, :],
                                            c.ps[:, 6 + e, :].rearrange("p (a n) -> p a n", a=4),
                                            k[:, SEQ + 4 * e:SEQ + 4 * e + 4].unsqueeze(2)
                                            .broadcast_to([P, 4, P]), ALU.mult).then_inc(outer, 1)
                for l in range(LEVELS):
                    if l + 1 < LEVELS:
                        difference(l + 1)
                    else:
                        dve.wait_ge(z_done, 8 * h + 6)
                        dve.wait_ge(zp_done, 8 * h + 6)
                        nc.vector.tensor_tensor(chunks(dd[:, 1, 0:SEQ]), chunks(b[:, :]),
                                                chunks(b[:, :])[:, :, P - 1:P].broadcast_to([P, CHUNKS, P]),
                                                ALU.subtract).then_inc(d_done, 1)
                    dve.wait_ge(scanned, 8 * h + (l + 1))
                    upper(l)
                    if l:
                        pick(l)
                pick(LEVELS)
                dve.wait_ge(exped, 17 * h + 16)
                nc.vector.tensor_tensor(dd[:, 0, 0:SEQ], dd[:, 0, 0:SEQ], q[:, 0:SEQ], ALU.mult) \
                  .then_inc(z_done, 1)
                dve.wait_ge(ds_summed, h + 1)
                dve.wait_ge(exped, 17 * h + 17)
                wait(dve, state_out, 16 * h)
                pair = PAIR[(9 + u) % 2]
                nc.vector.tensor_copy(states[:, 0, :], pair[:, 0, :]).then_inc(state_done, 1)
                for a in range(1, CHUNKS):
                    dve.wait_ge(state_done, CHUNKS * h + a)
                    nc.vector.scalar_tensor_tensor(states[:, a, :], states[:, a - 1, :], last[:, a:a + 1],
                                                   pair[:, a, :], op0=ALU.mult, op1=ALU.add) \
                      .then_inc(state_done, 1)
                if following is not None:
                    decay_and_key(following)
                dve.wait_ge(rs_done, h + 1)
                nc.vector.scalar_tensor_tensor(o[:, :], o[:, :], gn[:, 0:1], rs, op0=ALU.mult, op1=ALU.mult) \
                  .then_inc(normed, 1)
                dve.wait_ge(normed, h + 1)
                dve.wait_ge(acts, 4 * h + 4)
                nc.vector.tensor_tensor(out[:, bass.ds(h, 1), :].rearrange("p a t -> p (a t)"), o[:, :], gs[:, u, :],
                                        ALU.mult).then_inc(og_done, 1)

            dve.wait_ge(loads, 48)
            nc.vector.tensor_copy(masks[:, :, :], att[:, :, :]).then_inc(masks_done, 1)
            dve.wait_ge(masks_done, 1)
            nc.vector.memset(att[:, :, :], 0.0).then_inc(masks_done, 1)
            decay_and_key(0)
            heads_in_pairs(dve, head)


def hgrn_layer(c, layer):
    with Stage(c) as st:
        out = st.sb("heads_out", [P, KD, T])
        lb = st.sb("lb", [P, KD])
        olb = st.sb("one_less_lb", [P, KD])
        hgrn_lower_bound(c, layer, lb, olb)
        hgrn_heads(c, out, lb, olb)
        output_projection(c, c.dram["w_hgrn_out"], KD, out, following(layer))


CONV = 4


def rglru_decay_rate(c, m8, p8):
    nc, dram = c.nc, c.dram
    with Stage(c) as st:
        lam = st.sb("lam", [P, KD])
        neg = st.sb("neg", [P, KD])
        z = st.sb("z", [P, KD])
        s = st.sb("s", [P, KD])
        s2 = st.sb("s2", [P, KD])
        p = st.sb("p", [P, KD])
        loads = st.sem("loads")
        steps = st.sem("steps")
        exped = st.sem("exped")
        block = st.block()

        @block.sync
        def _(sp):
            sp.dma_start(lam[:, :], dram["rg_lam"]).then_inc(loads, 16)

        @block.scalar
        def _(act):
            load_ln_exp(nc)
            act.wait_ge(steps, 2)
            nc.scalar.activation(z[:, :], z[:, :], ACT.Exp, scale=-1.0).then_inc(exped, 1)

        @block.vector
        def _(dve):
            n = 0

            def step(ins):
                nonlocal n
                n += 1
                ins.then_inc(steps, 1)
                dve.wait_ge(steps, n)

            dve.wait_ge(loads, 16)
            step(nc.vector.tensor_scalar(neg[:, :], lam[:, :], -1.0, None, op0=ALU.mult))
            step(nc.vector.tensor_tensor(z[:, :], neg[:, :], lam[:, :], ALU.max))
            dve.wait_ge(exped, 1)
            step(nc.vector.tensor_scalar(s[:, :], z[:, :], 2.0, None, op0=ALU.add))
            step(nc.vector.reciprocal(s[:, :], s[:, :]))
            step(nc.vector.tensor_tensor(s[:, :], s[:, :], z[:, :], ALU.mult))
            step(nc.vector.tensor_tensor(s2[:, :], s[:, :], s[:, :], ALU.mult))
            step(nc.vector.tensor_scalar(p[:, :], s2[:, :], 1.0 / 17, 1.0 / 15, op0=ALU.mult, op1=ALU.add))
            for d in (13, 11, 9, 7, 5, 3, 1):
                step(nc.vector.tensor_tensor(p[:, :], p[:, :], s2[:, :], ALU.mult))
                step(nc.vector.tensor_scalar(p[:, :], p[:, :], 1.0 / d, None, op0=ALU.add))
            step(nc.vector.tensor_tensor(p[:, :], p[:, :], s[:, :], ALU.mult))
            step(nc.vector.tensor_scalar(neg[:, :], neg[:, :], 0.0, None, op0=ALU.max))
            step(nc.vector.scalar_tensor_tensor(p[:, :], p[:, :], 2.0, neg[:, :], op0=ALU.mult, op1=ALU.add))
            step(nc.vector.tensor_scalar(m8[:, :], p[:, :], -8.0, None, op0=ALU.mult))
            step(nc.vector.tensor_scalar(p8[:, :], p[:, :], 8.0, None, op0=ALU.mult))


def rglru_heads(c, out, m8, p8):
    nc, dram = c.nc, c.dram
    NU = 6
    PRE = CONV - 1
    with Stage(c) as st:
        ws = st.sb("w_slots", [P, 2, KD, P])
        w_hi = st.sb("w_hi", [P, 2, KD, P], F32R)
        w_lo = st.sb("w_lo", [P, 2, KD, P], F32R)
        h_hi = st.sb("normed_hi", [P, KD, T], F32R)
        h_lo = st.sb("normed_lo", [P, KD, T], F32R)
        wg = st.sb("w_gates", [P, 2, 2, P])
        xb = st.sb("xb", [P, 2, PRE + T])
        graw = st.sb("gate", [P, 2, T])
        y = st.sb("y", [P, T])
        r = st.sb("r", [P, T])
        th = r
        iy = st.sb("i", [P, T])
        a = st.sb("a", [P, T])
        a2 = st.sb("a2", [P, T])
        hs = st.sb("hs", [P, T])
        convw = st.sb("conv_w", [P, KD, CONV + 3])
        sconv = st.sb("state_conv", [P, KD, PRE, NS])
        slru = st.sb("state_lru", [P, KD, NS])
        oconvp = st.sb("o_conv_p", [P, KD, PRE])
        oconvs = st.sb("o_conv_s", [P, KD, PRE, NS])
        olrup = st.sb("o_lru_p", [P, KD])
        olrus = st.sb("o_lru_s", [P, KD, NS])

        loads = st.sem("loads")
        w_landed = [st.sem("w_landed_x"), st.sem("w_landed_g")]
        wg_landed = [st.sem("wg_landed0"), st.sem("wg_landed1")]
        w_hi_done = st.sem("w_hi_done")
        w_lo_done = st.sem("w_lo_done")
        h_hi_done = st.sem("h_hi_done")
        h_lo_done = st.sem("h_lo_done")
        zeroed = st.sem("zeroed")
        unit_summed = st.sem("unit_summed")
        unit_drained = st.sem("unit_drained")
        y_parts = st.sem("y_parts")
        ri_summed = st.sem("ri_summed")
        gs_done = st.sem("gs_done")
        r_done = st.sem("r_done")
        i_done = st.sem("i_done")
        iy_done = st.sem("iy_done")
        a_done = st.sem("a_done")
        th_done = st.sem("th_done")
        a2_done = st.sem("a2_done")
        m_done = st.sem("m_done")
        root_done = st.sem("root_done")
        u_done = st.sem("u_done")
        h_done = st.sem("h_done")
        kept = st.sem("kept")
        og_done = st.sem("og_done")
        stored = st.sem("stored")
        block = st.block()
        R, I = c.ps[:, 2:2 + NT, 0:TT], c.ps[:, 5:5 + NT, 0:TT]

        def heads(engine, head):
            head(0, 0, 1, 2)
            with engine.Fori(0, 2) as i:
                head(2 * i + 1, 1, 2 * i + 2, 2 * i + 3)
                head(2 * i + 2, 0, 2 * i + 3, 2 * i + 4)
            head(H - 3, 1, H - 2, H - 1)
            head(H - 2, 0, H - 1, None)
            head(H - 1, 1, None, None)

        @block.sync
        def _(sp):
            sp.dma_start(convw[:, :, :], dram["rg_small"]).then_inc(loads, 16)
            sp.dma_start(sconv[:, :, :, :], dram["state_conv"]).then_inc(loads, 16)
            sp.dma_start(slru[:, :, :], dram["state_lru"]).then_inc(loads, 16)

            def weights(h, u, first=False):
                for n in range(2):
                    if not first:
                        sp.wait_ge(w_lo_done, 2 * h + (n - 1))
                    sp.dma_start(ws[:, n, :, :], dram["w_rg"][n][bass.ds(h, 1)].rearrange("a p k m -> p (a k) m")) \
                      .then_inc(w_landed[n], 16)
                wait(sp, ri_summed, 2 * h - 2)
                sp.dma_start(wg[:, u, :, :], dram["w_rg_gates"][bass.ds(h, 1)].rearrange("a p k m -> p (a k) m")) \
                  .then_inc(wg_landed[u], 16)

            weights(0, 0, first=True)
            weights(1, 1)
            with sp.Fori(1, H // 2) as i:
                for u in range(2):
                    weights(2 * i + u, u)
            sp.wait_ge(kept, 5 * H)
            sp.dma_start(dram["o_conv_p"], oconvp[:, :, :]).then_inc(stored, 16)
            sp.dma_start(dram["o_conv_s"], oconvs[:, :, :, :]).then_inc(stored, 16)
            sp.dma_start(dram["o_lru_p"], olrup[:, :]).then_inc(stored, 16)
            sp.dma_start(dram["o_lru_s"], olrus[:, :, :]).then_inc(stored, 16)
            sp.wait_ge(stored, 64)

        @block.tensor
        def _(pe):
            def unit(h, n):
                kind, t = divmod(n, 3)
                wait(pe, unit_drained, NU * h + (n - 1))
                if t == 0:
                    pe.wait_ge(w_lo_done, 2 * h + (kind + 1))
                for kk in range(KD):
                    if isinstance(h, int) and h == 0 and n == 0:
                        pe.wait_ge(h_lo_done, kk + 1)
                    for e, (x, y) in enumerate(((w_hi, h_hi), (w_hi, h_lo), (w_lo, h_hi))):
                        mm = nc.tensor.matmul(c.ps[:, n % 2, 0:TT], x[:, kind, kk, :],
                                              y[:, kk, t * TT:(t + 1) * TT],
                                              start=(kk == 0 and e == 0), stop=(kk == KD - 1 and e == 2))
                mm.then_inc(unit_summed, 1)

            def head(h, u, following, after):
                if following is not None:
                    for n in range(3):
                        unit(following, n)
                pe.wait_ge(y_parts, 7 * h + 7)
                pe.wait_ge(wg_landed[u], 8 * h + (16 - 8 * u))
                for e, done in enumerate((r_done, i_done)):
                    wait(pe, done, h)
                    for t, cols in tiles():
                        mm = nc.tensor.matmul(c.ps[:, 2 + NT * e + t, 0:TT], wg[:, u, e, :], y[:, cols],
                                              start=True, stop=True)
                    mm.then_inc(ri_summed, 1)
                if following is not None:
                    for n in range(3, NU):
                        unit(following, n)

            for n in range(NU):
                unit(0, n)
            heads(pe, head)

        @block.scalar
        def _(act):
            def weight_hi(h, kind):
                act.wait_ge(w_landed[kind], 16 * h + 16)
                wait(act, unit_summed, NU * h + (3 * kind - 3))
                nc.scalar.activation(w_hi[:, kind, :, :], ws[:, kind, :, :], ACT.Copy).then_inc(w_hi_done, 1)

            def drain_unit(h, u, n):
                kind, t = divmod(n, 3)
                act.wait_ge(unit_summed, NU * h + (n + 1))
                if n == 0:
                    wait(act, kept, 5 * h - 5)
                    wait(act, y_parts, 7 * h - 7)
                if n == NT:
                    wait(act, og_done, h - 1)
                lo = PRE if kind == 0 else 0
                dst = (xb if kind == 0 else graw)[:, u, lo + t * TT:lo + (t + 1) * TT]
                nc.scalar.activation(dst, c.ps[:, n % 2, 0:TT], ACT.Copy).then_inc(unit_drained, 1)

            def head(h, u, following, after):
                act.wait_ge(unit_drained, NU * h + NU)
                if following is not None:
                    weight_hi(following, 1)
                nc.scalar.activation(graw[:, u, :], graw[:, u, :], ACT.Silu).then_inc(gs_done, 1)
                if following is not None:
                    for n in range(3):
                        drain_unit(following, 1 - u, n)
                act.wait_ge(loads, 48)
                act.wait_ge(ri_summed, 2 * h + 1)
                wait(act, m_done, h)
                nc.scalar.activation(split_tiles(r[:, :]), R, ACT.Sigmoid,
                                     bias=convw[:, bass.ds(h, 1), CONV + 1:CONV + 2].rearrange("p a k -> p (a k)")) \
                  .then_inc(r_done, 1)
                act.wait_ge(ri_summed, 2 * h + 2)
                wait(act, u_done, h)
                nc.scalar.activation(split_tiles(iy[:, :]), I, ACT.Sigmoid,
                                     bias=convw[:, bass.ds(h, 1), CONV + 2:CONV + 3].rearrange("p a k -> p (a k)")) \
                  .then_inc(i_done, 1)
                if following is not None:
                    drain_unit(following, 1 - u, 3)
                act.wait_ge(r_done, h + 1)
                wait(act, h_done, 3 * h)
                nc.scalar.activation(a[:, :], r[:, :], ACT.Exp, scale=m8[:, bass.ds(h, 1)]).then_inc(a_done, 1)
                nc.scalar.activation(th[:, :], r[:, :], ACT.Tanh, scale=p8[:, bass.ds(h, 1)]).then_inc(th_done, 1)
                act.wait_ge(a_done, h + 1)
                nc.scalar.activation(a2[:, :], a[:, :], ACT.Square).then_inc(a2_done, 1)
                if following is not None:
                    drain_unit(following, 1 - u, 4)
                if after is not None:
                    weight_hi(after, 0)
                act.wait_ge(m_done, h + 1)
                nc.scalar.activation(a2[:, :], a2[:, :], ACT.Sqrt).then_inc(root_done, 1)
                if following is not None:
                    drain_unit(following, 1 - u, 5)

            for kk in range(KD):
                nc.scalar.activation(h_hi[:, kk, :], c.h[:, kk, :], ACT.Copy).then_inc(h_hi_done, 1)
                if kk == 1:
                    weight_hi(0, 0)
            weight_hi(0, 1)
            act.wait_ge(zeroed, 1)
            for n in range(NU):
                drain_unit(0, 0, n)
            weight_hi(1, 0)
            heads(act, head)

        @block.gpsimd
        def _(pool):
            def weight_lo(h, kind):
                pool.wait_ge(w_hi_done, 2 * h + (kind + 1))
                nc.gpsimd.tensor_tensor(w_lo[:, kind, :, :], ws[:, kind, :, :], w_hi[:, kind, :, :].bitcast(F32),
                                        ALU.subtract).then_inc(w_lo_done, 1)

            def head(h, u, following, after):
                if following is not None:
                    weight_lo(following, 1)
                pool.wait_ge(i_done, h + 1)
                nc.gpsimd.tensor_tensor(iy[:, :], iy[:, :], y[:, :], ALU.mult).then_inc(iy_done, 1)
                if after is not None:
                    weight_lo(after, 0)
                pool.wait_ge(root_done, h + 1)
                pool.wait_ge(iy_done, h + 1)
                nc.gpsimd.tensor_tensor(a2[:, :], a2[:, :], iy[:, :], ALU.mult).then_inc(u_done, 1)
                pool.wait_ge(h_done, 3 * h + 3)
                pool.wait_ge(gs_done, h + 1)
                nc.gpsimd.tensor_tensor(out[:, bass.ds(h, 1), :].rearrange("p a t -> p (a t)"), hs[:, :], graw[:, u, :],
                                        ALU.mult).then_inc(og_done, 1)

            weight_lo(0, 0)
            weight_lo(0, 1)
            weight_lo(1, 0)
            heads(pool, head)

        @block.vector
        def _(dve):
            def one(buf, h, k):
                return buf[:, bass.ds(h, 1), k:k + 1].rearrange("p a k -> p (a k)")

            def head(h, u, following, after):
                dve.wait_ge(unit_drained, NU * h + 3)
                wait(dve, iy_done, h)
                wait(dve, ri_summed, 2 * h)
                nc.vector.tensor_scalar(y[:, :], xb[:, u, PRE:PRE + T], one(convw, h, PRE), one(convw, h, CONV),
                                        op0=ALU.mult, op1=ALU.add).then_inc(y_parts, 1)
                for n in range(PRE):
                    dve.wait_ge(y_parts, 7 * h + (2 * n + 1))
                    nc.vector.scalar_tensor_tensor(y[:, 0:SEQ], xb[:, u, n:n + SEQ], one(convw, h, n), y[:, 0:SEQ],
                                                   op0=ALU.mult, op1=ALU.add).then_inc(y_parts, 1)
                    nc.vector.scalar_tensor_tensor(
                        y[:, SEQ:T], sconv[:, bass.ds(h, 1), n, :].rearrange("p a s -> p (a s)"), one(convw, h, n),
                        y[:, SEQ:T], op0=ALU.mult, op1=ALU.add).then_inc(y_parts, 1)
                nc.vector.tensor_copy(oconvp[:, bass.ds(h, 1), :].rearrange("p a k -> p (a k)"),
                                      xb[:, u, SEQ:SEQ + PRE]).then_inc(kept, 1)
                nc.vector.tensor_copy(oconvs[:, bass.ds(h, 1), 0:PRE - 1, :].rearrange("p a k s -> p (a k) s"),
                                      sconv[:, bass.ds(h, 1), 1:PRE, :].rearrange("p a k s -> p (a k) s")) \
                  .then_inc(kept, 1)
                nc.vector.tensor_copy(oconvs[:, bass.ds(h, 1), PRE - 1, :].rearrange("p a s -> p (a s)"),
                                      xb[:, u, PRE + SEQ:PRE + T]).then_inc(kept, 1)
                dve.wait_ge(a2_done, h + 1)
                dve.wait_ge(th_done, h + 1)
                nc.vector.scalar_tensor_tensor(a2[:, :], a2[:, :], 1.0, th[:, :], op0=ALU.add, op1=ALU.mult) \
                  .then_inc(m_done, 1)
                dve.wait_ge(u_done, h + 1)
                wait(dve, og_done, h)
                wait(dve, kept, 5 * h)
                nc.vector.tensor_tensor_scan(hs[:, 0:SEQ], a[:, 0:SEQ], a2[:, 0:SEQ], 0.0,
                                             op0=ALU.mult, op1=ALU.add).then_inc(h_done, 1)
                nc.vector.tensor_tensor(hs[:, SEQ:T], a[:, SEQ:T],
                                        slru[:, bass.ds(h, 1), :].rearrange("p a s -> p (a s)"),
                                        ALU.mult).then_inc(h_done, 1)
                dve.wait_ge(h_done, 3 * h + 2)
                nc.vector.tensor_tensor(hs[:, SEQ:T], hs[:, SEQ:T], a2[:, SEQ:T], ALU.add).then_inc(h_done, 1)
                dve.wait_ge(h_done, 3 * h + 3)
                nc.vector.tensor_copy(olrup[:, bass.ds(h, 1)], hs[:, SEQ - 1:SEQ]).then_inc(kept, 1)
                nc.vector.tensor_copy(olrus[:, bass.ds(h, 1), :].rearrange("p a s -> p (a s)"), hs[:, SEQ:T]) \
                  .then_inc(kept, 1)

            nc.vector.memset(xb[:, :, 0:PRE], 0.0).then_inc(zeroed, 1)
            for kk in range(KD):
                dve.wait_ge(h_hi_done, kk + 1)
                nc.vector.tensor_tensor(h_lo[:, kk, :], c.h[:, kk, :], h_hi[:, kk, :].bitcast(F32),
                                        ALU.subtract).then_inc(h_lo_done, 1)
            dve.wait_ge(zeroed, 1)
            dve.wait_ge(loads, 48)
            heads(dve, head)


def rglru_layer(c, layer):
    with Stage(c) as st:
        out = c.h
        m8 = st.sb("m8", [P, KD])
        p8 = st.sb("p8", [P, KD])
        rglru_decay_rate(c, m8, p8)
        rglru_heads(c, out, m8, p8)
        output_projection(c, c.dram["w_rg_out"], KD, out, following(layer))


def store_residual(c):
    nc, dram = c.nc, c.dram
    with Stage(c) as st:
        stored = st.sem("stored")
        block = st.block()

        @block.sync
        def _(sp):
            sp.dma_start(dram["o_x"], c.x[:, :, :]).then_inc(stored, 16)
            sp.wait_ge(stored, 16)


def program(nc, dram):
    with ExitStack() as ctx:
        Stage.used = []
        c = Chip(nc, ctx, dram)
        load_inputs(c)
        mla_layer(c, 0, 0)
        hgrn_layer(c, 1)
        rglru_layer(c, 2)
        mla_layer(c, 3, 1)
        store_residual(c)



def feature_tiles(a):
    return np.moveaxis(a.reshape(*a.shape[:-1], a.shape[-1] // P, P), -1, -2)


def weight_blocks(w, width=P):
    k, n = w.shape
    return w.reshape(k // P, P, n // width, width).transpose(2, 1, 0, 3)


def stack(f, w):
    return np.stack([f(x) for x in w])


def shape_constants(past):
    pos = np.concatenate([np.arange(SEQ), np.full(NS, past)]).astype(np.float32)
    inv = (1.0 / (np.float32(10000.0) ** (np.arange(0, ROPE, 2, dtype=np.float32) / ROPE))).astype(np.float32)
    ang = (pos[None, :] * inv[:, None]).astype(np.float32)
    trig = np.zeros((P, T), np.float32)
    trig[NOPE:QK] = np.concatenate([np.cos(ang), np.cos(ang)])
    trig[QK:P] = np.concatenate([-np.sin(ang), np.sin(ang)])
    r = np.arange(P)
    s, t = r[:, None], r[None, :]
    masks = [s == t] + [(s // (2 * hf) == t // (2 * hf)) & (s // hf + 1 == t // hf)
                        for hf in (P >> (l + 1) for l in range(LEVELS))]
    return {
        "hgrn_masks": np.stack(masks, axis=1).astype(np.float32),
        "sel": np.repeat(np.eye(NS, dtype=np.float32)[:, :, None], P, axis=2),
        "ident": np.eye(P, dtype=np.float32), "ones": np.ones((P, P), np.float32),
        "const": np.tile(np.array(TINY, np.float32), (P, 1)), "trig": trig,
        "causal": np.where(r[None, :] <= r[:, None], 0.0, -1e30).astype(np.float32),
    }


def layouts(i):
    a = {k: np.asarray(v) for k, v in i.items()}
    x = np.concatenate([a["x_prompt"].reshape(SEQ, D), a["x_sample"].reshape(NS, D)])
    pages = np.concatenate([a["cache_ckv"], a["cache_kpe"]], axis=-1)
    nl, pool = pages.shape[:2]
    win = a["mla_w_in"]
    z = np.concatenate([win[:, :, :QL + KVL], win[:, :, QL + KVL + ROPE:]], axis=2)
    kpe = win[:, :, QL + KVL:QL + KVL + ROPE]
    half = ROPE // 2
    kpe = np.concatenate([kpe, kpe[:, :, half:], kpe[:, :, :half]], axis=2)
    uq = a["mla_w_uq"].reshape(nl, QL, H, QK)
    uq = np.concatenate([uq, uq[..., NOPE + half:], uq[..., NOPE:NOPE + half]], axis=3).reshape(nl, QL, H * P)
    ukv = a["mla_w_ukv"].reshape(nl, KVL, H, NOPE + DV)
    uk, uv = ukv[..., :NOPE].reshape(nl, KVL, H * NOPE), ukv[..., NOPE:].reshape(nl, KVL, H * DV)
    out = {
        "x": feature_tiles(x).transpose(1, 2, 0),
        "norm_g": feature_tiles(a["norm_g"]).transpose(1, 0, 2),
        "w_mla_in": stack(weight_blocks, z),
        "w_kpe": stack(lambda w: weight_blocks(w, 2 * ROPE)[0], kpe),
        "g_q_lora": feature_tiles(a["mla_g_q_lora"]),
        "g_kv": feature_tiles(a["mla_g_kv"]),
        "w_uq": stack(weight_blocks, uq),
        "w_uk": stack(lambda w: weight_blocks(w, NOPE), uk),
        "w_uk_all": stack(lambda w: weight_blocks(w, H * NOPE)[0], uk),
        "w_uk_t": uk.reshape(nl, KVL, H, NOPE).transpose(0, 3, 2, 1),
        "w_uv": stack(lambda w: weight_blocks(w, H * DV)[0], uv),
        "g_qk": np.stack([a["mla_g_q"], a["mla_g_k"]], axis=-1),
        "w_mla_out": stack(weight_blocks, a["mla_w_out"]),
        "page_table": a["page_table"].reshape(1, NS * PAGES),
        "pages": pages,
        "pages_t": a["cache_ckv"].transpose(0, 1, 3, 2).reshape(nl, pool, NKV, P, PAGE).transpose(0, 1, 3, 2, 4),
        "pages_kpe_t": a["cache_kpe"].transpose(0, 1, 3, 2),
    }
    w4 = a["hgrn_w_in"][0].reshape(D, 4, H, P)
    q_, f_, i_, g_ = (w4[:, n].reshape(D, H * P) for n in range(4))
    out["w_hgrn"] = np.stack([weight_blocks(w) for w in (f_, q_, i_, g_)])
    out["w_hgrn_out"] = weight_blocks(a["hgrn_w_out"][0])
    out["hgrn_bounds"] = feature_tiles(a["hgrn_lower_bounds"]).transpose(1, 0, 2)
    out["hgrn_g_norm"] = a["hgrn_g_norm"][0].reshape(P, 1)
    out["state_hgrn"] = a["state_hgrn"][0].transpose(1, 2, 0, 3)
    rg = a["rglru_w_in"][0]
    out["w_rg"] = np.stack([weight_blocks(rg[:, :D]), weight_blocks(rg[:, D:])])
    out["w_rg_gates"] = np.stack([a["rglru_w_a"][0], a["rglru_w_x"][0]], axis=2)
    out["w_rg_out"] = weight_blocks(a["rglru_w_out"][0])
    small = np.concatenate([a["rglru_conv_w"][0], a["rglru_conv_b"], a["rglru_b_a"], a["rglru_b_x"]])
    out["rg_small"] = feature_tiles(small).transpose(1, 2, 0)
    out["rg_lam"] = feature_tiles(a["rglru_L"][0])
    out["state_conv"] = feature_tiles(a["state_conv"][0]).transpose(2, 3, 1, 0)
    out["state_lru"] = feature_tiles(a["state_lru"][0]).transpose(1, 2, 0)
    out.update(shape_constants(PAGES * PAGE))
    return {k: np.ascontiguousarray(v) for k, v in out.items()}


def kernel(**inputs):
    import concourse.bacc as bacc
    from concourse.bass_utils import run_bass_kernel_spmd

    nl = inputs["cache_ckv"].shape[0]
    outs = {"o_x": (P, KD, T), "o_ckv": (nl, P, NKV, T), "o_kpe": (nl, ROPE, T),
            "o_hgrn_p": (H, P, P), "o_hgrn_s": (H, P, NS, P),
            "o_conv_p": (P, KD, CONV - 1), "o_conv_s": (P, KD, CONV - 1, NS), "o_lru_p": (P, KD),
            "o_lru_s": (P, KD, NS)}
    nc = bacc.Bacc("TRN2", target_bir_lowering=False, num_devices=1)
    arrays, dram = layouts(inputs), {}
    for name, a in arrays.items():
        dram[name] = nc.dram_tensor("in_" + name, a.shape, mybir.dt.from_np(a.dtype), kind="ExternalInput").ap()
    for name, shape in outs.items():
        dram[name] = nc.dram_tensor(name, shape, F32, kind="ExternalOutput").ap()
    program(nc, dram)
    r = run_bass_kernel_spmd(nc, [{"in_" + k: v for k, v in arrays.items()}], core_ids=[0]).results[0]

    x = r["o_x"].transpose(2, 1, 0).reshape(T, D)
    ckv = r["o_ckv"].transpose(0, 3, 2, 1).reshape(nl, T, KVL)
    kpe = r["o_kpe"].transpose(0, 2, 1)
    return (x[:SEQ].reshape(1, SEQ, D), x[SEQ:].reshape(NS, 1, D),
            ckv[:, :SEQ].reshape(nl, 1, SEQ, KVL), kpe[:, :SEQ].reshape(nl, 1, SEQ, ROPE),
            ckv[:, SEQ:].reshape(nl, NS, 1, KVL), kpe[:, SEQ:].reshape(nl, NS, 1, ROPE),
            r["o_hgrn_p"].reshape(1, 1, H, P, P), r["o_hgrn_s"].transpose(2, 0, 1, 3)[None],
            r["o_conv_p"].transpose(2, 1, 0).reshape(1, 1, CONV - 1, D),
            r["o_conv_s"].transpose(3, 2, 1, 0).reshape(1, NS, CONV - 1, D),
            r["o_lru_p"].T.reshape(1, 1, D), r["o_lru_s"].transpose(2, 1, 0).reshape(1, NS, D))
```
